# Optimizing a Trainium2 kernel written in Bass

```python
import jax, jax.numpy as jnp
from jax import lax
import numpy as np

D_MODEL = 1024
BATCH = 1
SEQ = 1024
DEPTH = 1

GRID_W = 64
CTX_LEN = 256
A_HEADS = 4
A_DQK = 128
A_DV = 256
A_QK_WIDTH = A_HEADS * A_DQK
A_WIDTH = A_HEADS * A_DV
MLSTM_CHUNK = 128
SHORT_CONV_W = 5
B_GROUPS = 4
B_WIDTH = 1024
B_CHUNK = 128
ROWS_PER_CHUNK = B_CHUNK // GRID_W
D_FF = -(-(8 * D_MODEL) // (3 * 256)) * 256
N_MOD = 6
EPS = 1e-6
IN_SIZES = (A_QK_WIDTH, A_QK_WIDTH, A_WIDTH, A_WIDTH, 4 * A_HEADS, B_WIDTH, B_WIDTH, D_MODEL, D_MODEL)
IN_WIDTH = sum(IN_SIZES)
IN_SPLITS = tuple(int(s) for s in np.cumsum(IN_SIZES)[:-1])

kernel_name = 'hybrid_mlstm_gmlp_diffusion_block'

def _rmsnorm(x, g):
    xf = x.astype(jnp.float32)
    y = xf * lax.rsqrt(jnp.mean(xf * xf, axis=-1, keepdims=True) + EPS)
    return (y * g.astype(jnp.float32)).astype(x.dtype)

def _modulate(h, shift, scale):
    return h * (1 + scale[:, None, :]) + shift[:, None, :]

def _short_conv(x, w, b):
    pad = SHORT_CONV_W // 2
    y = lax.conv_general_dilated(x, w[:, None, :].astype(x.dtype), window_strides=(1,), padding=[(pad, pad)], dimension_numbers=('NWC', 'WIO', 'NWC'), feature_group_count=x.shape[-1])
    return y + b

def _heads(t, d):
    B, N, _ = t.shape
    return t.reshape(B, N, -1, d).transpose(0, 2, 1, 3)

def _mlstm_chunkwise(q, k, v, log_i, log_f, state):
    q, k, v = (t.astype(jnp.float32) for t in (q, k, v))
    B, H, N, _ = q.shape
    L = MLSTM_CHUNK
    nc = N // L

    def to_chunks(t):
        return jnp.moveaxis(t.reshape(B, H, nc, L, *t.shape[3:]), 2, 0)

    xs = tuple(to_chunks(t) for t in (q, k, v, log_i, log_f))
    lower = jnp.tril(jnp.ones((L, L), dtype=bool))

    def step(carry, inp):
        C, n, m = carry
        qc, kc, vc, ic, fc = inp
        b = jnp.cumsum(fc, axis=-1)
        log_d = b[..., :, None] - b[..., None, :] + ic[..., None, :]
        log_d = jnp.where(lower, log_d, -jnp.inf)
        log_prev = b + m[..., None]
        m_t = jnp.maximum(log_prev, jnp.max(log_d, axis=-1))
        w_prev = jnp.exp(log_prev - m_t)
        s = jnp.einsum('bhtd,bhsd->bhts', qc, kc) * jnp.exp(log_d - m_t[..., None])
        num = jnp.einsum('bhts,bhsv->bhtv', s, vc) + w_prev[..., None] * jnp.einsum('bhtd,bhdv->bhtv', qc, C)
        den = jnp.sum(s, axis=-1) + w_prev * jnp.einsum('bhtd,bhd->bht', qc, n)
        h = num / jnp.maximum(jnp.abs(den), jnp.exp(-m_t))[..., None]
        b_end = b[..., -1]
        log_src = b_end[..., None] - b + ic
        m_new = jnp.maximum(b_end + m, jnp.max(log_src, axis=-1))
        w_src = jnp.exp(log_src - m_new[..., None])
        w_c = jnp.exp(b_end + m - m_new)
        kw = kc * w_src[..., None]
        C_new = w_c[..., None, None] * C + jnp.einsum('bhsd,bhsv->bhdv', kw, vc)
        n_new = w_c[..., None] * n + jnp.sum(kw, axis=2)
        return (C_new, n_new, m_new), h

    state, hs = lax.scan(step, state, xs)
    h = jnp.moveaxis(hs, 0, 2).reshape(B, H, N, v.shape[-1])
    return h, state

def _mlstm_direction(ctx_in, lat_in, reverse):
    if reverse:
        ctx_in = tuple(jnp.flip(t, axis=2) for t in ctx_in)
        lat_in = tuple(jnp.flip(t, axis=2) for t in lat_in)
    B = ctx_in[0].shape[0]
    state0 = (jnp.zeros((B, A_HEADS, A_DQK, A_DV), jnp.float32), jnp.zeros((B, A_HEADS, A_DQK), jnp.float32), jnp.zeros((B, A_HEADS), jnp.float32))
    h_c, state = _mlstm_chunkwise(*ctx_in, state0)
    h_x, _ = _mlstm_chunkwise(*lat_in, state)
    if reverse:
        h_c = jnp.flip(h_c, axis=2)
        h_x = jnp.flip(h_x, axis=2)
    return h_c, h_x

def _mix_inputs(h, w_in, conv_w, conv_b, gate_b):
    B, N, _ = h.shape
    z = jnp.einsum('bnd,de->bne', h, w_in)
    q_raw, k_raw, v_raw, o_raw, g_raw, u_raw, vb_raw, ga_raw, gb_raw = jnp.split(z, IN_SPLITS, axis=-1)
    qk = jax.nn.silu(_short_conv(jnp.concatenate([q_raw, k_raw], axis=-1), conv_w, conv_b))
    q, k = jnp.split(qk, 2, axis=-1)
    q = _heads(q, A_DQK) * (A_DQK ** -0.5)
    k = _heads(k, A_DQK)
    v = _heads(v_raw, A_DV)
    g = (g_raw + gate_b).astype(jnp.float32).reshape(B, N, 4, A_HEADS).transpose(2, 0, 3, 1)
    fwd = (q, k, v, g[0], jax.nn.log_sigmoid(g[1]))
    bwd = (q, k, v, g[2], jax.nn.log_sigmoid(g[3]))
    rest = (o_raw, u_raw, vb_raw, ga_raw, gb_raw)
    return fwd, bwd, rest

def _mix_outputs(h_a, rest, n_chunks, head_g, vnorm_g, w_sp, b_sp, w_pa, w_pb, w_out):
    o_raw, u_raw, vb_raw, ga_raw, gb_raw = rest
    B, N, _ = o_raw.shape
    y_a = _rmsnorm(h_a.astype(o_raw.dtype), head_g[:, None, :]).transpose(0, 2, 1, 3).reshape(B, N, A_WIDTH)
    y_a = y_a * jax.nn.sigmoid(o_raw)
    u = jax.nn.gelu(u_raw)
    vb = _rmsnorm(jax.nn.gelu(vb_raw), vnorm_g).reshape(B, n_chunks, B_CHUNK, B_GROUPS, B_WIDTH // B_GROUPS)
    sv = jnp.einsum('gts,bcsgd->bctgd', w_sp, vb) + b_sp.T[:, :, None]
    y_b = u * sv.reshape(B, N, B_WIDTH)
    merged = jax.nn.sigmoid(ga_raw) * jnp.einsum('bne,ed->bnd', y_a, w_pa) + jax.nn.sigmoid(gb_raw) * jnp.einsum('bne,ed->bnd', y_b, w_pb)
    return jnp.einsum('bnd,de->bne', merged, w_out)

def _swiglu(h, w1, w3, w2):
    a = jnp.einsum('bnd,df->bnf', h, w1)
    g = jnp.einsum('bnd,df->bnf', h, w3)
    return jnp.einsum('bnf,fd->bnd', jax.nn.silu(a) * g, w2)

def setup_inputs(seed: int = 0) -> dict:
    key = jax.random.key(seed)
    ks = jax.random.split(key, 24)
    L, D = DEPTH, D_MODEL

    def nrm(k, shape, scale):
        return jax.random.normal(k, shape, jnp.float32) * scale

    gate_i = nrm(ks[11], (L, 2, A_HEADS), 0.1)
    gate_f = jnp.linspace(3.0, 6.0, A_HEADS, dtype=jnp.float32) + nrm(ks[12], (L, 2, A_HEADS), 0.1)
    gate_b = jnp.stack([gate_i, gate_f], axis=2).reshape(L, 4 * A_HEADS)
    return {
        'x': nrm(ks[0], (BATCH, SEQ, D), 1.0),
        'c': nrm(ks[1], (BATCH, D), 1.0),
        'ctx': nrm(ks[2], (BATCH, CTX_LEN, D), 1.0),
        'c_ctx': nrm(ks[3], (D,), 1.0),
        'w_ada': nrm(ks[4], (L, D, N_MOD * D), 0.5 * D ** -0.5),
        'b_ada': nrm(ks[5], (L, N_MOD * D), 0.02),
        'norm1_g': 1.0 + nrm(ks[6], (L, D), 0.1),
        'norm2_g': 1.0 + nrm(ks[7], (L, D), 0.1),
        'w_in': nrm(ks[8], (L, D, IN_WIDTH), D ** -0.5),
        'conv_w': nrm(ks[9], (L, SHORT_CONV_W, 2 * A_QK_WIDTH), SHORT_CONV_W ** -0.5),
        'conv_b': nrm(ks[10], (L, 2 * A_QK_WIDTH), 0.02),
        'gate_b': gate_b,
        'head_g': 1.0 + nrm(ks[13], (L, A_HEADS, A_DV), 0.1),
        'vnorm_g': 1.0 + nrm(ks[14], (L, B_WIDTH), 0.1),
        'w_spatial': nrm(ks[15], (L, B_GROUPS, B_CHUNK, B_CHUNK), 0.5 * B_CHUNK ** -0.5),
        'b_spatial': 1.0 + nrm(ks[16], (L, B_GROUPS, B_CHUNK), 0.1),
        'w_pa': nrm(ks[17], (L, A_WIDTH, D), A_WIDTH ** -0.5),
        'w_pb': nrm(ks[18], (L, B_WIDTH, D), B_WIDTH ** -0.5),
        'w_out': nrm(ks[19], (L, D, D), D ** -0.5),
        'w_ff1': nrm(ks[20], (L, D, D_FF), D ** -0.5),
        'w_ff3': nrm(ks[21], (L, D, D_FF), D ** -0.5),
        'w_ff2': nrm(ks[22], (L, D_FF, D), D_FF ** -0.5),
        'final_g': 1.0 + nrm(ks[23], (D,), 0.1),
    }

def reference(x, c, ctx, c_ctx, w_ada, b_ada, norm1_g, norm2_g, w_in, conv_w, conv_b, gate_b, head_g, vnorm_g, w_spatial, b_spatial, w_pa, w_pb, w_out, w_ff1, w_ff3, w_ff2, final_g):
    rows = x.shape[1] // GRID_W
    lat_chunks = rows // ROWS_PER_CHUNK
    ctx_chunks = ctx.shape[1] // B_CHUNK
    mod_x = jnp.einsum('bd,lde->lbe', jax.nn.silu(c), w_ada) + b_ada[:, None, :]
    mod_c = jnp.einsum('d,lde->le', jax.nn.silu(c_ctx), w_ada)[:, None, :] + b_ada[:, None, :]
    xs, cs = x, ctx
    for l in range(DEPTH):
        last = l == DEPTH - 1
        sh1x, sc1x, g1x, sh2x, sc2x, g2x = jnp.split(mod_x[l], N_MOD, axis=-1)
        sh1c, sc1c, g1c, sh2c, sc2c, g2c = jnp.split(mod_c[l], N_MOD, axis=-1)
        hx = _modulate(_rmsnorm(xs, norm1_g[l]), sh1x, sc1x)
        hc = _modulate(_rmsnorm(cs, norm1_g[l]), sh1c, sc1c)
        fwd_x, bwd_x, rest_x = _mix_inputs(hx, w_in[l], conv_w[l], conv_b[l], gate_b[l])
        fwd_c, bwd_c, rest_c = _mix_inputs(hc, w_in[l], conv_w[l], conv_b[l], gate_b[l])
        hc_f, hx_f = _mlstm_direction(fwd_c, fwd_x, reverse=False)
        hc_b, hx_b = _mlstm_direction(bwd_c, bwd_x, reverse=True)
        out_x = _mix_outputs(hx_f + hx_b, rest_x, lat_chunks, head_g[l], vnorm_g[l], w_spatial[l], b_spatial[l], w_pa[l], w_pb[l], w_out[l])
        xs = xs + g1x[:, None, :] * out_x
        xs = xs + g2x[:, None, :] * _swiglu(_modulate(_rmsnorm(xs, norm2_g[l]), sh2x, sc2x), w_ff1[l], w_ff3[l], w_ff2[l])
        if not last:
            out_c = _mix_outputs(hc_f + hc_b, rest_c, ctx_chunks, head_g[l], vnorm_g[l], w_spatial[l], b_spatial[l], w_pa[l], w_pb[l], w_out[l])
            cs = cs + g1c[:, None, :] * out_c
            cs = cs + g2c[:, None, :] * _swiglu(_modulate(_rmsnorm(cs, norm2_g[l]), sh2c, sc2c), w_ff1[l], w_ff3[l], w_ff2[l])
    return _rmsnorm(xs, final_g)


_drawn_inputs = setup_inputs


def setup_inputs(seed=0):
    import zlib

    import numpy as np

    out = dict(_drawn_inputs(seed))
    spreads = {}
    factors = {'ctx': 6.6,
     'c_ctx': 3.809,
     'b_ada': 2.676,
     'norm1_g': 3.007,
     'conv_b': 64.0,
     'head_g': 5.695,
     'vnorm_g': 8.0,
     'b_spatial': 4.552,
     'norm2_g': 4.788}
    for name, (base, spread) in spreads.items():
        noise = np.random.default_rng([zlib.crc32(name.encode()), seed]).standard_normal(out[name].shape)
        drawn = base * np.exp(spread * noise) if base else spread * noise
        out[name] = __import__('jax').numpy.asarray(drawn.astype(out[name].dtype))
    for name, factor in factors.items():
        out[name] = (out[name] * factor).astype(out[name].dtype)
    return out
```

```python
from contextlib import ExitStack

import concourse.bass as bass
from concourse import mybir

F32 = mybir.dt.float32
F32R = mybir.dt.float32r
I32 = mybir.dt.int32
ALU = mybir.AluOpType
ACT = mybir.ActivationFunctionType
AX = mybir.AxisListType.X
ds = bass.ds

P = 128
D = 1024
KT = D // P
NLAT, NCTX = 1024, 256
LT, CT = NLAT // P, NCTX // P
TT = LT + CT
HALF = 512
HEADS, DQK, DV = 4, 128, 256
L = 128
DFF = 2816
CW = 256
NFB = DFF // CW
EPS = 1e-6
TAPS = 5
PAD = TAPS // 2
CQ, CK, CV, CO, CG, CU, CVB, CGA, CGB = 0, 512, 1024, 2048, 3072, 3088, 4112, 5136, 6160
NEG = -1.0e30
DVA = DV + 2
QSCALE = 0.25 * DQK ** -0.5

N_H, N_V, N_U, N_PB, N_PA, N_O, N_F = 0, 12, 16, 20, 28, 36, 40
T_H, T_V, T_U, T_PB, T_PA, T_O, T_X, T_F = 0, 40, 56, 64, 80, 96, 112, 120
HT = 10
FT = 12
A, B, C = 0, 1, 2
LINKS_H, LINKS_U, LINKS_O = 76, 4, 8
MAGIC = float(0x5F3759DF)


def tile_of(direction, j):
    if direction == 0:
        return j
    return CT - 1 - j if j < CT else TT + CT - 1 - j


class Chain:

    def __init__(self, eng, semaphore):
        self.eng, self.sem, self.base, self.i, self.per, self.n = eng, semaphore, 0, 0, 0, 0

    def link(self, instruction):
        self.n += 1
        instruction.then_inc(self.sem, 1)
        self.eng.wait_ge(self.sem, self.i * self.per + (self.base + self.n))

    def enter(self, i, per):
        self.base, self.n, self.i, self.per = self.base + self.n, 0, i, per

    def leave(self, passes):
        assert self.n == self.per, (self.n, self.per)
        self.base, self.n, self.i, self.per = self.base + passes * self.per, 0, 0, 0


def build(nc, x, c, ctx, c_ctx, w_ada, b_ada, norm1_g, norm2_g, w_in, conv_w, conv_b, gate_b, head_g,
          vnorm_g, w_spatial, b_spatial, w_pa, w_pb, w_out, w_ff1, w_ff3, w_ff2, final_g, out):
    def rows_first(w):
        return w.rearrange("o (k p) n -> (o p) k n", p=P)

    x_t, ctx_t, out_t = rows_first(x), rows_first(ctx), rows_first(out)
    ada_v, win_v = rows_first(w_ada), rows_first(w_in)
    pa_v, pb_v, wo_v = rows_first(w_pa), rows_first(w_pb), rows_first(w_out)
    f1_v, f3_v, f2_v = rows_first(w_ff1), rows_first(w_ff3), rows_first(w_ff2)
    ya_dram = nc.dram_tensor("ya_dram", [P, KT, NLAT], F32, kind="Internal").ap()

    es = ExitStack()
    with es:
        def sb(name, shape, dt=F32, stack=es):
            return stack.enter_context(nc.sbuf_tensor(name, shape, dt))

        def sem(name):
            return es.enter_context(nc.semaphore(name))

        ident = sb("ident", [P, P])
        one1 = sb("one1", [P, 1])
        cols = sb("cols", [P, P])
        cols2 = sb("cols2", [P, 16])
        csil = sb("csil", [P, 2, KT])
        mod = sb("mod", [P, 6, KT])
        b1 = sb("b1", [P, 2, 2 * KT])
        a1 = sb("a1", [P, 2, KT])
        a2 = sb("a2", [P, KT])
        note = sb("note", [P, 12])
        rs = sb("rs", [P, 4, 16])
        R_hi = sb("R_hi", [P, KT, NLAT], F32R)
        R_lo = sb("R_lo", [P, KT, NLAT], F32R)
        raw = [sb(f"raw{k}", [P, 4 * CW]) for k in range(2)]
        with ExitStack() as tmp:
            ada_raw = [sb(f"ada_raw{k}", [P, 2 * D], stack=tmp) for k in range(4)]
        whi = [sb(f"whi{k}", [P, 8 * CW], F32R) for k in range(2)]
        wlo = [sb(f"wlo{k}", [P, 8 * CW], F32R) for k in range(2)]

        with ExitStack() as sH:
            ctx_hi = sb("ctx_hi", [P, KT, NCTX], F32R, sH)
            ctx_lo = sb("ctx_lo", [P, KT, NCTX], F32R, sH)
            with ExitStack() as s0:
                xtok = sb("xtok", [P, TT, D], stack=s0)
                xnT = sb("xnT", [P, KT, TT * P], stack=s0)
                rows1 = sb("rows1", [P, P], stack=s0)
                rows2 = sb("rows2", [16, P], stack=s0)
                cth = sb("cth", [P, 2 * KT], stack=s0)
            with ExitStack() as s1:
                mask = sb("mask", [P, 2, L], stack=s1)
                G5 = sb("G5", [P, 5, 8, TT], stack=s1)
                nM = sb("nM", [8, NLAT], stack=s1)
                nMr = sb("nMr", [8, NLAT], stack=s1)
                hc = sb("hc", [P, 5, 2, TT], stack=s1)
                cwh = sb("cwh", [P, 2, 6], stack=s1)
                hgh = sb("hgh", [P, 2], stack=s1)
                selm = sb("selm", [8, 2, P], stack=s1)
                den = sb("den", [P, 2, 4], stack=s1)
                work = sb("work", [P, 2, NLAT + 2 * PAD], stack=s1)
                kcraw = sb("kcraw", [P, NCTX + 2 * PAD], stack=s1)
                qT = sb("qT", [P, NLAT], stack=s1)
                kT = sb("kT", [P, TT * P], stack=s1)
                WB = sb("WB", [P, 2, NLAT], stack=s1)
                ktok = sb("ktok", [P, TT, DQK], stack=s1)
                vaug = sb("vaug", [P, TT, DVA], stack=s1)
                Cst = sb("Cst", [P, 2, 2, DVA], stack=s1)
                junkH = sb("junkH", [P, DV], stack=s1)
                with ExitStack() as s2:
                    jrev = sb("jrev", [P, P], stack=s2)
                    wg = sb("wg", [P, KT, 16], stack=s2)
                    wg_hi = sb("wg_hi", [P, KT, 16], F32R, s2)
                    wg_lo = sb("wg_lo", [P, KT, 16], F32R, s2)
                    gbb = sb("gbb", [P, 16], stack=s2)
                    gt = sb("gt", [P, TT, 2, 2, HEADS], stack=s2)
                    gw = sb("gw", [P, 2, TT, 2 * HEADS], stack=s2)
                    Gp = sb("Gp", [P, 2, 2, TT, 8], stack=s2)
                    urow = sb("urow", [8, TT * P], stack=s2)
                    brow = sb("brow", [8, TT * P], stack=s2)
                    mrow = sb("mrow", [8, TT * P], stack=s2)
                    mpv = sb("mpv", [8, TT + 1], stack=s2)
                    dg8 = sb("dg8", [8, 2, 8, TT], stack=s2)
                    zer = sb("zer", [8, L], stack=s2)
                    ones8 = sb("ones8", [8, P], stack=s2)
                    revr = kT
                kw = sb("kw", [P, 2, TT, DQK], stack=s1)
                Hh = sb("Hh", [P, LT, DV], stack=s1)
                sgo = sb("sgo", [P, 2, NLAT], stack=s1)
        with ExitStack() as sU:
            with ExitStack() as s3:
                V = sb("V", [P, LT, D], stack=s3)
                junkV = sb("junkV", [P, D], stack=s3)
                ada2 = [sb(f"ada2_{k}", [P, D], stack=s3) for k in range(2)]
                Tacc = sb("Tacc", [P, D], stack=s3)
            with ExitStack() as s4:
                xs = sb("xs", [P, LT, D], stack=s4)
            Y_hi = sb("Y_hi", [P, LT, KT, P], F32R, sU)
            with ExitStack() as s5:
                ya_raw = sb("ya_raw", [P, LT, KT, P], stack=s5)
            Y_lo = sb("Y_lo", [P, LT, KT, P], F32R, sU)
            with ExitStack() as s6:
                vn_hi = [sb(f"vn_hi{k}", [P, LT, P], F32R, s6) for k in range(2)]
                vn_lo = [sb(f"vn_lo{k}", [P, LT, P], F32R, s6) for k in range(2)]
                uT = [sb(f"uT{k}", [P, NLAT], stack=s6) for k in range(2)]
                wsp = sb("wsp", [P, 4, P], stack=s6)
                wsp_hi = sb("wsp_hi", [P, 4, P], F32R, s6)
                wsp_lo = sb("wsp_lo", [P, 4, P], F32R, s6)
                bspB = sb("bspB", [P, 4, P], stack=s6)
            Mb = sb("Mb", [P, KT, NLAT], stack=sU)
            sg = sb("sg", [P, NLAT], stack=sU)
        with ExitStack() as sF:
            sb("xs_place", [P, LT, D], stack=sF)
            gB = sb("gB", [P, D], stack=sF)
            diag = sb("diag", [P, KT, P], stack=sF)
            onesP = sb("onesP", [P, P], stack=sF)
            junkF = sb("junkF", [P, D], stack=sF)
            fg = sb("fg", [P, D], stack=sF)
            with ExitStack() as s7:
                xn = sb("xn", [P, LT, D], stack=s7)
            wC_hi = sb("wC_hi", [P, 8 * CW], F32R, sF)
            wC_lo = sb("wC_lo", [P, 8 * CW], F32R, sF)
            f_hi = sb("f_hi", [P, 2, NLAT], F32R, sF)
            f_lo = sb("f_lo", [P, 2, NLAT], F32R, sF)
            sa = sb("sa", [P, 2, NLAT], stack=sF)
            hT = [sb(f"hT{k}", [P, NLAT], stack=sF) for k in range(2)]
        whi.append(wC_hi)
        wlo.append(wC_lo)

        PD = [es.enter_context(nc.psum_tensor(f"PD{s}", [P, 2 * HALF], F32)) for s in range(2)]
        PM = es.enter_context(nc.psum_tensor("PM", [P, 4 * HALF], F32))

        consts = sem("consts")
        vec_in = sem("vec_in")
        gate_in = sem("gate_in")
        x_in = [sem(f"x_in{t}") for t in range(TT)]
        ada_in = [sem(f"ada_in{k}") for k in range(4)]
        raw_in = [sem(f"raw_in{k}") for k in range(2)]
        hi_done = sem("hi_done")
        w_ready = [sem(f"w_ready{k}") for k in range(2)]
        tile_done = sem("tile_done")
        slot_free = [sem(f"slot_free{s}") for s in range(2)]
        dve_own = sem("dve_own")
        act_own = sem("act_own")
        pool_own = sem("pool_own")
        vecT = sem("vecT")
        cols_ready = sem("cols_ready")
        cth_ready = sem("cth_ready")
        csil_ready = sem("csil_ready")
        xn_ready = sem("xn_ready")
        xT_done = sem("xT_done")
        xT_read = [sem(f"xT_read{s}") for s in range(2)]
        ada_mm = sem("ada_mm")
        adarow_ready = sem("adarow_ready")
        adacol_done = sem("adacol_done")
        h_ready = sem("h_ready")
        h_hi = sem("h_hi")
        h_lo = sem("h_lo")
        wg_hi_done = sem("wg_hi_done")
        wg_ready = sem("wg_ready")
        gates_mm = sem("gates_mm")
        sig_arg = sem("sig_arg")
        sig_ln = sem("sig_ln")
        gp_ready = sem("gp_ready")
        grow_done = sem("grow_done")
        row_ready = sem("row_ready")
        gcol_done = sem("gcol_done")
        exp_arg = sem("exp_arg")
        g5_ready = sem("g5_ready")
        head_cols = sem("head_cols")
        conv_done = sem("conv_done")
        th_done = sem("th_done")
        qk_ready = sem("qk_ready")
        nb_done = sem("nb_done")
        nm_ready = sem("nm_ready")
        wb_ready = sem("wb_ready")
        d_ready = sem("d_ready")
        ktr_done = sem("ktr_done")
        ktok_ready = sem("ktok_ready")
        s_done = sem("s_done")
        sw_ready = sem("sw_ready")
        kw_ready = sem("kw_ready")
        qw_ready = sem("qw_ready")
        dc_done = sem("dc_done")
        c_ready = sem("c_ready")
        num_done = sem("num_done")
        h_written = sem("h_written")
        hn_ready = sem("hn_ready")
        yt_done = sem("yt_done")
        sgo_ready = sem("sgo_ready")
        pm_free = sem("pm_free")
        spill = sem("spill")
        small_in = sem("small_in")
        wspT_done = sem("wspT_done")
        wsp_hi_d = sem("wsp_hi_d")
        wsp_ready = sem("wsp_ready")
        ada2_in = [sem(f"ada2_in{k}") for k in range(2)]
        ada2_used = sem("ada2_used")
        T_mm = sem("T_mm")
        mod_ready = sem("mod_ready")
        v_scaled = sem("v_scaled")
        vn_hi_d = sem("vn_hi_d")
        vn_ready = sem("vn_ready")
        sv_done = sem("sv_done")
        y_f32 = sem("y_f32")
        y_hi_d = sem("y_hi_d")
        yb_ready = sem("yb_ready")
        ya_in = [sem(f"ya_in{k}") for k in range(KT)]
        ya_hi_d = sem("ya_hi_d")
        ya_ready = sem("ya_ready")
        sg_used = sem("sg_used")
        m_hi_d = sem("m_hi_d")
        m_ready = sem("m_ready")
        x2_in = sem("x2_in")
        ones_ready = sem("ones_ready")
        diag_ready = sem("diag_ready")
        gB_mm = sem("gB_mm")
        xn2_ready = sem("xn2_ready")
        h2_hi = sem("h2_hi")
        h2_lo = sem("h2_lo")
        sa_ready = sem("sa_ready")
        f_hi_d = sem("f_hi_d")
        f_lo_d = sem("f_lo_d")
        fg_in = sem("fg_in")
        o_ready = sem("o_ready")
        out_done = sem("out_done")

        block = es.enter_context(nc.Block())

        @block.sync
        def _(sp):
            for t in range(TT):
                src = ctx_t[:, t, :] if t < CT else x_t[:, t - CT, :]
                sp.dma_start(xtok[:, t, :], src).then_inc(x_in[t], 16)
            for k in range(KT):
                if k >= 4:
                    sp.wait_ge(ada_mm, k - 3)
                sp.dma_start(ada_raw[k % 4][:, :], ada_v[:, k, 0:2 * D]).then_inc(ada_in[k % 4], 16)

            def load(n, *sources):
                for half in range(2):
                    for view, col, width in sources:
                        sp.lower_ap_dma(view[:, 4 * half:4 * half + 4, ds(col, width)])
                    sp.wait_ge(w_ready[half], n + 1)
                    at = 0
                    for view, col, width in sources:
                        dst = raw[half][:, :].rearrange("p (k n) -> p k n", k=4)[:, :, at:at + width]
                        sp.dma_start(dst, view[:, 4 * half:4 * half + 4, ds(col, width)])\
                            .then_inc(raw_in[half], 16)
                        at += width

            def load_rows(n, block_no):
                for half in range(2):
                    sp.lower_ap_dma(f2_v[:, ds(block_no * 2 + half, 1), :])
                    sp.wait_ge(w_ready[half], n + 1)
                    dst = raw[half][:, :].rearrange("p (o n) -> p o n", o=1)
                    sp.dma_start(dst, f2_v[:, ds(block_no * 2 + half, 1), :]).then_inc(raw_in[half], 16)

            def load_qk(h):
                load(h * 3, (win_v, h * DQK + CQ, DQK), (win_v, h * DQK + CK, DQK))

            def load_vo(h):
                load(h * 3 + 1, (win_v, h * DV + CV, CW))
                load(h * 3 + 2, (win_v, h * DV + CO, CW))

            def spill_ya(h):
                sp.lower_ap_dma(ya_dram[:, ds(h * 2, 2), :])
                sp.wait_ge(pm_free, h * 2 + 4)
                sp.dma_start(ya_dram[:, ds(h * 2, 2), :], sgo[:, :, :]).then_inc(spill, 16)

            load_qk(0)
            with sp.Fori(0, HEADS - 1) as h:
                load_vo(h)
                load_qk(h + 1)
                spill_ya(h)
            load_vo(HEADS - 1)
            load(N_V, (win_v, CVB, CW))
            spill_ya(HEADS - 1)
            with sp.Fori(1, 4) as i:
                load(i + N_V, (win_v, i * CW + CVB, CW))
            with sp.Fori(0, 4) as i:
                load(i + N_U, (win_v, i * CW + CU, CW))
            with sp.Fori(0, 4) as i:
                load(i * 2 + N_PB, (win_v, i * CW + CGB, CW))
                load(i * 2 + (N_PB + 1), (pb_v, i * CW, CW))
            with sp.Fori(0, 4) as i:
                load(i * 2 + N_PA, (win_v, i * CW + CGA, CW))
                load(i * 2 + (N_PA + 1), (pa_v, i * CW, CW))
            with sp.Fori(0, 4) as i:
                load(i + N_O, (wo_v, i * CW, CW))
            load(N_F, (f1_v, 0, CW))
            load(N_F + 1, (f3_v, 0, CW))
            load(N_F + 2, (f1_v, CW, CW))
            with sp.Fori(0, NFB - 2) as r:
                load_rows(r * 3 + (N_F + 3), r)
                load(r * 3 + (N_F + 4), (f3_v, r * CW + CW, CW))
                load(r * 3 + (N_F + 5), (f1_v, r * CW + 2 * CW, CW))
            last = NFB - 2
            load_rows(N_F + 3 + 3 * last, last)
            load(N_F + 4 + 3 * last, (f3_v, (last + 1) * CW, CW))
            load_rows(N_F + 5 + 3 * last, last + 1)
            for t in range(LT):
                sp.wait_ge(o_ready, t + 1)
                sp.dma_start(out_t[:, t, :], xs[:, t, :]).then_inc(out_done, 16)
            sp.wait_ge(out_done, 16 * LT)

        @block.gpsimd
        def _(pool):
            own = Chain(pool, pool_own)
            own.link(nc.gpsimd.memset(ident[:, :], 0.0))
            nc.gpsimd.affine_select(out=ident[:, :], in_=ident[:, :], compare_op=ALU.not_equal, fill=1.0,
                                    base=0, pattern=[[-1, P]], channel_multiplier=1).then_inc(consts, 1)
            nc.gpsimd.memset(one1[:, :], 1.0).then_inc(consts, 1)
            credits = 0
            for s, count in ((w_ready[0], 1), (w_ready[1], 1), (spill, 1), (ada2_used, 2), (mod_ready, 1),
                             (sv_done, 2), (yb_ready, 2), (sg_used, 1)):
                for _ in range(count):
                    nc.gpsimd.memset(note[:, credits:credits + 1], 0.0).then_inc(s, 1)
                    credits += 1
            pool.wait_ge(h_lo, 2 * KT)
            own.link(nc.gpsimd.memset(jrev[:, :], 0.0))
            nc.gpsimd.affine_select(out=jrev[:, :], in_=jrev[:, :], compare_op=ALU.not_equal, fill=1.0,
                                    base=1 - P, pattern=[[1, P]], channel_multiplier=1).then_inc(consts, 1)
            nc.gpsimd.memset(zer[:, :], 0.0).then_inc(consts, 1)
            nc.gpsimd.memset(ones8[:, :], 1.0).then_inc(consts, 1)
            nc.gpsimd.memset(mpv[:, :], 0.0).then_inc(consts, 1)
            nc.gpsimd.memset(Gp[:, :, :, :, :], 0.0).then_inc(consts, 1)
            own.link(nc.gpsimd.memset(mask[:, :, :], 0.0))
            for d, sign in ((0, 1), (1, -1)):
                nc.gpsimd.affine_select(out=mask[:, d, :], in_=mask[:, d, :], compare_op=ALU.is_ge, fill=NEG,
                                        base=0, pattern=[[sign, L]], channel_multiplier=-sign)\
                    .then_inc(consts, 1)
            for pad in (slice(0, PAD), slice(PAD + NLAT, 2 * PAD + NLAT)):
                nc.gpsimd.memset(work[:, :, pad], 0.0).then_inc(consts, 1)
            for pad in (slice(0, PAD), slice(PAD + NCTX, 2 * PAD + NCTX)):
                nc.gpsimd.memset(kcraw[:, pad], 0.0).then_inc(consts, 1)
            nc.gpsimd.memset(vaug[:, :, DV:DVA], 1.0).then_inc(consts, 1)
            with pool.Fori(0, HEADS) as h:
                pool.wait_ge(wb_ready, h + 1)
                pool.wait_ge(qk_ready, h * 2 + 2)
                for d in range(2):
                    nc.gpsimd.tensor_tensor(WB[:, d, :], WB[:, d, :], qT[:, :], ALU.mult)\
                        .then_inc(qw_ready, 1)
                pool.wait_ge(ktok_ready, h * 2 + 2)
                for d in range(2):
                    nc.gpsimd.tensor_tensor(kw[:, d, :, :], ktok[:, :, :],
                                            hc[:, 1, d, :].unsqueeze(2).to_broadcast([P, TT, DQK]),
                                            ALU.mult).then_inc(kw_ready, 1)
            pool.wait_ge(spill, 16 * HEADS + 1)
            pool.dma_start(wsp[:, :, :], w_spatial.rearrange("o g t s -> (o t) g s")).then_inc(small_in, 16)
            pool.dma_start(bspB[:, :, :].rearrange("p g t -> p (g t)"),
                           b_spatial.rearrange("o g t -> o (g t)").to_broadcast([P, 4 * P]))\
                .then_inc(small_in, 16)
            with pool.Fori(0, 4) as i:
                for k in range(KT):
                    pool.wait_ge(ada2_used, i * KT + (k + 1))
                    pool.dma_start(ada2[k % 2][:, :], ada_v[:, k, ds(i * D + 2 * D, D)])\
                        .then_inc(ada2_in[k % 2], 16)
            pool.wait_ge(tile_done, T_PA)
            for k in range(KT):
                pool.dma_start(ya_raw[:, :, k, :], ya_dram[:, k, :].rearrange("p (c t) -> p c t", t=P))\
                    .then_inc(ya_in[k], 16)
            pool.wait_ge(tile_done, T_O)
            pool.wait_ge(m_ready, KT)
            nc.gpsimd.memset(onesP[:, :], 1.0).then_inc(ones_ready, 1)
            for t in range(LT):
                pool.dma_start(xs[:, t, :], x_t[:, t, :]).then_inc(x2_in, 16)
            pool.dma_start(fg[:, :], final_g.rearrange("(o n) -> o n", o=1).to_broadcast([P, D]))\
                .then_inc(fg_in, 16)

        @block.scalar
        def _(act):
            own = Chain(act, act_own)
            for at, v in ((0, c), (8, c_ctx.rearrange("(o n) -> o n", o=1)), (16, norm1_g), (24, norm2_g)):
                act.dma_start(rows1[at:at + KT, :], v.rearrange("o (k p) -> (o k) p", p=P)).then_inc(vec_in, 16)
            act.dma_start(rows1[32:80, :], b_ada.rearrange("o (k p) -> (o k) p", p=P)).then_inc(vec_in, 16)
            act.dma_start(rows1[80:88, :], conv_b.rearrange("o (k p) -> (o k) p", p=P)).then_inc(vec_in, 16)
            act.dma_start(rows1[88:128, :], conv_w.rearrange("o m (k p) -> (o m k) p", p=P)).then_inc(vec_in, 16)
            act.dma_start(rows2[0:8, :], head_g.rearrange("o h (k p) -> (o h k) p", p=P)).then_inc(vec_in, 16)
            act.dma_start(rows2[8:16, :], vnorm_g.rearrange("o (k p) -> (o k) p", p=P)).then_inc(vec_in, 16)

            def split_hi(raw_at, buf, free=None):
                if free is not None:
                    act.wait_ge(tile_done, free)
                for half in range(2):
                    act.wait_ge(raw_in[half], raw_at)
                    nc.scalar.activation(whi[buf][:, half * 4 * CW:(half + 1) * 4 * CW], raw[half][:, :],
                                         ACT.Copy).then_inc(hi_done, 1)

            def split_next(n, buf, free):
                split_hi(n * 16 + 80, buf, free)

            act.wait_ge(cols_ready, 1)
            nc.scalar.activation(cth[:, :], cols[:, 0:2 * KT], ACT.Tanh, scale=0.5).then_inc(cth_ready, 1)
            for t in range(TT):
                act.wait_ge(x_in[t], 16)
                own.link(nc.scalar.activation(xnT[:, 0, 0:D], xtok[:, t, :], ACT.Square,
                                              accum_out=rs[:, 0, t:t + 1]))
            for t in range(0, TT, 2):
                act.wait_ge(xT_done, t + 1)
                nc.scalar.activation(xnT[:, :, t * P:(t + 1) * P],
                                     PD[0][:, :].rearrange("p (k t) -> p k t", k=KT), ACT.Copy)\
                    .then_inc(xT_read[0], 1)
            for n in range(2 * KT):
                k = n % KT
                act.wait_ge(h_ready, n + 1)
                dst, src = (R_hi[:, k, :], xnT[:, k, NCTX:]) if n < KT else (ctx_hi[:, k, :], xnT[:, k, 0:NCTX])
                nc.scalar.activation(dst, src, ACT.Copy).then_inc(h_hi, 1)
            act.wait_ge(h_lo, 2 * KT)
            act.dma_start(wg[:, :, :], win_v[:, :, CG:CG + 16]).then_inc(gate_in, 16)
            act.dma_start(gbb[:, :], gate_b.to_broadcast([P, 16])).then_inc(gate_in, 16)
            act.wait_ge(gate_in, 32)
            nc.scalar.activation(wg_hi[:, :, :], wg[:, :, :], ACT.Copy).then_inc(wg_hi_done, 1)
            act.wait_ge(sig_arg, 1)
            own.link(nc.scalar.activation(gw[:, 1, :, :], gw[:, 0, :, :], ACT.Exp, scale=-1.0))
            nc.scalar.activation(gw[:, 1, :, :], gw[:, 1, :, :], ACT.Ln, bias=1.0).then_inc(sig_ln, 1)
            act.wait_ge(exp_arg, 1)
            nc.scalar.activation(G5[:, 1, :, :], G5[:, 1, :, :], ACT.Exp).then_inc(g5_ready, 1)
            nc.scalar.activation(G5[:, 2, :, :], G5[:, 2, :, :], ACT.Exp, scale=-1.0).then_inc(g5_ready, 1)
            nc.scalar.activation(G5[:, 4, :, :], G5[:, 4, :, :], ACT.Exp).then_inc(g5_ready, 1)
            act.wait_ge(consts, 14)

            with act.Fori(0, HEADS) as h:
                T = h * HT + T_H
                act.wait_ge(slot_free[1], h * 5 + 1)
                split_hi(h * 64 + 32, A)
                act.wait_ge(tile_done, T + 1)
                nc.scalar.activation(work[:, 0, PAD:PAD + NLAT], PD[0][:, :], ACT.Copy).then_inc(slot_free[0], 1)
                split_hi(h * 64 + 48, B)
                act.wait_ge(tile_done, T + 2)
                nc.scalar.activation(work[:, 1, PAD:PAD + NLAT], PD[1][:, :], ACT.Copy).then_inc(slot_free[1], 1)
                act.wait_ge(tile_done, T + 3)
                nc.scalar.activation(kcraw[:, PAD:PAD + NCTX], PD[0][:, 0:NCTX], ACT.Copy)\
                    .then_inc(slot_free[0], 1)
                act.wait_ge(conv_done, h * 3 + 1)
                nc.scalar.activation(WB[:, 0, :], qT[:, :], ACT.Tanh, scale=0.5).then_inc(th_done, 1)

                def v_out(n):
                    s = (3 + n) % 2
                    act.wait_ge(tile_done, T + (4 + n))
                    nc.scalar.activation(vaug[:, 2 * n:2 * n + 2, 0:DV],
                                         PD[s][:, :].rearrange("p (t n) -> p t n", t=2)[:, :, 0:DV],
                                         ACT.Copy).then_inc(slot_free[s], 1)

                act.wait_ge(conv_done, h * 3 + 2)
                nc.scalar.activation(WB[:, 1, :], kT[:, NCTX:], ACT.Tanh, scale=0.5).then_inc(th_done, 1)
                v_out(0)
                act.wait_ge(conv_done, h * 3 + 3)
                nc.scalar.activation(junkH[:, :], kT[:, 0:NCTX], ACT.Tanh, scale=0.5).then_inc(th_done, 1)
                split_hi(h * 64 + 64, A, T + 3)
                v_out(1)
                act.wait_ge(nb_done, h + 1)
                act.wait_ge(qk_ready, h * 2 + 2)
                for d in range(2):
                    act.wait_ge(nm_ready, h * 2 + (d + 1))
                    for t in range(LT):
                        at = d * NLAT + t * L
                        i = nc.scalar.activation(WB[:, d, t * L:(t + 1) * L], PM[:, at:at + L], ACT.Exp,
                                                 bias=hc[:, 3, d, CT + t:CT + t + 1])
                i.then_inc(wb_ready, 1)
                for n in range(2, 5):
                    v_out(n)
                act.wait_ge(nm_ready, h * 2 + 2)
                for d in range(2):
                    for t in range(LT):
                        at = PAD + t * L
                        i = nc.scalar.activation(work[:, d, at:at + L], work[:, d, at:at + L], ACT.Exp,
                                                 bias=hc[:, 0, d, CT + t:CT + t + 1])
                i.then_inc(d_ready, 1)
                for m in range(2):
                    act.wait_ge(spill, h * 16 + 1)
                    act.wait_ge(tile_done, T + (9 + m))
                    nc.scalar.activation(sgo[:, m, :], PD[m][:, :], ACT.Tanh, scale=0.5).then_inc(slot_free[m], 1)
                    act.wait_ge(slot_free[m], h * 5 + 6)
                    nc.scalar.activation(sgo[:, m, :], sgo[:, m, :], ACT.Identity, scale=hgh[:, m:m + 1],
                                         bias=hgh[:, m:m + 1]).then_inc(sgo_ready, 1)
                own.enter(h, LT)
                for n, t in enumerate((4, 3, 5, 2, 6, 1, 7, 0)):
                    act.wait_ge(h_written, h * 16 + (10 + n // 2 * 2))
                    own.link(nc.scalar.activation(junkH[:, :], Hh[:, t, :], ACT.Square,
                                                  accum_out=rs[:, 0, t:t + 1]))
                own.leave(HEADS)

            split_next(N_V, A, T_V)
            act.wait_ge(pm_free, 10)
            with act.Fori(0, 2) as i:
                for cc in range(2):
                    if cc == 0:
                        split_next(i * 2 + (N_V + 1), B, i * 8 + T_V)
                    else:
                        split_next(i * 2 + (N_V + 2), A, i * 8 + (T_V + 4))
                    for p in range(4):
                        act.wait_ge(tile_done, i * 8 + (T_V + 4 * cc + p + 1))
                        nc.scalar.activation(V[:, 2 * p:2 * p + 2, ds(i * (2 * CW) + cc * CW, CW)],
                                             PD[p % 2][:, :].rearrange("p (t n) -> p t n", t=2)[:, :, 0:CW],
                                             ACT.Gelu_apprx_tanh).then_inc(slot_free[p % 2], 1)
            for s in range(2):
                act.wait_ge(slot_free[s], T_U // 2 + 1)
            for t in range(LT):
                own.link(nc.scalar.activation(junkV[:, :], V[:, t, :], ACT.Square, accum_out=rs[:, 0, t:t + 1]))
            act.wait_ge(wspT_done, 1)
            nc.scalar.activation(wsp_hi[:, :, :], PM[:, HALF:2 * HALF].rearrange("p (g t) -> p g t", g=4),
                                 ACT.Copy).then_inc(wsp_hi_d, 1)

            act.wait_ge(v_scaled, LT)
            with act.Fori(0, 2) as i:
                for jj in range(4):
                    b = jj % 2
                    if jj == 0:
                        split_next(i * 2 + (N_U + 1), B, i * 4 + T_U)
                    if jj == 2:
                        split_next(i * 2 + (N_U + 2), A, i * 4 + (T_U + 2))
                    act.wait_ge(sv_done, i * 4 + (jj + 1))
                    nc.scalar.activation(vn_hi[b][:, :, :], V[:, :, ds(i * (4 * P) + jj * P, P)], ACT.Copy)\
                        .then_inc(vn_hi_d, 1)
                    act.wait_ge(yb_ready, i * 4 + (jj + 1))
                    act.wait_ge(tile_done, i * 4 + (T_U + jj + 1))
                    nc.scalar.activation(uT[b][:, :], PD[b][:, :], ACT.Gelu_apprx_tanh).then_inc(slot_free[b], 1)
                    act.wait_ge(y_f32, i * 4 + (jj + 1))
                    nc.scalar.activation(Y_hi[:, :, ds(i * 4 + jj, 1), :],
                                         uT[b][:, :].rearrange("p (c o t) -> p c o t", o=1, t=P), ACT.Copy)\
                        .then_inc(y_hi_d, 1)

            act.wait_ge(yb_ready, KT + 2)
            act.wait_ge(y_hi_d, KT)
            with act.Fori(0, 4) as i:
                for m in range(2):
                    if m == 0:
                        split_next(i * 2 + (N_PB + 1), B, i * 4 + T_PB)
                    else:
                        split_next(i * 2 + (N_PB + 2), A, i * 4 + (T_PB + 2))
                    act.wait_ge(tile_done, i * 4 + (T_PB + m + 1))
                    nc.scalar.activation(Mb[:, ds(i * 2 + m, 1), :],
                                         PD[m][:, :].rearrange("p (o t) -> p o t", o=1), ACT.Tanh, scale=0.5)\
                        .then_inc(slot_free[m], 1)

            for k in range(KT):
                act.wait_ge(ya_in[k], 16)
                nc.scalar.activation(Y_hi[:, :, k, :], ya_raw[:, :, k, :], ACT.Copy).then_inc(ya_hi_d, 1)
            with act.Fori(0, 4) as i:
                for m in range(2):
                    if m == 0:
                        split_next(i * 2 + (N_PA + 1), B, i * 4 + T_PA)
                    else:
                        split_next(i * 2 + (N_PA + 2), A, i * 4 + (T_PA + 3))
                    act.wait_ge(sg_used, i * 2 + (m + 1))
                    act.wait_ge(tile_done, i * 4 + (T_PA + 2 * m + 1))
                    nc.scalar.activation(sg[:, :], PD[0][:, :], ACT.Tanh, scale=0.5).then_inc(slot_free[0], 1)
            for k in range(KT):
                if k == 0:
                    act.wait_ge(tile_done, T_O - 1)
                act.wait_ge(sg_used, k + 2)
                nc.scalar.activation(R_hi[:, k, :], Mb[:, k, :], ACT.Copy, scale=0.5).then_inc(m_hi_d, 1)

            with act.Fori(0, 2) as i:
                split_next(i * 2 + (N_O + 1), B, i * 8 + T_O)
                split_next(i * 2 + (N_O + 2), A, i * 8 + (T_O + 4))
            split_next(N_F + 1, B, T_X)
            for s in range(2):
                act.wait_ge(slot_free[s], T_X // 2 + 1)
            for t in range(LT):
                own.link(nc.scalar.activation(junkF[:, :], xs[:, t, :], ACT.Square, accum_out=rs[:, 0, t:t + 1]))
            for k in range(KT):
                act.wait_ge(slot_free[k % 2], (T_X + k) // 2 + 2)
                nc.scalar.activation(R_hi[:, k, :], hT[k % 2][:, :], ACT.Copy).then_inc(h2_hi, 1)

            def silu_out(free, m):
                act.wait_ge(tile_done, free)
                nc.scalar.activation(sa[:, m, :], PD[m][:, :], ACT.Silu).then_inc(slot_free[m], 1)

            def f_split(count, m):
                act.wait_ge(slot_free[m], count)
                nc.scalar.activation(f_hi[:, m, :], sa[:, m, :], ACT.Copy).then_inc(f_hi_d, 1)

            silu_out(T_F + 1, 0)
            silu_out(T_F + 2, 1)
            split_next(N_F + 2, A, T_F + 2)
            for m in range(2):
                f_split(T_F // 2 + 3, m)

            def ffn(r, last):
                T = r * FT + (T_F + 4)
                n = r * 3 + (N_F + 3)
                split_next(n, C, T - 2)
                for m in range(2):
                    act.wait_ge(f_lo_d, r * 2 + (m + 1))
                    silu_out(T + (m + 1), m)
                split_next(n + 1, B, T)
                if not last:
                    split_next(n + 2, A, T + 2)
                for m in range(2):
                    f_split(r * 6 + (T_F // 2 + 9), m)

            with act.Fori(0, NFB - 2) as r:
                ffn(r, False)
            ffn(NFB - 2, True)
            split_next(N_F + 3 * NFB - 1, C, T_F + 4 + FT * (NFB - 2) + 10)
            for t in range(LT):
                act.wait_ge(slot_free[t % 2], (T_F + 4 + FT * (NFB - 1) + t) // 2 + 2)
                own.link(nc.scalar.activation(junkF[:, :], xs[:, t, :], ACT.Square, accum_out=rs[:, 0, t:t + 1]))

        @block.vector
        def _(dve):
            own = Chain(dve, dve_own)
            v = nc.vector

            def rsqrt(n, count):
                s, a, y, t = (rs[:, k, 0:n] for k in range(4))
                own.link(v.tensor_scalar(a, s, 1.0 / count, EPS, ALU.mult, ALU.add))
                own.link(v.tensor_scalar(t.bitcast(I32), a.bitcast(I32), 1, None, ALU.logical_shift_right))
                own.link(v.tensor_scalar(y.bitcast(I32), t.bitcast(I32), -1.0, MAGIC, ALU.mult, ALU.add))
                for _ in range(3):
                    own.link(v.tensor_tensor(t, y, y, ALU.mult))
                    own.link(v.tensor_tensor(t, t, a, ALU.mult))
                    own.link(v.tensor_scalar(t, t, -0.5, 1.5, ALU.mult, ALU.add))
                    own.link(v.tensor_tensor(y, y, t, ALU.mult))

            def split_lo(n, buf):
                for half in range(2):
                    at = slice(half * 4 * CW, (half + 1) * 4 * CW)
                    dve.wait_ge(hi_done, n * 2 + (half + 1))
                    v.tensor_tensor(wlo[buf][:, at], raw[half][:, :], whi[buf][:, at].bitcast(F32),
                                    ALU.subtract).then_inc(w_ready[half], 1)

            dve.wait_ge(vecT, 1)
            own.link(v.tensor_copy(cols2[:, :], PM[:, P:P + 16]))
            v.tensor_copy(cols[:, :], PM[:, 0:P]).then_inc(cols_ready, 1)
            dve.wait_ge(cth_ready, 1)
            dve.wait_ge(cols_ready, 1)
            flat = csil[:, :, :].rearrange("p s k -> p (s k)")
            own.link(v.scalar_tensor_tensor(out=flat, in0=cth[:, :], scalar=1.0, in1=cols[:, 0:2 * KT],
                                            op0=ALU.add, op1=ALU.mult))
            v.tensor_scalar(flat, flat, 0.5, None, ALU.mult).then_inc(csil_ready, 1)
            dve.wait_ge(act_own, TT)
            rsqrt(TT, D)
            for t in range(TT):
                v.tensor_scalar(xtok[:, t, :], xtok[:, t, :], rs[:, 2, t:t + 1], None, ALU.mult)\
                    .then_inc(xn_ready, 1)
            for t in range(1, TT, 2):
                dve.wait_ge(xT_done, t + 1)
                v.tensor_copy(xnT[:, :, t * P:(t + 1) * P], PD[1][:, :].rearrange("p (k t) -> p k t", k=KT))\
                    .then_inc(xT_read[1], 1)
            dve.wait_ge(ada_mm, KT)
            v.tensor_copy(xtok[0:2, 0:2, :].rearrange("p a b -> p (a b)"), PM[0:2, :]).then_inc(adarow_ready, 1)
            dve.wait_ge(adacol_done, 1)
            own.link(v.tensor_tensor(b1[:, :, :], PM[:, 0:4 * KT].rearrange("p (j s) -> p s j", s=2),
                                     cols[:, 32:48].unsqueeze(1).to_broadcast([P, 2, 2 * KT]), ALU.add))
            for s in range(2):
                own.link(v.scalar_tensor_tensor(out=a1[:, s, :], in0=b1[:, s, KT:2 * KT], scalar=1.0,
                                                in1=cols[:, 16:24], op0=ALU.add, op1=ALU.mult))
            dve.wait_ge(xT_read[0], TT // 2)
            dve.wait_ge(xT_read[1], TT // 2)
            for n in range(2 * KT + 1):
                if n < 2 * KT:
                    k, s = n % KT, n // KT
                    span = xnT[:, k, NCTX:] if s == 0 else xnT[:, k, 0:NCTX]
                    v.tensor_scalar(span, span, a1[:, s, k:k + 1], b1[:, s, k:k + 1], ALU.mult, ALU.add)\
                        .then_inc(h_ready, 1)
                if n >= 1:
                    k, s = (n - 1) % KT, (n - 1) // KT
                    dve.wait_ge(h_hi, n)
                    if s == 0:
                        v.tensor_tensor(R_lo[:, k, :], xnT[:, k, NCTX:], R_hi[:, k, :].bitcast(F32),
                                        ALU.subtract).then_inc(h_lo, 1)
                    else:
                        v.tensor_tensor(ctx_lo[:, k, :], xnT[:, k, 0:NCTX], ctx_hi[:, k, :].bitcast(F32),
                                        ALU.subtract).then_inc(h_lo, 1)

            dve.wait_ge(wg_hi_done, 1)
            v.tensor_tensor(wg_lo[:, :, :], wg[:, :, :], wg_hi[:, :, :].bitcast(F32), ALU.subtract)\
                .then_inc(wg_ready, 1)
            dve.wait_ge(gates_mm, 1)
            own.link(v.tensor_tensor(gt[:, :, :, :, :].rearrange("p t d k h -> p t (d k h)"),
                                     PM[:, 0:16 * TT].rearrange("p (t g) -> p t g", g=16),
                                     gbb[:, :].unsqueeze(1).to_broadcast([P, TT, 16]), ALU.add))
            f_gates = gt[:, :, :, 1, :]
            shape4 = [P, TT, 2, HEADS]
            fw = [gw[:, k, :, :].rearrange("p t (d h) -> p t d h", d=2) for k in range(2)]
            own.link(v.tensor_scalar(fw[0], f_gates, -1.0, None, ALU.mult))
            v.tensor_tensor(fw[0], fw[0], f_gates, ALU.max).then_inc(sig_arg, 1)
            dve.wait_ge(consts, 7)
            for d in range(2):
                v.tensor_copy(Gp[:, 0, d, :, 4 * d:4 * d + 4], gt[:, :, d, 0, :]).then_inc(gp_ready, 1)
            dve.wait_ge(sig_ln, 1)
            for d in range(2):
                own.link(v.tensor_scalar(fw[0][:, :, d, :], f_gates[:, :, d, :], 0.0, None, ALU.min))
                v.tensor_tensor(Gp[:, 1, d, :, 4 * d:4 * d + 4], fw[0][:, :, d, :], fw[1][:, :, d, :],
                                ALU.subtract).then_inc(gp_ready, 1)
            dve.wait_ge(grow_done, 1)
            v.tensor_copy(urow[:, 0:D], PD[0][0:8, :]).then_inc(slot_free[0], 1)
            v.tensor_copy(urow[:, D:], PD[1][0:8, 0:NCTX]).then_inc(slot_free[1], 1)
            for j in range(TT):
                at = slice(j * L, (j + 1) * L)
                i = v.tensor_tensor_scan(brow[:, at], PM[0:8, at], zer[:, :], 0.0, ALU.add, ALU.add)
            own.link(i)
            own.link(v.tensor_tensor(urow[:, :], urow[:, :], brow[:, :], ALU.subtract))
            for j in range(TT):
                at = slice(j * L, (j + 1) * L)
                own.link(v.tensor_tensor_scan(mrow[:, at], urow[:, at], urow[:, at], mpv[:, j:j + 1],
                                              ALU.max, ALU.max))
                end = slice((j + 1) * L - 1, (j + 1) * L)
                own.link(v.tensor_tensor(mpv[:, j + 1:j + 2], brow[:, end], mrow[:, end], ALU.add))
            for k, vals in ((0, mrow[:, L - 1::L]), (1, mpv[:, 0:TT])):
                v.tensor_tensor(dg8[:, k, :, :], ident[0:8, 0:8].unsqueeze(2).to_broadcast([8, 8, TT]),
                                vals.unsqueeze(1).to_broadcast([8, 8, TT]), ALU.mult)
            v.tensor_scalar(nM[:, :], mrow[:, NCTX:], -1.0, None, ALU.mult)
            own.link(v.tensor_tensor(brow[:, :], brow[:, :], mrow[:, :], ALU.add))
            own.link(v.tensor_copy(nMr[:, :], nM[:, NLAT - 1::-1]))
            v.tensor_copy(revr[0:8, 0:NCTX], urow[:, NCTX - 1::-1])
            v.tensor_copy(revr[0:8, NCTX:], urow[:, TT * P - 1:NCTX - 1:-1])
            v.tensor_copy(mrow[:, 0:NCTX], brow[:, NCTX - 1::-1])
            v.tensor_copy(mrow[:, NCTX:], brow[:, TT * P - 1:NCTX - 1:-1]).then_inc(row_ready, 1)
            dve.wait_ge(gcol_done, 1)
            for k, g in ((0, 0), (1, 2)):
                v.tensor_copy(G5[:, g, :, :], PM[:, 80 * k:80 * k + 80].rearrange("p (t r) -> p r t", r=8))
            for k, g in ((0, 4), (1, 3)):
                on_all = PM[:, 160 + 80 * k:240 + 80 * k].rearrange("p (r j) -> p r j", j=TT)
                v.tensor_copy(G5[:, g, 0:4, :], on_all[:, 0:4, :])
                v.tensor_copy(G5[:, g, 4:8, 0:CT], on_all[:, 4:8, CT - 1::-1])
                i = v.tensor_copy(G5[:, g, 4:8, CT:], on_all[:, 4:8, TT - 1:CT - 1:-1])
                i.then_inc(pm_free, 1)
            dve.wait_ge(pm_free, 2)
            own.link(v.tensor_tensor(G5[:, 1, :, :], G5[:, 0, :, :], G5[:, 4, :, :], ALU.subtract))
            v.tensor_tensor(G5[:, 4, :, :], G5[:, 3, :, :], G5[:, 4, :, :], ALU.subtract).then_inc(exp_arg, 1)
            dve.wait_ge(g5_ready, 3)
            dve.wait_ge(consts, 14)

            with dve.Fori(0, HEADS) as h:
                own.enter(h, LINKS_H)
                v.tensor_copy(hc[:, :, :, :],
                              G5[:, :, :, :].rearrange("p g (d h) t -> p g d (h t)", d=2)[:, :, :, ds(h * TT, TT)])
                taps = cols[:, 80:128].rearrange("p (m t) -> p m t", t=8)
                v.tensor_copy(cwh[:, 0, :].unsqueeze(2), taps[:, :, ds(h, 1)])
                v.tensor_copy(cwh[:, 1, :].unsqueeze(2), taps[:, :, ds(h + HEADS, 1)])
                v.tensor_scalar(hgh[:, :], cols2[:, ds(h * 2, 2)], 0.5, None, ALU.mult)
                for d in range(2):
                    i = v.tensor_copy(selm[:, d, :], ident[0:8, ds(h + HEADS * d, 1)].to_broadcast([8, P]))
                i.then_inc(head_cols, 1)
                dve.wait_ge(head_cols, h + 1)
                split_lo(h * 3 + N_H, A)

                def conv(dst, src, which, width):
                    own.link(v.tensor_scalar(dst, src[:, 0:width], cwh[:, which, 1:2], cwh[:, which, 0:1],
                                             ALU.mult, ALU.add))
                    for m in range(1, TAPS):
                        i = v.scalar_tensor_tensor(out=dst, in0=src[:, m:m + width],
                                                   scalar=cwh[:, which, m + 1:m + 2], in1=dst,
                                                   op0=ALU.mult, op1=ALU.add)
                        if m < TAPS - 1:
                            own.link(i)
                    i.then_inc(conv_done, 1)

                dve.wait_ge(slot_free[0], h * 5 + 2)
                conv(qT[:, :], work[:, 0, :], 0, NLAT)
                split_lo(h * 3 + 1, B)
                dve.wait_ge(slot_free[1], h * 5 + 2)
                conv(kT[:, NCTX:], work[:, 1, :], 1, NLAT)
                dve.wait_ge(slot_free[0], h * 5 + 3)
                conv(kT[:, 0:NCTX], kcraw[:, :], 1, NCTX)
                dve.wait_ge(th_done, h * 3 + 1)
                own.link(v.scalar_tensor_tensor(out=qT[:, :], in0=WB[:, 0, :], scalar=1.0, in1=qT[:, :],
                                                op0=ALU.add, op1=ALU.mult))
                v.tensor_scalar(qT[:, :], qT[:, :], QSCALE, None, ALU.mult).then_inc(qk_ready, 1)
                dve.wait_ge(th_done, h * 3 + 3)
                v.scalar_tensor_tensor(out=kT[:, NCTX:], in0=WB[:, 1, :], scalar=1.0, in1=kT[:, NCTX:],
                                       op0=ALU.add, op1=ALU.mult)
                v.scalar_tensor_tensor(out=kT[:, 0:NCTX], in0=junkH[:, :], scalar=1.0, in1=kT[:, 0:NCTX],
                                       op0=ALU.add, op1=ALU.mult).then_inc(qk_ready, 1)
                split_lo(h * 3 + 2, A)
                dve.wait_ge(nb_done, h + 1)
                for d in range(2):
                    v.tensor_tensor(work[:, d, PAD:PAD + NLAT].rearrange("p (c t) -> p c t", t=L),
                                    PM[:, d * NLAT:(d + 1) * NLAT].rearrange("p (c t) -> p c t", t=L),
                                    mask[:, d, :].unsqueeze(1).to_broadcast([P, LT, L]), ALU.add)\
                        .then_inc(nm_ready, 1)
                dve.wait_ge(ktr_done, h + 1)
                v.tensor_copy(ktok[:, 0:CT, :].rearrange("p t d -> p (t d)"), PM[:, 0:NCTX])\
                    .then_inc(ktok_ready, 1)
                v.tensor_copy(ktok[:, CT:, :].rearrange("p t d -> p (t d)"), PM[:, NLAT:2 * NLAT])\
                    .then_inc(ktok_ready, 1)
                dve.wait_ge(s_done, h + 1)
                dve.wait_ge(d_ready, h + 1)
                for d in range(2):
                    v.tensor_tensor(work[:, d, PAD:PAD + NLAT], PM[:, 0:NLAT], work[:, d, PAD:PAD + NLAT],
                                    ALU.mult).then_inc(sw_ready, 1)
                for j in range(TT):
                    for d in range(2):
                        if j == TT - 1:
                            continue
                        bank = PM[:, (2 + d) * HALF:(2 + d) * HALF + DVA - 1]
                        dve.wait_ge(dc_done, h * 18 + (2 * j + d + 1))
                        if j == 0:
                            v.tensor_copy(Cst[:, d, 1, 0:DVA - 1], bank).then_inc(c_ready, 1)
                        else:
                            dve.wait_ge(c_ready, h * 18 + (2 * j + d - 1))
                            t = tile_of(d, j)
                            v.scalar_tensor_tensor(out=Cst[:, d, (j + 1) % 2, 0:DVA - 1],
                                                   in0=Cst[:, d, j % 2, 0:DVA - 1], scalar=hc[:, 4, d, t:t + 1],
                                                   in1=bank, op0=ALU.mult, op1=ALU.add).then_inc(c_ready, 1)
                    if j < CT:
                        continue
                    for d in range(2):
                        t = tile_of(d, j)
                        bank = PM[:, d * HALF:d * HALF + DV]
                        bden = PM[:, d * HALF + DV:d * HALF + DV + 1]
                        dve.wait_ge(num_done, h * 16 + (2 * (j - CT) + d + 1))
                        own.link(v.tensor_scalar(den[:, d, 0:1], bden, -1.0, hc[:, 2, d, t:t + 1],
                                                 ALU.mult, ALU.max))
                        own.link(v.tensor_tensor(den[:, d, 1:2], bden, den[:, d, 0:1], ALU.max))
                        own.link(v.reciprocal(den[:, d, 2:3], den[:, d, 1:2]))
                        first = (j - CT < LT // 2)
                        if first:
                            v.tensor_scalar(Hh[:, t - CT, :], bank, den[:, d, 2:3], None, ALU.mult)\
                                .then_inc(h_written, 1)
                        else:
                            v.scalar_tensor_tensor(out=Hh[:, t - CT, :], in0=bank, scalar=den[:, d, 2:3],
                                                   in1=Hh[:, t - CT, :], op0=ALU.mult, op1=ALU.add)\
                                .then_inc(h_written, 1)
                dve.wait_ge(act_own, h * LT + (TT + 1 + LT))
                rsqrt(LT, DV)
                for t in range(LT):
                    i = v.tensor_scalar(Hh[:, t, :], Hh[:, t, :], rs[:, 2, t:t + 1], None, ALU.mult)
                i.then_inc(hn_ready, 1)
                dve.wait_ge(yt_done, h + 1)
                for m in range(2):
                    dve.wait_ge(sgo_ready, h * 2 + (m + 1))
                    v.tensor_tensor(sgo[:, m, :], PM[:, m * NLAT:(m + 1) * NLAT], sgo[:, m, :], ALU.mult)\
                        .then_inc(pm_free, 1)
                own.leave(HEADS)

            split_lo(N_V, A)
            with dve.Fori(0, 2) as i:
                for cc in range(2):
                    split_lo(i * 2 + (N_V + 1 + cc), B if cc == 0 else A)
                    q = i * 2 + cc
                    for k in range(KT):
                        dve.wait_ge(ada2_in[k % 2], q * 64 + (k // 2 * 16 + 16))
                        if k == 0:
                            v.tensor_scalar(Tacc[:, :], ada2[0][:, :], csil[:, 0, 0:1], None, ALU.mult)\
                                .then_inc(ada2_used, 1)
                        else:
                            dve.wait_ge(ada2_used, q * KT + (k + 2))
                            v.scalar_tensor_tensor(out=Tacc[:, :], in0=ada2[k % 2][:, :],
                                                   scalar=csil[:, 0, k:k + 1], in1=Tacc[:, :],
                                                   op0=ALU.mult, op1=ALU.add).then_inc(ada2_used, 1)
                    dve.wait_ge(T_mm, q + 1)
                    v.tensor_tensor(mod[:, ds(q + 2, 1), :], PM[:, 0:KT].rearrange("p (o k) -> p o k", o=1),
                                    cols[:, ds(q * KT + 48, KT)].unsqueeze(1), ALU.add).then_inc(mod_ready, 1)
            dve.wait_ge(mod_ready, 5)
            own.link(v.scalar_tensor_tensor(out=a2[:, :], in0=mod[:, 4, :], scalar=1.0, in1=cols[:, 24:32],
                                            op0=ALU.add, op1=ALU.mult))
            dve.wait_ge(act_own, TT + 1 + HEADS * LT + LT)
            rsqrt(LT, D)
            for t in range(LT):
                v.tensor_scalar(V[:, t, :], V[:, t, :], rs[:, 2, t:t + 1], None, ALU.mult).then_inc(v_scaled, 1)
            dve.wait_ge(wsp_hi_d, 1)
            v.tensor_tensor(wsp_lo[:, :, :], PM[:, HALF:2 * HALF].rearrange("p (g t) -> p g t", g=4),
                            wsp_hi[:, :, :].bitcast(F32), ALU.subtract).then_inc(wsp_ready, 1)

            dve.wait_ge(small_in, 32)
            with dve.Fori(0, 2) as i:
                own.enter(i, LINKS_U)
                for jj in range(4):
                    b = jj % 2
                    if jj % 2 == 0:
                        split_lo(i * 2 + (N_U + 1 + jj // 2), B if jj == 0 else A)
                    dve.wait_ge(v_scaled, LT)
                    dve.wait_ge(vn_hi_d, i * 4 + (jj + 1))
                    v.tensor_tensor(vn_lo[b][:, :, :], V[:, :, ds(i * (4 * P) + jj * P, P)],
                                    vn_hi[b][:, :, :].bitcast(F32), ALU.subtract).then_inc(vn_ready, 1)
                    dve.wait_ge(sv_done, i * 4 + (jj + 3))
                    half = PM[:, b * NLAT:(b + 1) * NLAT]
                    own.link(v.scalar_tensor_tensor(
                        out=half.rearrange("p (c t) -> p c t", t=P), in0=half.rearrange("p (c t) -> p c t", t=P),
                        scalar=cols2[:, ds(i * 4 + (8 + jj), 1)],
                        in1=bspB[:, ds(i * 2 + jj // 2, 1), :].to_broadcast([P, LT, P]),
                        op0=ALU.mult, op1=ALU.add))
                    dve.wait_ge(slot_free[b], i * 2 + (T_U // 2 + 2 + jj // 2))
                    v.tensor_tensor(uT[b][:, :], half, uT[b][:, :], ALU.mult).then_inc(y_f32, 1)
                    dve.wait_ge(y_hi_d, i * 4 + (jj + 1))
                    v.tensor_tensor(Y_lo[:, :, ds(i * 4 + jj, 1), :],
                                    uT[b][:, :].rearrange("p (c o t) -> p c o t", o=1, t=P),
                                    Y_hi[:, :, ds(i * 4 + jj, 1), :].bitcast(F32), ALU.subtract)\
                        .then_inc(yb_ready, 1)
                own.leave(2)

            with dve.Fori(0, 4) as i:
                for m in range(2):
                    split_lo(i * 2 + (N_PB + 1 + m), B if m == 0 else A)
                for m in range(2):
                    at = Mb[:, ds(i * 2 + m, 1), :]
                    dve.wait_ge(slot_free[m], i * 2 + (T_PB // 2 + 2))
                    dve.wait_ge(tile_done, i * 4 + (T_PB + m + 3))
                    v.scalar_tensor_tensor(out=at, in0=at, scalar=1.0,
                                           in1=PD[m][:, :].rearrange("p (o t) -> p o t", o=1),
                                           op0=ALU.add, op1=ALU.mult).then_inc(slot_free[m], 1)

            for k in range(KT):
                dve.wait_ge(ya_hi_d, k + 1)
                v.tensor_tensor(Y_lo[:, :, k, :], ya_raw[:, :, k, :], Y_hi[:, :, k, :].bitcast(F32),
                                ALU.subtract).then_inc(ya_ready, 1)
            with dve.Fori(0, 4) as i:
                for m in range(2):
                    split_lo(i * 2 + (N_PA + 1 + m), B if m == 0 else A)
                    at = Mb[:, ds(i * 2 + m, 1), :]
                    dve.wait_ge(slot_free[0], i * 2 + (T_PA // 2 + 2 + m))
                    dve.wait_ge(tile_done, i * 4 + (T_PA + 2 * m + 2))
                    v.scalar_tensor_tensor(out=sg[:, :], in0=sg[:, :], scalar=1.0, in1=PD[1][:, :],
                                           op0=ALU.add, op1=ALU.mult).then_inc(slot_free[1], 1)
                    dve.wait_ge(slot_free[1], i * 2 + (T_PA // 2 + 2 + m))
                    v.tensor_tensor(at, at, sg[:, :].unsqueeze(1), ALU.add).then_inc(sg_used, 1)
            for k in range(KT):
                dve.wait_ge(m_hi_d, k + 1)
                v.scalar_tensor_tensor(out=R_lo[:, k, :], in0=Mb[:, k, :], scalar=0.5,
                                       in1=R_hi[:, k, :].bitcast(F32), op0=ALU.mult, op1=ALU.subtract)\
                    .then_inc(m_ready, 1)

            def broadcast_gate(which, count):
                v.tensor_tensor(diag[:, :, :], ident[:, :].unsqueeze(1).to_broadcast([P, KT, P]),
                                mod[:, which, :].unsqueeze(2).to_broadcast([P, KT, P]), ALU.mult)\
                    .then_inc(diag_ready, 1)
                dve.wait_ge(gB_mm, count)
                own.link(v.tensor_copy(gB[:, :], PM[:, 0:D]))

            dve.wait_ge(tile_done, T_O)
            broadcast_gate(2, 1)
            dve.wait_ge(x2_in, 16 * LT)
            with dve.Fori(0, 2) as i:
                own.enter(i, LINKS_O)
                for cc in range(2):
                    split_lo(i * 2 + (N_O + 1 + cc), B if cc == 0 else A)
                    for p in range(4):
                        at = i * (2 * CW) + cc * CW
                        src = PD[p % 2][:, :].rearrange("p (t n) -> p t n", t=2)[:, :, 0:CW]
                        dst = xs[:, 2 * p:2 * p + 2, ds(at, CW)]
                        dve.wait_ge(tile_done, i * 8 + (T_O + 4 * cc + p + 1))
                        own.link(v.tensor_tensor(src, src, gB[:, ds(at, CW)].unsqueeze(1)
                                                 .to_broadcast([P, 2, CW]), ALU.mult))
                        v.tensor_tensor(dst, src, dst, ALU.add).then_inc(slot_free[p % 2], 1)
                own.leave(2)
            split_lo(N_F + 1, B)
            broadcast_gate(5, 2)
            dve.wait_ge(act_own, TT + 1 + HEADS * LT + 2 * LT)
            rsqrt(LT, D)
            for t in range(LT):
                v.tensor_scalar(xn[:, t, :], xs[:, t, :], rs[:, 2, t:t + 1], None, ALU.mult).then_inc(xn2_ready, 1)
            for k in range(KT + 1):
                if k < KT:
                    dve.wait_ge(tile_done, T_X + k + 1)
                    if k >= 2:
                        dve.wait_ge(h2_lo, k - 1)
                    v.tensor_scalar(hT[k % 2][:, :], PD[k % 2][:, :], a2[:, k:k + 1], mod[:, 3, k:k + 1],
                                    ALU.mult, ALU.add).then_inc(slot_free[k % 2], 1)
                if k >= 1:
                    dve.wait_ge(h2_hi, k)
                    v.tensor_tensor(R_lo[:, k - 1, :], hT[(k - 1) % 2][:, :], R_hi[:, k - 1, :].bitcast(F32),
                                    ALU.subtract).then_inc(h2_lo, 1)

            def gate_out(tile, free, m):
                dve.wait_ge(slot_free[m], free)
                dve.wait_ge(tile_done, tile)
                v.tensor_tensor(sa[:, m, :], PD[m][:, :], sa[:, m, :], ALU.mult).then_inc(slot_free[m], 1)

            def f_lo_out(count, m):
                dve.wait_ge(f_hi_d, count)
                v.tensor_tensor(f_lo[:, m, :], sa[:, m, :], f_hi[:, m, :].bitcast(F32), ALU.subtract)\
                    .then_inc(f_lo_d, 1)

            for m in range(2):
                gate_out(T_F + 3 + m, T_F // 2 + 2, m)
            split_lo(N_F + 2, A)
            for m in range(2):
                f_lo_out(m + 1, m)

            def accumulate(tile, t):
                dve.wait_ge(tile_done, tile)
                own.link(v.tensor_tensor(PD[t % 2][:, :], PD[t % 2][:, :], gB[:, :], ALU.mult))
                v.tensor_tensor(xs[:, t, :], PD[t % 2][:, :], xs[:, t, :], ALU.add).then_inc(slot_free[t % 2], 1)

            def ffn(r, last):
                T = r * FT + (T_F + 4)
                n = r * 3 + (N_F + 3)
                split_lo(n, C)
                split_lo(n + 1, B)
                for t in range(LT):
                    accumulate(T + (3 + t), t)
                if not last:
                    split_lo(n + 2, A)
                for m in range(2):
                    gate_out(T + (11 + m), r * 6 + (T_F // 2 + 4), m)
                for m in range(2):
                    f_lo_out(r * 2 + (m + 3), m)

            with dve.Fori(0, NFB - 2) as r:
                own.enter(r, LT)
                ffn(r, False)
                own.leave(NFB - 2)
            ffn(NFB - 2, True)
            split_lo(N_F + 3 * NFB - 1, C)
            for t in range(LT):
                accumulate(T_F + 4 + FT * (NFB - 1) + t + 1, t)
            dve.wait_ge(act_own, TT + 1 + HEADS * LT + 3 * LT)
            rsqrt(LT, D)
            dve.wait_ge(fg_in, 16)
            for t in range(LT):
                v.scalar_tensor_tensor(out=xs[:, t, :], in0=xs[:, t, :], scalar=rs[:, 2, t:t + 1], in1=fg[:, :],
                                       op0=ALU.mult, op1=ALU.mult).then_inc(o_ready, 1)

        @block.tensor
        def _(pe):
            mm = nc.tensor.matmul

            def ready(n, half):
                pe.wait_ge(w_ready[half], n + 2)

            def halves(src, k):
                if src is Y_hi or src is Y_lo:
                    return [src[:, 4 * e:4 * e + 4, k, :] for e in range(2)]
                if src is ctx_hi or src is ctx_lo:
                    return [src[:, k, :]]
                return [src[:, k, e * HALF:(e + 1) * HALF] for e in range(2)]

            def channels(s, n, buf, m, hi, lo, tile_wait=None):
                w = [q[buf][:, :].rearrange("p (k n) -> p k n", k=KT)[:, :, m * P:(m + 1) * P]
                     for q in (whi, wlo)]
                width = NCTX if hi is ctx_hi else HALF
                for k in range(KT):
                    if k % 4 == 0:
                        ready(n, k // 4)
                    if tile_wait is not None:
                        tile_wait(k)
                    for step, (wk, src) in enumerate(((w[0], hi), (w[0], lo), (w[1], hi))):
                        for e, part in enumerate(halves(src, k)):
                            i = mm(PD[s][:, e * HALF:e * HALF + width], wk[:, k, :], part,
                                   start=(k == 0 and step == 0), stop=(k == KT - 1 and step == 2))
                i.then_inc(tile_done, 1)

            def tokens(s, n, buf, hi, lo, tiles, wait=None):
                w = [q[buf][:, :].rearrange("p (k n) -> p k n", k=KT) for q in (whi, wlo)]
                for e, t in enumerate(tiles):
                    at = slice(t * P, (t + 1) * P)
                    for k in range(KT):
                        if k % 4 == 0:
                            ready(n, k // 4)
                        if wait is not None:
                            wait(k)
                        for step, (src, wk) in enumerate(((hi, w[0]), (hi, w[1]), (lo, w[0]))):
                            i = mm(PD[s][:, e * HALF:e * HALF + CW], src[:, k, at], wk[:, k, :],
                                   start=(k == 0 and step == 0), stop=(k == KT - 1 and step == 2))
                i.then_inc(tile_done, 1)

            pe.wait_ge(consts, 2)
            pe.wait_ge(vec_in, 16 * 9)
            nc.tensor.transpose(PM[:, 0:P], rows1[:, :], ident[:, :])
            nc.tensor.transpose(PM[:, P:P + 16], rows2[:, :], ident[0:16, 0:16]).then_inc(vecT, 1)
            for t in range(TT):
                pe.wait_ge(xn_ready, t + 1)
                if t >= 2:
                    pe.wait_ge(xT_read[t % 2], t // 2)
                for k in range(KT):
                    i = nc.tensor.transpose(PD[t % 2][:, k * P:(k + 1) * P], xtok[:, t, k * P:(k + 1) * P],
                                            ident[:, :])
                i.then_inc(xT_done, 1)
            pe.wait_ge(csil_ready, 1)
            for k in range(KT):
                pe.wait_ge(ada_in[k % 4], k // 4 * 16 + 16)
                for e in range(4):
                    i = mm(PM[0:2, e * HALF:(e + 1) * HALF], csil[:, :, k], ada_raw[k % 4][:, e * HALF:(e + 1) * HALF],
                           start=(k == 0), stop=(k == KT - 1))
                i.then_inc(ada_mm, 1)
            pe.wait_ge(adarow_ready, 1)
            for j in range(2 * KT):
                i = mm(PM[:, 2 * j:2 * j + 2], xtok[0:2, j // KT, (j % KT) * P:(j % KT + 1) * P], ident[0:2, 0:2],
                       start=True, stop=True)
            i.then_inc(adacol_done, 1)

            pe.wait_ge(h_lo, 2 * KT)
            pe.wait_ge(wg_ready, 1)
            for t in range(TT):
                hi, lo = (ctx_hi, ctx_lo) if t < CT else (R_hi, R_lo)
                at = slice(t * P, (t + 1) * P) if t < CT else slice((t - CT) * P, (t - CT + 1) * P)
                for k in range(KT):
                    for step, (src, wk) in enumerate(((hi, wg_hi), (hi, wg_lo), (lo, wg_hi))):
                        i = mm(PM[:, 16 * t:16 * t + 16], src[:, k, at], wk[:, k, :],
                               start=(k == 0 and step == 0), stop=(k == KT - 1 and step == 2))
            i.then_inc(gates_mm, 1)
            pe.wait_ge(consts, 3)
            for kind in range(2):
                pe.wait_ge(gp_ready, 2 * kind + 2)
                for j in range(TT):
                    if kind == 1:
                        dst = PM[0:8, j * L:(j + 1) * L]
                    else:
                        dst = PD[j // KT][0:8, (j % KT) * L:(j % KT + 1) * L]
                    for d, order in ((0, ident), (1, jrev)):
                        i = mm(dst, Gp[:, kind, d, tile_of(d, j), :], order[:, :], start=(d == 0), stop=(d == 1))
            i.then_inc(grow_done, 1)
            pe.wait_ge(row_ready, 1)
            pe.wait_ge(consts, 5)
            for kind, (fwd, bwd) in enumerate(((urow, revr), (brow, mrow))):
                for t in range(TT):
                    for d, rows in ((0, fwd), (1, bwd)):
                        at = 80 * kind + 8 * t + 4 * d
                        mm(PM[:, at:at + 4], rows[0:8, t * P:(t + 1) * P], ident[0:8, 4 * d:4 * d + 4],
                           start=True, stop=True)
            mm(PM[:, 160:320], ones8[:, :], dg8[:, :, :, :].rearrange("p k r j -> p (k r j)"),
               start=True, stop=True).then_inc(gcol_done, 1)

            with pe.Fori(0, HEADS) as h:
                def free(c):
                    pe.wait_ge(slot_free[c % 2], h * 5 + (c // 2 + 1))

                n = h * 3 + N_H
                for m in range(2):
                    free(m)
                    channels(m, n, A, m, R_hi, R_lo)
                free(2)
                channels(0, n, A, 1, ctx_hi, ctx_lo)
                pe.wait_ge(head_cols, h + 1)
                pe.wait_ge(pm_free, h * 2 + 2)
                for d, rows in ((0, nM), (1, nMr)):
                    for e in range(2):
                        at = d * NLAT + e * HALF
                        i = mm(PM[:, at:at + HALF], selm[:, d, :], rows[:, e * HALF:(e + 1) * HALF],
                               start=True, stop=True)
                i.then_inc(nb_done, 1)
                free(3)
                tokens(1, n + 1, B, ctx_hi, ctx_lo, (0, 1))
                for p in range(4):
                    free(4 + p)
                    tokens(p % 2, n + 1, B, R_hi, R_lo, (2 * p, 2 * p + 1))
                for m in range(2):
                    free(8 + m)
                    channels(m, n + 2, A, m, R_hi, R_lo)
                pe.wait_ge(qk_ready, h * 2 + 2)
                pe.wait_ge(nm_ready, h * 2 + 2)
                pe.wait_ge(wb_ready, h + 1)
                for t in range(TT):
                    at = t * P if t < CT else NLAT + (t - CT) * P
                    i = nc.tensor.transpose(PM[:, at:at + P], kT[:, t * P:(t + 1) * P], ident[:, :])
                i.then_inc(ktr_done, 1)
                pe.wait_ge(ktok_ready, h * 2 + 1)
                for t in range(LT):
                    i = mm(PM[:, t * L:(t + 1) * L], kT[:, NCTX + t * L:NCTX + (t + 1) * L],
                           qT[:, t * L:(t + 1) * L], start=True, stop=True)
                i.then_inc(s_done, 1)
                pe.wait_ge(ktok_ready, h * 2 + 2)
                pe.wait_ge(kw_ready, h * 2 + 2)
                for s in range(2):
                    pe.wait_ge(slot_free[s], h * 5 + 5)
                for j in range(TT):
                    for d in range(2):
                        if j == TT - 1:
                            continue
                        t = tile_of(d, j)
                        if j >= 1:
                            pe.wait_ge(c_ready, h * 18 + (2 * j + d - 1))
                        mm(PM[:, (2 + d) * HALF:(2 + d) * HALF + DVA - 1], kw[:, d, t, :], vaug[:, t, 0:DVA - 1],
                           start=True, stop=True).then_inc(dc_done, 1)
                    if j < CT:
                        continue
                    if j == CT:
                        pe.wait_ge(sw_ready, h * 2 + 2)
                        pe.wait_ge(qw_ready, h * 2 + 2)
                    for d in range(2):
                        t = tile_of(d, j)
                        lat = (t - CT) * L
                        bank = PM[:, d * HALF:d * HALF + DVA - 1]
                        pe.wait_ge(c_ready, h * 18 + (2 * j + d - 1))
                        if j > CT:
                            pe.wait_ge(h_written, h * 16 + (2 * (j - CT) + d - 1))
                        mm(bank, work[:, d, PAD + lat:PAD + lat + L], vaug[:, t, 0:DVA - 1], start=True, stop=False)
                        mm(bank, WB[:, d, lat:lat + L], Cst[:, d, j % 2, 0:DVA - 1], start=False, stop=True)\
                            .then_inc(num_done, 1)
                pe.wait_ge(hn_ready, h + 1)
                for m in range(2):
                    for t in range(LT):
                        at = m * NLAT + t * P
                        i = nc.tensor.transpose(PM[:, at:at + P], Hh[:, t, m * P:(m + 1) * P], ident[:, :])
                i.then_inc(yt_done, 1)

            def free(T):
                pe.wait_ge(slot_free[T % 2], T // 2 + 1)

            pe.wait_ge(pm_free, 2 * HEADS + 2)
            with pe.Fori(0, 2) as i:
                for cc in range(2):
                    for p in range(4):
                        pe.wait_ge(slot_free[p % 2], i * 4 + (T_V // 2 + 2 * cc + p // 2 + 1))
                        tokens(p % 2, i * 2 + (N_V + cc), cc, R_hi, R_lo, (2 * p, 2 * p + 1))
                    q = i * 2 + cc
                    pe.wait_ge(ada2_used, q * KT + (KT + 2))
                    pe.wait_ge(mod_ready, q + 1)
                    for k in range(KT):
                        last = mm(PM[:, k:k + 1], Tacc[:, k * P:(k + 1) * P], one1[:, :], start=True, stop=True)
                    last.then_inc(T_mm, 1)
            pe.wait_ge(small_in, 32)
            for g in range(4):
                i = nc.tensor.transpose(PM[:, HALF + g * P:HALF + (g + 1) * P], wsp[:, g, :], ident[:, :])
            i.then_inc(wspT_done, 1)

            with pe.Fori(0, 2) as i:
                for jj in range(4):
                    b = jj % 2
                    pe.wait_ge(slot_free[b], i * 2 + (T_U // 2 + jj // 2 + 1))
                    channels(b, i * 2 + (N_U + jj // 2), jj // 2, b, R_hi, R_lo)
                    pe.wait_ge(vn_ready, i * 4 + (jj + 1))
                    pe.wait_ge(wsp_ready, 1)
                    pe.wait_ge(yb_ready, i * 4 + (jj + 1))
                    g = ds(i * 2 + jj // 2, 1)
                    for c8 in range(LT):
                        dst = PM[:, b * NLAT + c8 * P:b * NLAT + (c8 + 1) * P].unsqueeze(1)
                        for step, (src, wk) in enumerate(((vn_hi[b], wsp_hi), (vn_hi[b], wsp_lo),
                                                          (vn_lo[b], wsp_hi))):
                            last = mm(dst, src[:, c8, :], wk[:, g, :], start=(step == 0), stop=(step == 2))
                    last.then_inc(sv_done, 1)

            with pe.Fori(0, 4) as i:
                for m in range(4):
                    pe.wait_ge(slot_free[m % 2], i * 2 + (T_PB // 2 + m // 2 + 1))
                    if m < 2:
                        channels(m, i * 2 + N_PB, A, m, R_hi, R_lo)
                    else:
                        if m == 2:
                            pe.wait_ge(yb_ready, KT + 2)
                        channels(m - 2, i * 2 + (N_PB + 1), B, m - 2, Y_hi, Y_lo)

            with pe.Fori(0, 4) as i:
                for m in range(2):
                    pe.wait_ge(slot_free[0], i * 2 + (T_PA // 2 + m + 1))
                    channels(0, i * 2 + N_PA, A, m, R_hi, R_lo)
                    pe.wait_ge(slot_free[1], i * 2 + (T_PA // 2 + m + 1))
                    channels(1, i * 2 + (N_PA + 1), B, m, Y_hi, Y_lo,
                             (lambda k: pe.wait_ge(ya_ready, k + 1)) if m == 0 else None)

            def broadcast_gate(count):
                pe.wait_ge(diag_ready, count)
                pe.wait_ge(ones_ready, 1)
                for e in range(2):
                    last = mm(PM[:, e * HALF:(e + 1) * HALF], onesP[:, :], diag[:, 4 * e:4 * e + 4, :],
                              start=True, stop=True)
                last.then_inc(gB_mm, 1)

            broadcast_gate(1)
            with pe.Fori(0, 2) as i:
                for cc in range(2):
                    for p in range(4):
                        pe.wait_ge(slot_free[p % 2], i * 4 + (T_O // 2 + 2 * cc + p // 2 + 1))
                        tokens(p % 2, i * 2 + (N_O + cc), cc, R_hi, R_lo, (2 * p, 2 * p + 1),
                               (lambda k: pe.wait_ge(m_ready, k + 1)) if cc + p == 0 else None)
            broadcast_gate(2)
            for t in range(LT):
                pe.wait_ge(xn2_ready, t + 1)
            for k in range(KT):
                free(T_X + k)
                for t in range(LT):
                    last = nc.tensor.transpose(PD[k % 2][:, t * P:(t + 1) * P], xn[:, t, k * P:(k + 1) * P],
                                               ident[:, :])
                last.then_inc(tile_done, 1)

            def down(T, n):
                w = [q[C][:, :].rearrange("p (k n) -> p k n", k=2) for q in (whi, wlo)]
                for t in range(LT):
                    pe.wait_ge(slot_free[t % 2], T[t])
                    at = slice(t * P, (t + 1) * P)
                    for k in range(2):
                        if t == 0:
                            ready(n, k)
                        for step, (src, wk) in enumerate(((f_hi, w[0]), (f_hi, w[1]), (f_lo, w[0]))):
                            for e in range(2):
                                last = mm(PD[t % 2][:, e * HALF:(e + 1) * HALF], src[:, k, at],
                                          wk[:, k, e * HALF:(e + 1) * HALF],
                                          start=(k == 0 and step == 0), stop=(k == 1 and step == 2))
                    last.then_inc(tile_done, 1)

            for m in range(2):
                free(T_F + m)
                channels(m, N_F, A, m, R_hi, R_lo, (lambda k: pe.wait_ge(h2_lo, k + 1)) if m == 0 else None)
            for m in range(2):
                free(T_F + 2 + m)
                channels(m, N_F + 1, B, m, R_hi, R_lo)
            with pe.Fori(0, NFB - 1) as r:
                base = (T_F + 4) // 2 + 1
                n = r * 3 + (N_F + 3)
                for m in range(2):
                    pe.wait_ge(slot_free[m], r * 6 + base)
                    channels(m, n - 1, A, m, R_hi, R_lo)
                pe.wait_ge(f_lo_d, r * 2 + 2)
                down([r * 6 + (base + 1 + t // 2) for t in range(LT)], n)
                for m in range(2):
                    pe.wait_ge(slot_free[m], r * 6 + (base + 5))
                    channels(m, n + 1, B, m, R_hi, R_lo)
            pe.wait_ge(f_lo_d, 2 * NFB)
            T_end = T_F + 4 + FT * (NFB - 1)
            down([(T_end + t) // 2 + 1 for t in range(LT)], N_F + 3 * NFB - 1)


_NAMES = ['x', 'c', 'ctx', 'c_ctx', 'w_ada', 'b_ada', 'norm1_g', 'norm2_g', 'w_in', 'conv_w', 'conv_b', 'gate_b',
          'head_g', 'vnorm_g', 'w_spatial', 'b_spatial', 'w_pa', 'w_pb', 'w_out', 'w_ff1', 'w_ff3', 'w_ff2',
          'final_g']


def kernel(**inputs):
    import concourse.bacc as bacc
    import numpy as np
    from concourse.bass_utils import run_bass_kernel_spmd

    nc = bacc.Bacc("TRN2", target_bir_lowering=False, num_devices=1)
    arrays, aps = {}, []
    for name in _NAMES:
        a = np.ascontiguousarray(inputs[name])
        arrays[f"in_{name}"] = a
        aps.append(nc.dram_tensor(f"in_{name}", a.shape, mybir.dt.from_np(a.dtype), kind="ExternalInput").ap())
    out = nc.dram_tensor("out_x", (1, NLAT, D), F32, kind="ExternalOutput").ap()
    build(nc, *aps, out)
    r = run_bass_kernel_spmd(nc, [arrays], core_ids=[0])
    return r.results[0]["out_x"]
```

```python
from contextlib import ExitStack

import concourse.bass as bass
from concourse import mybir

F32 = mybir.dt.float32
F32R = mybir.dt.float32r
I32 = mybir.dt.int32
ALU = mybir.AluOpType
ACT = mybir.ActivationFunctionType
AX = mybir.AxisListType.X
ds = bass.ds

P = 128
D = 1024
KT = D // P
NLAT, NCTX = 1024, 256
LT, CT = NLAT // P, NCTX // P
TT = LT + CT
HALF = 512
HEADS, DQK, DV = 4, 128, 256
L = 128
DFF = 2816
CW = 256
NFB = DFF // CW
EPS = 1e-6
TAPS = 5
GM = 40
PAD = TAPS // 2
CQ, CK, CV, CO, CG, CU, CVB, CGA, CGB = 0, 512, 1024, 2048, 3072, 3088, 4112, 5136, 6160
NEG = -1.0e30
DVA = DV + 2
QSCALE = 0.25 * DQK ** -0.5

N_H, N_V, N_U, N_PB, N_PA, N_O, N_F = 0, 12, 16, 20, 28, 36, 40
T_H, T_V, T_U, T_PB, T_PA, T_O, T_X, T_F = 0, 40, 56, 64, 80, 88, 104, 112
HT = 10
FT = 12
A, B, C = 0, 1, 2
LINKS_H, LINKS_U, LINKS_O = 76, 4, 8
MAGIC = float(0x5F3759DF)


def tile_of(direction, j):
    if direction == 0:
        return j
    return CT - 1 - j if j < CT else TT + CT - 1 - j


class Chain:

    def __init__(self, eng, semaphore):
        self.eng, self.sem, self.base, self.i, self.per, self.n = eng, semaphore, 0, 0, 0, 0

    def link(self, instruction):
        self.n += 1
        instruction.then_inc(self.sem, 1)
        self.eng.wait_ge(self.sem, self.i * self.per + (self.base + self.n))

    def enter(self, i, per):
        self.base, self.n, self.i, self.per = self.base + self.n, 0, i, per

    def leave(self, passes):
        assert self.n == self.per, (self.n, self.per)
        self.base, self.n, self.i, self.per = self.base + passes * self.per, 0, 0, 0


def build(nc, x, c, ctx, c_ctx, w_ada, b_ada, norm1_g, norm2_g, w_in, conv_w, conv_b, gate_b, head_g,
          vnorm_g, w_spatial, b_spatial, w_pa, w_pb, w_out, w_ff1, w_ff3, w_ff2, final_g, out):
    def rows_first(w):
        return w.rearrange("o (k p) n -> (o p) k n", p=P)

    x_t, ctx_t, out_t = rows_first(x), rows_first(ctx), rows_first(out)
    ada_v, win_v = rows_first(w_ada), rows_first(w_in)
    pa_v, pb_v, wo_v = rows_first(w_pa), rows_first(w_pb), rows_first(w_out)
    f1_v, f3_v, f2_v = rows_first(w_ff1), rows_first(w_ff3), rows_first(w_ff2)
    ya_dram = nc.dram_tensor("ya_dram", [P, KT, NLAT], F32, kind="Internal").ap()

    es = ExitStack()
    with es:
        def sb(name, shape, dt=F32, stack=es):
            return stack.enter_context(nc.sbuf_tensor(name, shape, dt))

        def sem(name):
            return es.enter_context(nc.semaphore(name))

        ident = sb("ident", [P, P])
        one1 = sb("one1", [P, 1])
        gb8 = sb("gb8", [8, 2])
        cols = sb("cols", [P, P])
        cols2 = sb("cols2", [P, 16])
        csil = sb("csil", [P, 2, KT])
        mod = sb("mod", [P, 6, KT])
        b1 = sb("b1", [P, 2, 2 * KT])
        a1 = sb("a1", [P, 2, KT])
        a2 = sb("a2", [P, KT])
        note = sb("note", [P, 16])
        rs = sb("rs", [P, 4, 16])
        R_hi = sb("R_hi", [P, KT, NLAT], F32R)
        with ExitStack() as tmp:
            rows1 = sb("rows1", [P, P], stack=tmp)
            rows2 = sb("rows2", [16, P], stack=tmp)
            wg = sb("wg", [P, KT, 16], stack=tmp)
            wgz = sb("wgz", [P, KT, 2, GM], stack=tmp)
        R_lo = sb("R_lo", [P, KT, NLAT], F32R)
        raw = [sb(f"raw{k}", [P, 4 * CW]) for k in range(2)]
        with ExitStack() as tmp:
            ada_raw = [sb(f"ada_raw{k}", [P, 2 * D], stack=tmp) for k in range(4)]
        whi = [sb(f"whi{k}", [P, 8 * CW], F32R) for k in range(2)]
        wlo = [sb(f"wlo{k}", [P, 8 * CW], F32R) for k in range(2)]

        with ExitStack() as sH:
            ctx_hi = sb("ctx_hi", [P, KT, NCTX], F32R, sH)
            ctx_lo = sb("ctx_lo", [P, KT, NCTX], F32R, sH)
            with ExitStack() as s0:
                xtok = sb("xtok", [P, TT, D], stack=s0)
                xnT = sb("xnT", [P, KT, TT * P], stack=s0)
                cth = sb("cth", [P, 2 * KT], stack=s0)
                wg_hi = sb("wg_hi", [P, KT, 2, GM], F32R, s0)
                wg_lo = sb("wg_lo", [P, KT, 2, GM], F32R, s0)
            with ExitStack() as s1:
                mask = sb("mask", [P, 2, L], stack=s1)
                G5 = sb("G5", [P, 5, 8, TT], stack=s1)
                nM = sb("nM", [8, NLAT], stack=s1)
                nMr = sb("nMr", [8, NLAT], stack=s1)
                hc = sb("hc", [P, 5, 2, TT], stack=s1)
                cwh = sb("cwh", [P, 2, 6], stack=s1)
                hgh = sb("hgh", [P, 2], stack=s1)
                selm = sb("selm", [8, 2, P], stack=s1)
                den = sb("den", [P, 2, 4], stack=s1)
                work = sb("work", [P, 2, NLAT + 2 * PAD], stack=s1)
                kcraw = sb("kcraw", [P, NCTX + 2 * PAD], stack=s1)
                qT = sb("qT", [P, NLAT], stack=s1)
                kT = sb("kT", [P, TT * P], stack=s1)
                WB = sb("WB", [P, 2, NLAT], stack=s1)
                ktok = sb("ktok", [P, TT, DQK], stack=s1)
                vaug = sb("vaug", [P, TT, DVA], stack=s1)
                Cst = sb("Cst", [P, 2, 2, DVA], stack=s1)
                junkH = sb("junkH", [P, DV], stack=s1)
                with ExitStack() as s2:
                    frow = sb("frow", [8, TT * P], stack=s2)
                    lrow = sb("lrow", [8, TT * P], stack=s2)
                    urow = sb("urow", [8, TT * P], stack=s2)
                    brow = sb("brow", [8, TT * P], stack=s2)
                    mrow = sb("mrow", [8, TT * P], stack=s2)
                    mpv = sb("mpv", [8, TT + 1], stack=s2)
                    dg8 = sb("dg8", [8, 2, 8, TT], stack=s2)
                    zer = sb("zer", [8, L], stack=s2)
                    ones8 = sb("ones8", [8, P], stack=s2)
                    revr = kT
                kw = sb("kw", [P, 2, TT, DQK], stack=s1)
                Hh = sb("Hh", [P, LT, DV], stack=s1)
                sgo = sb("sgo", [P, 2, NLAT], stack=s1)
        with ExitStack() as sU:
            with ExitStack() as s3:
                V = sb("V", [P, LT, D], stack=s3)
                junkV = sb("junkV", [P, D], stack=s3)
                ada2 = [sb(f"ada2_{k}", [P, D], stack=s3) for k in range(2)]
                Tacc = sb("Tacc", [P, 4, D], stack=s3)
            with ExitStack() as s4:
                xs = sb("xs", [P, LT, D], stack=s4)
            Y_hi = sb("Y_hi", [P, LT, KT, P], F32R, sU)
            with ExitStack() as s5:
                ya_raw = sb("ya_raw", [P, LT, KT, P], stack=s5)
            Y_lo = sb("Y_lo", [P, LT, KT, P], F32R, sU)
            with ExitStack() as s6:
                vn_hi = [sb(f"vn_hi{k}", [P, LT, P], F32R, s6) for k in range(2)]
                vn_lo = [sb(f"vn_lo{k}", [P, LT, P], F32R, s6) for k in range(2)]
                uT = [sb(f"uT{k}", [P, NLAT], stack=s6) for k in range(2)]
                wsp = sb("wsp", [P, 4, P], stack=s6)
                wsp_hi = sb("wsp_hi", [P, 4, P], F32R, s6)
                wsp_lo = sb("wsp_lo", [P, 4, P], F32R, s6)
                bspB = sb("bspB", [P, 4, P], stack=s6)
            Mb = sb("Mb", [P, KT, NLAT], stack=sU)
            sg = sb("sg", [P, NLAT], stack=sU)
        with ExitStack() as sF:
            sb("xs_place", [P, LT, D], stack=sF)
            g2B = sb("g2B", [P, D], stack=sF)
            junkF = sb("junkF", [P, D], stack=sF)
            fg = sb("fg", [P, D], stack=sF)
            with ExitStack() as s7:
                xn = sb("xn", [P, LT, D], stack=s7)
            wC_hi = sb("wC_hi", [P, 8 * CW], F32R, sF)
            wC_lo = sb("wC_lo", [P, 8 * CW], F32R, sF)
            f_hi = sb("f_hi", [P, 2, NLAT], F32R, sF)
            f_lo = sb("f_lo", [P, 2, NLAT], F32R, sF)
            sa = sb("sa", [P, 2, NLAT], stack=sF)
            hT = [sb(f"hT{k}", [P, NLAT], stack=sF) for k in range(2)]
        whi.append(wC_hi)
        wlo.append(wC_lo)

        PD = [es.enter_context(nc.psum_tensor(f"PD{s}", [P, 2 * HALF], F32)) for s in range(2)]
        PM = es.enter_context(nc.psum_tensor("PM", [P, 4 * HALF], F32))

        consts = sem("consts")
        vec_in = sem("vec_in")
        gate_in = sem("gate_in")
        x_in = [sem(f"x_in{t}") for t in range(TT)]
        ada_in = [sem(f"ada_in{k}") for k in range(4)]
        raw_in = [sem(f"raw_in{k}") for k in range(2)]
        hi_done = sem("hi_done")
        w_ready = [sem(f"w_ready{k}") for k in range(2)]
        tile_done = sem("tile_done")
        slot_free = [sem(f"slot_free{s}") for s in range(2)]
        dve_own = sem("dve_own")
        act_own = sem("act_own")
        pool_own = sem("pool_own")
        vecT = sem("vecT")
        cols_ready = sem("cols_ready")
        cth_ready = sem("cth_ready")
        csil_ready = sem("csil_ready")
        mod1_ready = sem("mod1_ready")
        xn_ready = sem("xn_ready")
        xT_done = sem("xT_done")
        xT_read = [sem(f"xT_read{s}") for s in range(2)]
        ada_mm = sem("ada_mm")
        adarow_ready = sem("adarow_ready")
        adacol_done = sem("adacol_done")
        h_ready = sem("h_ready")
        h_hi = sem("h_hi")
        h_lo = sem("h_lo")
        wgz_ready = sem("wgz_ready")
        wg_hi_done = sem("wg_hi_done")
        f_copied = sem("f_copied")
        wg_ready = sem("wg_ready")
        gates_mm = sem("gates_mm")
        sig_arg = sem("sig_arg")
        sig_ln = sem("sig_ln")
        row_ready = sem("row_ready")
        gcol_done = sem("gcol_done")
        exp_arg = sem("exp_arg")
        g5_ready = sem("g5_ready")
        head_cols = sem("head_cols")
        conv_done = sem("conv_done")
        th_done = sem("th_done")
        qk_ready = sem("qk_ready")
        nb_done = sem("nb_done")
        nm_ready = sem("nm_ready")
        wb_ready = sem("wb_ready")
        d_ready = sem("d_ready")
        ktr_done = sem("ktr_done")
        ktok_ready = sem("ktok_ready")
        s_done = sem("s_done")
        sw_ready = sem("sw_ready")
        kw_ready = sem("kw_ready")
        qw_ready = sem("qw_ready")
        dc_done = sem("dc_done")
        c_ready = sem("c_ready")
        num_done = sem("num_done")
        h_written = sem("h_written")
        hn_ready = sem("hn_ready")
        yt_done = sem("yt_done")
        sgo_ready = sem("sgo_ready")
        pm_free = sem("pm_free")
        spill = sem("spill")
        small_in = sem("small_in")
        wspT_done = sem("wspT_done")
        wsp_hi_d = sem("wsp_hi_d")
        wsp_ready = sem("wsp_ready")
        ada2_in = [sem(f"ada2_in{k}") for k in range(2)]
        ada2_used = sem("ada2_used")
        T_mm = sem("T_mm")
        mod_ready = sem("mod_ready")
        v_scaled = sem("v_scaled")
        vn_hi_d = sem("vn_hi_d")
        vn_ready = sem("vn_ready")
        sv_done = sem("sv_done")
        y_f32 = sem("y_f32")
        y_hi_d = sem("y_hi_d")
        yb_ready = sem("yb_ready")
        ya_in = [sem(f"ya_in{k}") for k in range(KT)]
        ya_hi_d = sem("ya_hi_d")
        ya_ready = sem("ya_ready")
        ga_done = sem("ga_done")
        ga_th = sem("ga_th")
        ga_used = sem("ga_used")
        m_hi_d = sem("m_hi_d")
        m_ready = sem("m_ready")
        x2_in = sem("x2_in")
        gB_mm = sem("gB_mm")
        xn2_ready = sem("xn2_ready")
        h2_hi = sem("h2_hi")
        h2_lo = sem("h2_lo")
        sa_ready = sem("sa_ready")
        f_hi_d = sem("f_hi_d")
        f_lo_d = sem("f_lo_d")
        fg_in = sem("fg_in")
        o_ready = sem("o_ready")
        out_done = sem("out_done")

        block = es.enter_context(nc.Block())

        @block.sync
        def _(sp):
            for t in range(TT):
                src = ctx_t[:, t, :] if t < CT else x_t[:, t - CT, :]
                sp.dma_start(xtok[:, t, :], src).then_inc(x_in[t], 16)
            for k in range(KT):
                if k >= 4:
                    sp.wait_ge(ada_mm, k - 3)
                sp.dma_start(ada_raw[k % 4][:, :], ada_v[:, k, 0:2 * D]).then_inc(ada_in[k % 4], 16)

            def load(n, *sources):
                for half in range(2):
                    for view, col, width in sources:
                        sp.lower_ap_dma(view[:, 4 * half:4 * half + 4, ds(col, width)])
                    sp.wait_ge(w_ready[half], n + 1)
                    at = 0
                    for view, col, width in sources:
                        dst = raw[half][:, :].rearrange("p (k n) -> p k n", k=4)[:, :, at:at + width]
                        sp.dma_start(dst, view[:, 4 * half:4 * half + 4, ds(col, width)])\
                            .then_inc(raw_in[half], 16)
                        at += width

            def load_rows(n, block_no):
                for half in range(2):
                    sp.lower_ap_dma(f2_v[:, ds(block_no * 2 + half, 1), :])
                    sp.wait_ge(w_ready[half], n + 1)
                    dst = raw[half][:, :].rearrange("p (o n) -> p o n", o=1)
                    sp.dma_start(dst, f2_v[:, ds(block_no * 2 + half, 1), :]).then_inc(raw_in[half], 16)

            def load_qk(h):
                load(h * 3, (win_v, h * DQK + CQ, DQK), (win_v, h * DQK + CK, DQK))

            def load_v(h):
                load(h * 3 + 1, (win_v, h * DV + CV, CW))

            def load_o(h):
                load(h * 3 + 2, (win_v, h * DV + CO, CW))

            def spill_ya(h):
                sp.lower_ap_dma(ya_dram[:, ds(h * 2, 2), :])
                sp.wait_ge(pm_free, h * 2 + 4)
                sp.dma_start(ya_dram[:, ds(h * 2, 2), :], sgo[:, :, :]).then_inc(spill, 16)

            load_qk(0)
            load_v(0)
            with sp.Fori(0, HEADS - 1) as h:
                load_o(h)
                load_qk(h + 1)
                load_v(h + 1)
                spill_ya(h)
            load_o(HEADS - 1)
            load(N_V, (win_v, CVB, DQK), (win_v, CVB + DQK, DQK))
            load(N_V + 1, (win_v, CVB + CW, CW))
            spill_ya(HEADS - 1)
            with sp.Fori(2, 4) as i:
                load(i + N_V, (win_v, i * CW + CVB, CW))
            with sp.Fori(0, 4) as i:
                load(i + N_U, (win_v, i * CW + CU, CW))
            with sp.Fori(0, 4) as i:
                load(i * 2 + N_PB, (win_v, i * CW + CGB, CW))
                load(i * 2 + (N_PB + 1), (pb_v, i * CW, CW))
            with sp.Fori(0, 4) as i:
                load(i * 2 + N_PA, (win_v, i * CW + CGA, CW))
                load(i * 2 + (N_PA + 1), (pa_v, i * CW, CW))
            with sp.Fori(0, 4) as i:
                load(i + N_O, (wo_v, i * CW, CW))
            load(N_F, (f1_v, 0, CW))
            load(N_F + 1, (f3_v, 0, CW))
            load(N_F + 2, (f1_v, CW, CW))
            with sp.Fori(0, NFB - 2) as r:
                load_rows(r * 3 + (N_F + 3), r)
                load(r * 3 + (N_F + 4), (f3_v, r * CW + CW, CW))
                load(r * 3 + (N_F + 5), (f1_v, r * CW + 2 * CW, CW))
            last = NFB - 2
            load_rows(N_F + 3 + 3 * last, last)
            load(N_F + 4 + 3 * last, (f3_v, (last + 1) * CW, CW))
            load_rows(N_F + 5 + 3 * last, last + 1)
            for t in range(LT):
                sp.wait_ge(o_ready, t + 1)
                sp.dma_start(out_t[:, t, :], xs[:, t, :]).then_inc(out_done, 16)
            sp.wait_ge(out_done, 16 * LT)

        @block.gpsimd
        def _(pool):
            own = Chain(pool, pool_own)
            own.link(nc.gpsimd.memset(ident[:, :], 0.0))
            nc.gpsimd.affine_select(out=ident[:, :], in_=ident[:, :], compare_op=ALU.not_equal, fill=1.0,
                                    base=0, pattern=[[-1, P]], channel_multiplier=1).then_inc(consts, 1)
            nc.gpsimd.memset(one1[:, :], 1.0).then_inc(consts, 1)
            nc.gpsimd.memset(wgz[:, :, :, :], 0.0).then_inc(consts, 1)
            credits = 0
            for s, count in ((w_ready[0], 1), (w_ready[1], 1), (spill, 1), (ada2_used, 2),
                             (sv_done, 2), (yb_ready, 2), (ga_th, 2), (ga_used, 1),
                             (slot_free[0], 1), (slot_free[1], 1)):
                for _ in range(count):
                    nc.gpsimd.memset(note[:, credits:credits + 1], 0.0).then_inc(s, 1)
                    credits += 1
            pool.wait_ge(h_lo, 2 * KT)
            pool.wait_ge(gates_mm, 1)
            nc.gpsimd.memset(zer[:, :], 0.0).then_inc(consts, 1)
            nc.gpsimd.memset(ones8[:, :], 1.0).then_inc(consts, 1)
            nc.gpsimd.memset(mpv[:, :], 0.0).then_inc(consts, 1)
            own.link(nc.gpsimd.memset(mask[:, :, :], 0.0))
            for d, sign in ((0, 1), (1, -1)):
                nc.gpsimd.affine_select(out=mask[:, d, :], in_=mask[:, d, :], compare_op=ALU.is_ge, fill=NEG,
                                        base=0, pattern=[[sign, L]], channel_multiplier=-sign)\
                    .then_inc(consts, 1)
            for pad in (slice(0, PAD), slice(PAD + NLAT, 2 * PAD + NLAT)):
                nc.gpsimd.memset(work[:, :, pad], 0.0).then_inc(consts, 1)
            for pad in (slice(0, PAD), slice(PAD + NCTX, 2 * PAD + NCTX)):
                nc.gpsimd.memset(kcraw[:, pad], 0.0).then_inc(consts, 1)
            nc.gpsimd.memset(vaug[:, :, DV:DVA], 1.0).then_inc(consts, 1)
            with pool.Fori(0, HEADS) as h:
                pool.wait_ge(wb_ready, h + 1)
                pool.wait_ge(qk_ready, h * 2 + 2)
                for d in range(2):
                    nc.gpsimd.tensor_tensor(WB[:, d, :], WB[:, d, :], qT[:, :], ALU.mult)\
                        .then_inc(qw_ready, 1)
                pool.wait_ge(ktok_ready, h * 2 + 2)
                for d in range(2):
                    nc.gpsimd.tensor_tensor(kw[:, d, :, :], ktok[:, :, :],
                                            hc[:, 1, d, :].unsqueeze(2).to_broadcast([P, TT, DQK]),
                                            ALU.mult).then_inc(kw_ready, 1)
            pool.wait_ge(spill, 16 * HEADS + 1)
            pool.dma_start(wsp[:, :, :], w_spatial.rearrange("o g t s -> (o t) g s")).then_inc(small_in, 16)
            pool.dma_start(bspB[:, :, :].rearrange("p g t -> p (g t)"),
                           b_spatial.rearrange("o g t -> o (g t)").to_broadcast([P, 4 * P]))\
                .then_inc(small_in, 16)
            with pool.Fori(0, 4) as i:
                for k in range(KT):
                    pool.wait_ge(ada2_used, i * KT + (k + 1))
                    pool.dma_start(ada2[k % 2][:, :], ada_v[:, k, ds(i * D + 2 * D, D)])\
                        .then_inc(ada2_in[k % 2], 16)
            pool.wait_ge(tile_done, T_PA)
            for k in range(KT):
                pool.dma_start(ya_raw[:, :, k, :], ya_dram[:, k, :].rearrange("p (c t) -> p c t", t=P))\
                    .then_inc(ya_in[k], 16)
            pool.wait_ge(tile_done, T_O)
            for t in range(LT):
                pool.dma_start(xs[:, t, :], x_t[:, t, :]).then_inc(x2_in, 16)
            pool.dma_start(fg[:, :], final_g.rearrange("(o n) -> o n", o=1).to_broadcast([P, D]))\
                .then_inc(fg_in, 16)

        @block.scalar
        def _(act):
            own = Chain(act, act_own)
            for at, v in ((0, c), (8, c_ctx.rearrange("(o n) -> o n", o=1)), (16, norm1_g), (24, norm2_g)):
                act.dma_start(rows1[at:at + KT, :], v.rearrange("o (k p) -> (o k) p", p=P)).then_inc(vec_in, 16)
            act.dma_start(rows1[32:80, :], b_ada.rearrange("o (k p) -> (o k) p", p=P)).then_inc(vec_in, 16)
            act.dma_start(rows1[80:88, :], conv_b.rearrange("o (k p) -> (o k) p", p=P)).then_inc(vec_in, 16)
            act.dma_start(rows1[88:128, :], conv_w.rearrange("o m (k p) -> (o m k) p", p=P)).then_inc(vec_in, 16)
            act.dma_start(rows2[0:8, :], head_g.rearrange("o h (k p) -> (o h k) p", p=P)).then_inc(vec_in, 16)
            act.dma_start(rows2[8:16, :], vnorm_g.rearrange("o (k p) -> (o k) p", p=P)).then_inc(vec_in, 16)

            act.dma_start(wg[:, :, :], win_v[:, :, CG:CG + 16]).then_inc(gate_in, 16)
            for d in range(2):
                for kind in range(2):
                    at = 8 * d + 4 * kind
                    act.dma_start(gb8[4 * d:4 * d + 4, kind:kind + 1],
                                  gate_b[:, at:at + 4].rearrange("o (h e) -> (o h) e", e=1)).then_inc(gate_in, 16)

            def split_hi(raw_at, buf, free=None):
                if free is not None:
                    act.wait_ge(tile_done, free)
                for half in range(2):
                    act.wait_ge(raw_in[half], raw_at)
                    nc.scalar.activation(whi[buf][:, half * 4 * CW:(half + 1) * 4 * CW], raw[half][:, :],
                                         ACT.Copy).then_inc(hi_done, 1)

            def split_next(n, buf, free):
                split_hi(n * 16 + 96, buf, free)

            for t in range(TT):
                if t == 7:
                    act.wait_ge(cols_ready, 1)
                    nc.scalar.activation(cth[:, :], cols[:, 0:2 * KT], ACT.Tanh, scale=0.5).then_inc(cth_ready, 1)
                act.wait_ge(x_in[t], 16)
                own.link(nc.scalar.activation(xnT[:, 0, 0:D], xtok[:, t, :], ACT.Square,
                                              accum_out=rs[:, 0, t:t + 1]))
            for t in range(TT):
                act.wait_ge(xT_done, t + 1)
                nc.scalar.activation(xnT[:, :, t * P:(t + 1) * P],
                                     PD[t % 2][:, :].rearrange("p (k t) -> p k t", k=KT), ACT.Copy)\
                    .then_inc(xT_read[t % 2], 1)
            act.wait_ge(wgz_ready, 4)
            nc.scalar.activation(wg_hi[:, :, :, :], wgz[:, :, :, :], ACT.Copy).then_inc(wg_hi_done, 1)
            act.wait_ge(mod1_ready, 1)
            act.wait_ge(xT_read[1], TT // 2)
            act.wait_ge(xT_read[0], TT // 2)
            for k in range(KT):
                for s, dst, src in ((0, R_hi, xnT[:, k, NCTX:]), (1, ctx_hi, xnT[:, k, 0:NCTX])):
                    nc.scalar.activation(dst[:, k, :], src, ACT.Identity, scale=a1[:, s, k:k + 1],
                                         bias=b1[:, s, k:k + 1]).then_inc(h_hi, 1)
            act.wait_ge(ada_mm, KT)
            split_hi(32, A)
            split_hi(48, B)
            act.wait_ge(gates_mm, 1)
            for (at, width), src in (((0, NCTX), PM[32:GM, NLAT:NLAT + NCTX]), ((NCTX, NLAT), PM[32:GM, 0:NLAT])):
                nc.scalar.activation(frow[:, at:at + width], src, ACT.Copy).then_inc(f_copied, 1)
            act.wait_ge(sig_arg, 1)
            own.link(nc.scalar.activation(lrow[:, :], lrow[:, :], ACT.Exp, scale=-1.0))
            nc.scalar.activation(lrow[:, :], lrow[:, :], ACT.Ln, bias=1.0).then_inc(sig_ln, 1)
            act.wait_ge(exp_arg, 1)
            nc.scalar.activation(G5[:, 1, :, :], G5[:, 1, :, :], ACT.Exp).then_inc(g5_ready, 1)
            nc.scalar.activation(G5[:, 2, :, :], G5[:, 2, :, :], ACT.Exp, scale=-1.0).then_inc(g5_ready, 1)
            nc.scalar.activation(G5[:, 4, :, :], G5[:, 4, :, :], ACT.Exp).then_inc(g5_ready, 1)
            act.wait_ge(consts, 13)

            with act.Fori(0, HEADS) as h:
                T = h * HT + T_H
                act.wait_ge(tile_done, T + 1)
                nc.scalar.activation(work[:, 0, PAD:PAD + NLAT], PD[0][:, :], ACT.Copy).then_inc(slot_free[0], 1)
                act.wait_ge(tile_done, T + 2)
                nc.scalar.activation(work[:, 1, PAD:PAD + NLAT], PD[1][:, :], ACT.Copy).then_inc(slot_free[1], 1)
                act.wait_ge(tile_done, T + 3)
                nc.scalar.activation(kcraw[:, PAD:PAD + NCTX], PD[0][:, 0:NCTX], ACT.Copy)\
                    .then_inc(slot_free[0], 1)
                act.wait_ge(conv_done, h * 3 + 1)
                nc.scalar.activation(WB[:, 0, :], qT[:, :], ACT.Tanh, scale=0.5).then_inc(th_done, 1)

                def v_out(n):
                    s = (3 + n) % 2
                    act.wait_ge(tile_done, T + (4 + n))
                    nc.scalar.activation(vaug[:, 2 * n:2 * n + 2, 0:DV],
                                         PD[s][:, :].rearrange("p (t n) -> p t n", t=2)[:, :, 0:DV],
                                         ACT.Copy).then_inc(slot_free[s], 1)

                act.wait_ge(conv_done, h * 3 + 2)
                nc.scalar.activation(WB[:, 1, :], kT[:, NCTX:], ACT.Tanh, scale=0.5).then_inc(th_done, 1)
                v_out(0)
                act.wait_ge(conv_done, h * 3 + 3)
                nc.scalar.activation(junkH[:, :], kT[:, 0:NCTX], ACT.Tanh, scale=0.5).then_inc(th_done, 1)
                split_hi(h * 64 + 64, A, T + 3)
                v_out(1)
                act.wait_ge(nb_done, h + 1)
                act.wait_ge(qk_ready, h * 2 + 2)
                for d in range(2):
                    act.wait_ge(nm_ready, h * 2 + (d + 1))
                    for t in range(LT):
                        at = d * NLAT + t * L
                        i = nc.scalar.activation(WB[:, d, t * L:(t + 1) * L], PM[:, at:at + L], ACT.Exp,
                                                 bias=hc[:, 3, d, CT + t:CT + t + 1])
                i.then_inc(wb_ready, 1)
                for n in range(2, 5):
                    v_out(n)
                act.wait_ge(nm_ready, h * 2 + 2)
                for d in range(2):
                    for t in range(LT):
                        at = PAD + t * L
                        i = nc.scalar.activation(work[:, d, at:at + L], work[:, d, at:at + L], ACT.Exp,
                                                 bias=hc[:, 0, d, CT + t:CT + t + 1])
                i.then_inc(d_ready, 1)
                for m in range(2):
                    act.wait_ge(spill, h * 16 + 1)
                    act.wait_ge(tile_done, T + (9 + m))
                    nc.scalar.activation(sgo[:, m, :], PD[m][:, :], ACT.Tanh, scale=0.5).then_inc(slot_free[m], 1)
                    act.wait_ge(slot_free[m], h * 5 + 6)
                    nc.scalar.activation(sgo[:, m, :], sgo[:, m, :], ACT.Identity, scale=hgh[:, m:m + 1],
                                         bias=hgh[:, m:m + 1]).then_inc(sgo_ready, 1)
                split_hi(h * 64 + 96, A)
                split_hi(h * 64 + 112, B)
                own.enter(h, LT)
                for n, t in enumerate((4, 3, 5, 2, 6, 1, 7, 0)):
                    act.wait_ge(h_written, h * 16 + (10 + n // 2 * 2))
                    own.link(nc.scalar.activation(junkH[:, :], Hh[:, t, :], ACT.Square,
                                                  accum_out=rs[:, 0, t:t + 1]))
                own.leave(HEADS)

            act.wait_ge(pm_free, 10)
            with act.Fori(0, 2) as i:
                for cc in range(2):
                    for p in range(4):
                        act.wait_ge(tile_done, i * 8 + (T_V + 4 * cc + p + 1))
                        nc.scalar.activation(V[:, 2 * p:2 * p + 2, ds(i * (2 * CW) + cc * CW, CW)],
                                             PD[p % 2][:, :].rearrange("p (t n) -> p t n", t=2)[:, :, 0:CW],
                                             ACT.Gelu_apprx_tanh).then_inc(slot_free[p % 2], 1)
                    split_next(i * 2 + (N_V + 2 + cc), cc, i * 8 + (T_V + 4 * cc + 4))
            for s in range(2):
                act.wait_ge(slot_free[s], T_U // 2 + 1)
            for t in range(LT):
                own.link(nc.scalar.activation(junkV[:, :], V[:, t, :], ACT.Square, accum_out=rs[:, 0, t:t + 1]))
            act.wait_ge(wspT_done, 1)
            nc.scalar.activation(wsp_hi[:, :, :], PM[:, HALF:2 * HALF].rearrange("p (g t) -> p g t", g=4),
                                 ACT.Copy).then_inc(wsp_hi_d, 1)

            act.wait_ge(v_scaled, LT)
            with act.Fori(0, 2) as i:
                for hh in range(2):
                    for jj in (2 * hh, 2 * hh + 1):
                        b = jj % 2
                        act.wait_ge(sv_done, i * 4 + (jj + 1))
                        nc.scalar.activation(vn_hi[b][:, :, :], V[:, :, ds(i * (4 * P) + jj * P, P)], ACT.Copy)\
                            .then_inc(vn_hi_d, 1)
                    for jj in (2 * hh, 2 * hh + 1):
                        b = jj % 2
                        act.wait_ge(yb_ready, i * 4 + (jj + 1))
                        act.wait_ge(tile_done, i * 4 + (T_U + jj + 1))
                        nc.scalar.activation(uT[b][:, :], PD[b][:, :], ACT.Gelu_apprx_tanh)\
                            .then_inc(slot_free[b], 1)
                    for jj in (2 * hh, 2 * hh + 1):
                        b = jj % 2
                        act.wait_ge(y_f32, i * 4 + (jj + 1))
                        nc.scalar.activation(Y_hi[:, :, ds(i * 4 + jj, 1), :],
                                             uT[b][:, :].rearrange("p (c o t) -> p c o t", o=1, t=P), ACT.Copy)\
                            .then_inc(y_hi_d, 1)
                    split_next(i * 2 + (N_U + 2 + hh), hh, i * 4 + (T_U + 2 * hh + 2))

            act.wait_ge(yb_ready, KT + 2)
            act.wait_ge(y_hi_d, KT)
            with act.Fori(0, 4) as i:
                for m in range(2):
                    act.wait_ge(tile_done, i * 4 + (T_PB + m + 1))
                    nc.scalar.activation(Mb[:, ds(i * 2 + m, 1), :],
                                         PD[m][:, :].rearrange("p (o t) -> p o t", o=1), ACT.Tanh, scale=0.5)\
                        .then_inc(slot_free[m], 1)
                split_next(i * 2 + (N_PB + 2), A, i * 4 + (T_PB + 2))
                split_next(i * 2 + (N_PB + 3), B, i * 4 + (T_PB + 4))

            for k in range(KT):
                act.wait_ge(ya_in[k], 16)
                nc.scalar.activation(Y_hi[:, :, k, :], ya_raw[:, :, k, :], ACT.Copy).then_inc(ya_hi_d, 1)

            def m_hi(k):
                act.wait_ge(slot_free[k % 2], (T_PA + k) // 2 + 2)
                nc.scalar.activation(R_hi[:, k, :], Mb[:, k, :], ACT.Copy, scale=0.5).then_inc(m_hi_d, 1)

            def gates_a(i, last):
                for m in range(2):
                    act.wait_ge(ga_done, i * 2 + (m + 1))
                    act.wait_ge(ga_used, i * 2 + (m + 1))
                    nc.scalar.activation(sg[:, :], PM[:, m * NLAT:(m + 1) * NLAT], ACT.Tanh, scale=0.5)\
                        .then_inc(ga_th, 1)
                split_next(i * 2 + (N_PA + 2), A, None)
                if last:
                    for k in range(KT):
                        m_hi(k)
                split_next(i * 2 + (N_PA + 3), B, i * 2 + (T_PA + 2))

            with act.Fori(0, 3) as i:
                gates_a(i, False)
            gates_a(3, True)

            with act.Fori(0, 2) as i:
                for cc in range(2):
                    split_next(i * 2 + (N_O + 2 + cc), cc, i * 8 + (T_O + 4 * cc + 4))
            for s in range(2):
                act.wait_ge(slot_free[s], T_X // 2 + 1)
            for t in range(LT):
                own.link(nc.scalar.activation(junkF[:, :], xs[:, t, :], ACT.Square, accum_out=rs[:, 0, t:t + 1]))
            for k in range(KT):
                act.wait_ge(slot_free[k % 2], (T_X + k) // 2 + 2)
                nc.scalar.activation(R_hi[:, k, :], hT[k % 2][:, :], ACT.Copy).then_inc(h2_hi, 1)

            def silu_out(free, m):
                act.wait_ge(tile_done, free)
                nc.scalar.activation(sa[:, m, :], PD[m][:, :], ACT.Silu).then_inc(slot_free[m], 1)

            def f_split(count, m):
                act.wait_ge(slot_free[m], count)
                nc.scalar.activation(f_hi[:, m, :], sa[:, m, :], ACT.Copy).then_inc(f_hi_d, 1)

            silu_out(T_F + 1, 0)
            silu_out(T_F + 2, 1)
            split_next(N_F + 2, A, T_F + 2)
            for m in range(2):
                f_split(T_F // 2 + 3, m)

            def ffn(r, last):
                T = r * FT + (T_F + 4)
                n = r * 3 + (N_F + 3)
                split_next(n, C, T - 2)
                for m in range(2):
                    act.wait_ge(f_lo_d, r * 2 + (m + 1))
                    silu_out(T + (m + 1), m)
                split_next(n + 1, B, T)
                if not last:
                    split_next(n + 2, A, T + 2)
                for m in range(2):
                    f_split(r * 6 + (T_F // 2 + 9), m)

            with act.Fori(0, NFB - 2) as r:
                ffn(r, False)
            ffn(NFB - 2, True)
            split_next(N_F + 3 * NFB - 1, C, T_F + 4 + FT * (NFB - 2) + 10)
            for t in range(LT):
                act.wait_ge(slot_free[t % 2], (T_F + 4 + FT * (NFB - 1) + t) // 2 + 2)
                own.link(nc.scalar.activation(junkF[:, :], xs[:, t, :], ACT.Square, accum_out=rs[:, 0, t:t + 1]))

        @block.vector
        def _(dve):
            own = Chain(dve, dve_own)
            v = nc.vector

            def rsqrt(n, count, first=0):
                s, a, y, t = (rs[:, k, first:n] for k in range(4))
                own.link(v.tensor_scalar(a, s, 1.0 / count, EPS, ALU.mult, ALU.add))
                own.link(v.tensor_scalar(t.bitcast(I32), a.bitcast(I32), 1, None, ALU.logical_shift_right))
                own.link(v.tensor_scalar(y.bitcast(I32), t.bitcast(I32), -1.0, MAGIC, ALU.mult, ALU.add))
                for _ in range(3):
                    own.link(v.tensor_tensor(t, y, y, ALU.mult))
                    own.link(v.tensor_tensor(t, t, a, ALU.mult))
                    own.link(v.tensor_scalar(t, t, -0.5, 1.5, ALU.mult, ALU.add))
                    own.link(v.tensor_tensor(y, y, t, ALU.mult))

            def split_lo(n, buf, halves=(0, 1)):
                for half in halves:
                    at = slice(half * 4 * CW, (half + 1) * 4 * CW)
                    dve.wait_ge(hi_done, n * 2 + (half + 1))
                    v.tensor_tensor(wlo[buf][:, at], raw[half][:, :], whi[buf][:, at].bitcast(F32),
                                    ALU.subtract).then_inc(w_ready[half], 1)

            for first, end in ((0, 4), (4, 7), (7, TT)):
                dve.wait_ge(act_own, end)
                rsqrt(end, D, first)
                for t in range(first, end):
                    v.tensor_scalar(xtok[:, t, :], xtok[:, t, :], rs[:, 2, t:t + 1], None, ALU.mult)\
                        .then_inc(xn_ready, 1)
                if first == 0:
                    dve.wait_ge(vecT, 1)
                    own.link(v.tensor_copy(cols2[:, :], PM[:, P:P + 16]))
                    v.tensor_copy(cols[:, :], PM[:, 0:P]).then_inc(cols_ready, 1)
                    dve.wait_ge(cth_ready, 1)
                    dve.wait_ge(cols_ready, 1)
                    flat = csil[:, :, :].rearrange("p s k -> p (s k)")
                    own.link(v.scalar_tensor_tensor(out=flat, in0=cth[:, :], scalar=1.0, in1=cols[:, 0:2 * KT],
                                                    op0=ALU.add, op1=ALU.mult))
                    v.tensor_scalar(flat, flat, 0.5, None, ALU.mult).then_inc(csil_ready, 1)
            dve.wait_ge(gate_in, 16 * 5)
            dve.wait_ge(consts, 3)
            for kind in range(2):
                for d in range(2):
                    at = 32 * kind + 4 * d
                    i = v.tensor_copy(wgz[:, :, d, at:at + 4], wg[:, :, 8 * d + 4 * kind:8 * d + 4 * kind + 4])
                    i.then_inc(wgz_ready, 1)
            dve.wait_ge(wg_hi_done, 1)
            v.tensor_tensor(wg_lo[:, :, :, :], wgz[:, :, :, :], wg_hi[:, :, :, :].bitcast(F32), ALU.subtract)\
                .then_inc(wg_ready, 1)
            dve.wait_ge(ada_mm, KT)
            v.tensor_copy(xtok[0:2, 0:2, :].rearrange("p a b -> p (a b)"), PM[0:2, :]).then_inc(adarow_ready, 1)
            dve.wait_ge(adacol_done, 1)
            own.link(v.tensor_tensor(b1[:, :, :], PM[:, 0:4 * KT].rearrange("p (j s) -> p s j", s=2),
                                     cols[:, 32:48].unsqueeze(1).to_broadcast([P, 2, 2 * KT]), ALU.add))
            for s in range(2):
                i = v.scalar_tensor_tensor(out=a1[:, s, :], in0=b1[:, s, KT:2 * KT], scalar=1.0,
                                           in1=cols[:, 16:24], op0=ALU.add, op1=ALU.mult)
                if s == 0:
                    own.link(i)
            i.then_inc(mod1_ready, 1)
            dve.wait_ge(mod1_ready, 1)
            dve.wait_ge(xT_read[0], TT // 2)
            dve.wait_ge(xT_read[1], TT // 2)
            h32 = xtok[:, :, :].rearrange("p t n -> p (t n)")
            for n in range(2 * KT + 1):
                if n < 2 * KT:
                    k, s = n // 2, n % 2
                    src = xnT[:, k, NCTX:] if s == 0 else xnT[:, k, 0:NCTX]
                    at = k * TT * P + (0 if s == 0 else NLAT)
                    v.tensor_scalar(h32[:, at:at + (NLAT if s == 0 else NCTX)], src, a1[:, s, k:k + 1],
                                    b1[:, s, k:k + 1], ALU.mult, ALU.add).then_inc(h_ready, 1)
                if n >= 1:
                    k, s = (n - 1) // 2, (n - 1) % 2
                    at = k * TT * P + (0 if s == 0 else NLAT)
                    dve.wait_ge(h_hi, n)
                    dve.wait_ge(h_ready, n)
                    hi, lo = ((R_hi, R_lo), (ctx_hi, ctx_lo))[s]
                    v.tensor_tensor(lo[:, k, :], h32[:, at:at + (NLAT if s == 0 else NCTX)],
                                    hi[:, k, :].bitcast(F32), ALU.subtract).then_inc(h_lo, 1)
            split_lo(N_H, A)
            split_lo(N_H + 1, B)

            dve.wait_ge(gates_mm, 1)
            own.link(v.tensor_scalar(urow[:, 0:NCTX], PM[0:8, NLAT:NLAT + NCTX], gb8[:, 0:1], None, ALU.add))
            own.link(v.tensor_scalar(urow[:, NCTX:], PM[0:8, 0:NLAT], gb8[:, 0:1], None, ALU.add))
            dve.wait_ge(f_copied, 2)
            own.link(v.tensor_scalar(frow[:, :], frow[:, :], gb8[:, 1:2], None, ALU.add))
            v.scalar_tensor_tensor(out=lrow[:, :], in0=frow[:, :], scalar=-1.0, in1=frow[:, :],
                                   op0=ALU.mult, op1=ALU.max).then_inc(sig_arg, 1)
            dve.wait_ge(sig_ln, 1)
            own.link(v.scalar_tensor_tensor(out=frow[:, :], in0=frow[:, :], scalar=0.0, in1=lrow[:, :],
                                            op0=ALU.min, op1=ALU.subtract))
            dve.wait_ge(consts, 6)
            for j in range(TT):
                at = slice(j * L, (j + 1) * L)
                i = v.tensor_tensor_scan(brow[:, at], frow[:, at], zer[:, :], 0.0, ALU.add, ALU.add)
            own.link(i)
            own.link(v.tensor_tensor(urow[:, :], urow[:, :], brow[:, :], ALU.subtract))
            for j in range(TT):
                at = slice(j * L, (j + 1) * L)
                own.link(v.tensor_tensor_scan(mrow[:, at], urow[:, at], urow[:, at], mpv[:, j:j + 1],
                                              ALU.max, ALU.max))
                end = slice((j + 1) * L - 1, (j + 1) * L)
                own.link(v.tensor_tensor(mpv[:, j + 1:j + 2], brow[:, end], mrow[:, end], ALU.add))
            for k, vals in ((0, mrow[:, L - 1::L]), (1, mpv[:, 0:TT])):
                v.tensor_tensor(dg8[:, k, :, :], ident[0:8, 0:8].unsqueeze(2).to_broadcast([8, 8, TT]),
                                vals.unsqueeze(1).to_broadcast([8, 8, TT]), ALU.mult)
            v.tensor_scalar(nM[:, :], mrow[:, NCTX:], -1.0, None, ALU.mult)
            own.link(v.tensor_tensor(brow[:, :], brow[:, :], mrow[:, :], ALU.add))
            own.link(v.tensor_copy(nMr[:, :], nM[:, NLAT - 1::-1]))
            v.tensor_copy(revr[0:8, 0:NCTX], urow[:, NCTX - 1::-1])
            v.tensor_copy(revr[0:8, NCTX:], urow[:, TT * P - 1:NCTX - 1:-1])
            v.tensor_copy(mrow[:, 0:NCTX], brow[:, NCTX - 1::-1])
            v.tensor_copy(mrow[:, NCTX:], brow[:, TT * P - 1:NCTX - 1:-1]).then_inc(row_ready, 1)
            dve.wait_ge(gcol_done, 1)
            for k, g in ((0, 0), (1, 2)):
                v.tensor_copy(G5[:, g, :, :], PM[:, 80 * k:80 * k + 80].rearrange("p (t r) -> p r t", r=8))
            for k, g in ((0, 4), (1, 3)):
                on_all = PM[:, 160 + 80 * k:240 + 80 * k].rearrange("p (r j) -> p r j", j=TT)
                v.tensor_copy(G5[:, g, 0:4, :], on_all[:, 0:4, :])
                v.tensor_copy(G5[:, g, 4:8, 0:CT], on_all[:, 4:8, CT - 1::-1])
                i = v.tensor_copy(G5[:, g, 4:8, CT:], on_all[:, 4:8, TT - 1:CT - 1:-1])
                i.then_inc(pm_free, 1)
            dve.wait_ge(pm_free, 2)
            own.link(v.tensor_tensor(G5[:, 1, :, :], G5[:, 0, :, :], G5[:, 4, :, :], ALU.subtract))
            v.tensor_tensor(G5[:, 4, :, :], G5[:, 3, :, :], G5[:, 4, :, :], ALU.subtract).then_inc(exp_arg, 1)
            dve.wait_ge(g5_ready, 3)
            dve.wait_ge(consts, 13)

            with dve.Fori(0, HEADS) as h:
                own.enter(h, LINKS_H)
                v.tensor_copy(hc[:, :, :, :],
                              G5[:, :, :, :].rearrange("p g (d h) t -> p g d (h t)", d=2)[:, :, :, ds(h * TT, TT)])
                taps = cols[:, 80:128].rearrange("p (m t) -> p m t", t=8)
                v.tensor_copy(cwh[:, 0, :].unsqueeze(2), taps[:, :, ds(h, 1)])
                v.tensor_copy(cwh[:, 1, :].unsqueeze(2), taps[:, :, ds(h + HEADS, 1)])
                v.tensor_scalar(hgh[:, :], cols2[:, ds(h * 2, 2)], 0.5, None, ALU.mult)
                for d in range(2):
                    i = v.tensor_copy(selm[:, d, :], ident[0:8, ds(h + HEADS * d, 1)].to_broadcast([8, P]))
                i.then_inc(head_cols, 1)
                dve.wait_ge(head_cols, h + 1)

                def conv(dst, src, which, width):
                    own.link(v.tensor_scalar(dst, src[:, 0:width], cwh[:, which, 1:2], cwh[:, which, 0:1],
                                             ALU.mult, ALU.add))
                    for m in range(1, TAPS):
                        i = v.scalar_tensor_tensor(out=dst, in0=src[:, m:m + width],
                                                   scalar=cwh[:, which, m + 1:m + 2], in1=dst,
                                                   op0=ALU.mult, op1=ALU.add)
                        if m < TAPS - 1:
                            own.link(i)
                    i.then_inc(conv_done, 1)

                dve.wait_ge(slot_free[0], h * 5 + 2)
                conv(qT[:, :], work[:, 0, :], 0, NLAT)
                dve.wait_ge(slot_free[1], h * 5 + 2)
                conv(kT[:, NCTX:], work[:, 1, :], 1, NLAT)
                dve.wait_ge(slot_free[0], h * 5 + 3)
                conv(kT[:, 0:NCTX], kcraw[:, :], 1, NCTX)
                dve.wait_ge(th_done, h * 3 + 1)
                own.link(v.scalar_tensor_tensor(out=qT[:, :], in0=WB[:, 0, :], scalar=1.0, in1=qT[:, :],
                                                op0=ALU.add, op1=ALU.mult))
                v.tensor_scalar(qT[:, :], qT[:, :], QSCALE, None, ALU.mult).then_inc(qk_ready, 1)
                dve.wait_ge(th_done, h * 3 + 3)
                v.scalar_tensor_tensor(out=kT[:, NCTX:], in0=WB[:, 1, :], scalar=1.0, in1=kT[:, NCTX:],
                                       op0=ALU.add, op1=ALU.mult)
                v.scalar_tensor_tensor(out=kT[:, 0:NCTX], in0=junkH[:, :], scalar=1.0, in1=kT[:, 0:NCTX],
                                       op0=ALU.add, op1=ALU.mult).then_inc(qk_ready, 1)
                split_lo(h * 3 + 2, A)
                dve.wait_ge(nb_done, h + 1)
                for d in range(2):
                    v.tensor_tensor(work[:, d, PAD:PAD + NLAT].rearrange("p (c t) -> p c t", t=L),
                                    PM[:, d * NLAT:(d + 1) * NLAT].rearrange("p (c t) -> p c t", t=L),
                                    mask[:, d, :].unsqueeze(1).to_broadcast([P, LT, L]), ALU.add)\
                        .then_inc(nm_ready, 1)
                dve.wait_ge(ktr_done, h + 1)
                v.tensor_copy(ktok[:, 0:CT, :].rearrange("p t d -> p (t d)"), PM[:, 0:NCTX])\
                    .then_inc(ktok_ready, 1)
                v.tensor_copy(ktok[:, CT:, :].rearrange("p t d -> p (t d)"), PM[:, NLAT:2 * NLAT])\
                    .then_inc(ktok_ready, 1)
                dve.wait_ge(s_done, h + 1)
                dve.wait_ge(d_ready, h + 1)
                for d in range(2):
                    v.tensor_tensor(work[:, d, PAD:PAD + NLAT], PM[:, 0:NLAT], work[:, d, PAD:PAD + NLAT],
                                    ALU.mult).then_inc(sw_ready, 1)
                for j in range(TT):
                    for d in range(2):
                        if j == TT - 1:
                            continue
                        bank = PM[:, (2 + d) * HALF:(2 + d) * HALF + DVA - 1]
                        dve.wait_ge(dc_done, h * 18 + (2 * j + d + 1))
                        if j == 0:
                            v.tensor_copy(Cst[:, d, 1, 0:DVA - 1], bank).then_inc(c_ready, 1)
                        else:
                            dve.wait_ge(c_ready, h * 18 + (2 * j + d - 1))
                            t = tile_of(d, j)
                            v.scalar_tensor_tensor(out=Cst[:, d, (j + 1) % 2, 0:DVA - 1],
                                                   in0=Cst[:, d, j % 2, 0:DVA - 1], scalar=hc[:, 4, d, t:t + 1],
                                                   in1=bank, op0=ALU.mult, op1=ALU.add).then_inc(c_ready, 1)
                    if j in (2, 3):
                        split_lo(h * 3 + (N_H + 3), A, (j - 2,))
                    if j in (6, 7):
                        split_lo(h * 3 + (N_H + 4), B, (j - 6,))
                    if j < CT:
                        continue
                    for d in range(2):
                        t = tile_of(d, j)
                        bank = PM[:, d * HALF:d * HALF + DV]
                        bden = PM[:, d * HALF + DV:d * HALF + DV + 1]
                        dve.wait_ge(num_done, h * 16 + (2 * (j - CT) + d + 1))
                        own.link(v.tensor_scalar(den[:, d, 0:1], bden, -1.0, hc[:, 2, d, t:t + 1],
                                                 ALU.mult, ALU.max))
                        own.link(v.tensor_tensor(den[:, d, 1:2], bden, den[:, d, 0:1], ALU.max))
                        own.link(v.reciprocal(den[:, d, 2:3], den[:, d, 1:2]))
                        first = (j - CT < LT // 2)
                        if first:
                            v.tensor_scalar(Hh[:, t - CT, :], bank, den[:, d, 2:3], None, ALU.mult)\
                                .then_inc(h_written, 1)
                        else:
                            v.scalar_tensor_tensor(out=Hh[:, t - CT, :], in0=bank, scalar=den[:, d, 2:3],
                                                   in1=Hh[:, t - CT, :], op0=ALU.mult, op1=ALU.add)\
                                .then_inc(h_written, 1)
                dve.wait_ge(act_own, h * LT + (TT + 1 + LT))
                rsqrt(LT, DV)
                for t in range(LT):
                    i = v.tensor_scalar(Hh[:, t, :], Hh[:, t, :], rs[:, 2, t:t + 1], None, ALU.mult)
                i.then_inc(hn_ready, 1)
                dve.wait_ge(yt_done, h + 1)
                for m in range(2):
                    dve.wait_ge(sgo_ready, h * 2 + (m + 1))
                    v.tensor_tensor(sgo[:, m, :], PM[:, m * NLAT:(m + 1) * NLAT], sgo[:, m, :], ALU.mult)\
                        .then_inc(pm_free, 1)
                own.leave(HEADS)

            with dve.Fori(0, 2) as i:
                for cc in range(2):
                    q = i * 2 + cc
                    acc = Tacc[:, ds(q, 1), :]
                    for k in range(KT):
                        dve.wait_ge(ada2_in[k % 2], q * 64 + (k // 2 * 16 + 16))
                        src = ada2[k % 2][:, :].unsqueeze(1)
                        if k == 0:
                            v.tensor_scalar(acc, src, csil[:, 0, 0:1], None, ALU.mult).then_inc(ada2_used, 1)
                        else:
                            dve.wait_ge(ada2_used, q * KT + (k + 2))
                            v.scalar_tensor_tensor(out=acc, in0=src, scalar=csil[:, 0, k:k + 1], in1=acc,
                                                   op0=ALU.mult, op1=ALU.add).then_inc(ada2_used, 1)
                    split_lo(i * 2 + (N_V + 2 + cc), cc)
            dve.wait_ge(T_mm, 1)
            v.tensor_tensor(mod[:, 2:6, :].rearrange("p q k -> p (q k)"), PM[:, 0:4 * KT], cols[:, 48:80], ALU.add)\
                .then_inc(mod_ready, 1)
            dve.wait_ge(mod_ready, 1)
            own.link(v.scalar_tensor_tensor(out=a2[:, :], in0=mod[:, 4, :], scalar=1.0, in1=cols[:, 24:32],
                                            op0=ALU.add, op1=ALU.mult))
            dve.wait_ge(act_own, TT + 1 + HEADS * LT + LT)
            rsqrt(LT, D)
            for t in range(LT):
                v.tensor_scalar(V[:, t, :], V[:, t, :], rs[:, 2, t:t + 1], None, ALU.mult).then_inc(v_scaled, 1)
            dve.wait_ge(wsp_hi_d, 1)
            v.tensor_tensor(wsp_lo[:, :, :], PM[:, HALF:2 * HALF].rearrange("p (g t) -> p g t", g=4),
                            wsp_hi[:, :, :].bitcast(F32), ALU.subtract).then_inc(wsp_ready, 1)

            dve.wait_ge(small_in, 32)
            with dve.Fori(0, 2) as i:
                own.enter(i, LINKS_U)
                for hh in range(2):
                    for jj in (2 * hh, 2 * hh + 1):
                        b = jj % 2
                        dve.wait_ge(v_scaled, LT)
                        dve.wait_ge(vn_hi_d, i * 4 + (jj + 1))
                        v.tensor_tensor(vn_lo[b][:, :, :], V[:, :, ds(i * (4 * P) + jj * P, P)],
                                        vn_hi[b][:, :, :].bitcast(F32), ALU.subtract).then_inc(vn_ready, 1)
                    for jj in (2 * hh, 2 * hh + 1):
                        b = jj % 2
                        dve.wait_ge(sv_done, i * 4 + (jj + 3))
                        half = PM[:, b * NLAT:(b + 1) * NLAT]
                        own.link(v.scalar_tensor_tensor(
                            out=half.rearrange("p (c t) -> p c t", t=P), in0=half.rearrange("p (c t) -> p c t", t=P),
                            scalar=cols2[:, ds(i * 4 + (8 + jj), 1)],
                            in1=bspB[:, ds(i * 2 + jj // 2, 1), :].to_broadcast([P, LT, P]),
                            op0=ALU.mult, op1=ALU.add))
                        dve.wait_ge(slot_free[b], i * 2 + (T_U // 2 + 2 + jj // 2))
                        v.tensor_tensor(uT[b][:, :], half, uT[b][:, :], ALU.mult).then_inc(y_f32, 1)
                        dve.wait_ge(y_hi_d, i * 4 + (jj + 1))
                        v.tensor_tensor(Y_lo[:, :, ds(i * 4 + jj, 1), :],
                                        uT[b][:, :].rearrange("p (c o t) -> p c o t", o=1, t=P),
                                        Y_hi[:, :, ds(i * 4 + jj, 1), :].bitcast(F32), ALU.subtract)\
                            .then_inc(yb_ready, 1)
                    split_lo(i * 2 + (N_U + 2 + hh), hh)
                own.leave(2)

            with dve.Fori(0, 4) as i:
                split_lo(i * 2 + (N_PB + 2), A)
                for m in range(2):
                    at = Mb[:, ds(i * 2 + m, 1), :]
                    dve.wait_ge(slot_free[m], i * 2 + (T_PB // 2 + 2))
                    dve.wait_ge(tile_done, i * 4 + (T_PB + m + 3))
                    v.scalar_tensor_tensor(out=at, in0=at, scalar=1.0,
                                           in1=PD[m][:, :].rearrange("p (o t) -> p o t", o=1),
                                           op0=ALU.add, op1=ALU.mult).then_inc(slot_free[m], 1)

                split_lo(i * 2 + (N_PB + 3), B)

            for k in range(KT):
                dve.wait_ge(ya_hi_d, k + 1)
                v.tensor_tensor(Y_lo[:, :, k, :], ya_raw[:, :, k, :], Y_hi[:, :, k, :].bitcast(F32),
                                ALU.subtract).then_inc(ya_ready, 1)

            def m_lo(k):
                dve.wait_ge(m_hi_d, k + 1)
                v.scalar_tensor_tensor(out=R_lo[:, k, :], in0=Mb[:, k, :], scalar=0.5,
                                       in1=R_hi[:, k, :].bitcast(F32), op0=ALU.mult, op1=ALU.subtract)\
                    .then_inc(m_ready, 1)

            def merge_a(i, last):
                for m in range(2):
                    at = Mb[:, ds(i * 2 + m, 1), :]
                    tile = PD[m][:, :]
                    dve.wait_ge(ga_th, i * 2 + (m + 3))
                    dve.wait_ge(tile_done, i * 2 + (T_PA + m + 1))
                    v.scalar_tensor_tensor(out=tile, in0=sg[:, :], scalar=1.0, in1=tile,
                                           op0=ALU.add, op1=ALU.mult).then_inc(ga_used, 1)
                    dve.wait_ge(ga_used, i * 2 + (m + 2))
                    v.tensor_tensor(at, at, tile.unsqueeze(1), ALU.add).then_inc(slot_free[m], 1)
                    if m == 0:
                        split_lo(i * 2 + (N_PA + 2), A)
                        if last:
                            for k in range(KT - 2):
                                m_lo(k)
                if last:
                    for k in range(KT - 2, KT):
                        m_lo(k)
                split_lo(i * 2 + (N_PA + 3), B)

            with dve.Fori(0, 3) as i:
                merge_a(i, False)
            merge_a(3, True)

            dve.wait_ge(gB_mm, 1)
            own.link(v.tensor_copy(sg[:, :], PM[:, 0:D]))
            dve.wait_ge(x2_in, 16 * LT)
            with dve.Fori(0, 2) as i:
                own.enter(i, LINKS_O)
                for cc in range(2):
                    for p in range(4):
                        at = i * (2 * CW) + cc * CW
                        src = PD[p % 2][:, :].rearrange("p (t n) -> p t n", t=2)[:, :, 0:CW]
                        dst = xs[:, 2 * p:2 * p + 2, ds(at, CW)]
                        dve.wait_ge(tile_done, i * 8 + (T_O + 4 * cc + p + 1))
                        own.link(v.tensor_tensor(src, src, sg[:, ds(at, CW)].unsqueeze(1)
                                                 .to_broadcast([P, 2, CW]), ALU.mult))
                        v.tensor_tensor(dst, src, dst, ALU.add).then_inc(slot_free[p % 2], 1)
                    split_lo(i * 2 + (N_O + 2 + cc), cc)
                own.leave(2)
            dve.wait_ge(gB_mm, 2)
            own.link(v.tensor_copy(g2B[:, :], PM[:, 0:D]))
            dve.wait_ge(act_own, TT + 1 + HEADS * LT + 2 * LT)
            rsqrt(LT, D)
            for t in range(LT):
                v.tensor_scalar(xn[:, t, :], xs[:, t, :], rs[:, 2, t:t + 1], None, ALU.mult).then_inc(xn2_ready, 1)
            for k in range(KT + 1):
                if k < KT:
                    dve.wait_ge(tile_done, T_X + k + 1)
                    if k >= 2:
                        dve.wait_ge(h2_lo, k - 1)
                    v.tensor_scalar(hT[k % 2][:, :], PD[k % 2][:, :], a2[:, k:k + 1], mod[:, 3, k:k + 1],
                                    ALU.mult, ALU.add).then_inc(slot_free[k % 2], 1)
                if k >= 1:
                    dve.wait_ge(h2_hi, k)
                    v.tensor_tensor(R_lo[:, k - 1, :], hT[(k - 1) % 2][:, :], R_hi[:, k - 1, :].bitcast(F32),
                                    ALU.subtract).then_inc(h2_lo, 1)

            def gate_out(tile, free, m):
                dve.wait_ge(slot_free[m], free)
                dve.wait_ge(tile_done, tile)
                v.tensor_tensor(sa[:, m, :], PD[m][:, :], sa[:, m, :], ALU.mult).then_inc(slot_free[m], 1)

            def f_lo_out(count, m):
                dve.wait_ge(f_hi_d, count)
                v.tensor_tensor(f_lo[:, m, :], sa[:, m, :], f_hi[:, m, :].bitcast(F32), ALU.subtract)\
                    .then_inc(f_lo_d, 1)

            for m in range(2):
                gate_out(T_F + 3 + m, T_F // 2 + 2, m)
            split_lo(N_F + 2, A)
            for m in range(2):
                f_lo_out(m + 1, m)

            def accumulate(tile, t):
                dve.wait_ge(tile_done, tile)
                own.link(v.tensor_tensor(PD[t % 2][:, :], PD[t % 2][:, :], g2B[:, :], ALU.mult))
                v.tensor_tensor(xs[:, t, :], PD[t % 2][:, :], xs[:, t, :], ALU.add).then_inc(slot_free[t % 2], 1)

            def ffn(r, last):
                T = r * FT + (T_F + 4)
                n = r * 3 + (N_F + 3)
                split_lo(n, C)
                split_lo(n + 1, B)
                for t in range(LT):
                    accumulate(T + (3 + t), t)
                if not last:
                    split_lo(n + 2, A)
                for m in range(2):
                    gate_out(T + (11 + m), r * 6 + (T_F // 2 + 4), m)
                for m in range(2):
                    f_lo_out(r * 2 + (m + 3), m)

            with dve.Fori(0, NFB - 2) as r:
                own.enter(r, LT)
                ffn(r, False)
                own.leave(NFB - 2)
            ffn(NFB - 2, True)
            split_lo(N_F + 3 * NFB - 1, C)
            dve.wait_ge(fg_in, 16)
            for t in range(LT):
                accumulate(T_F + 4 + FT * (NFB - 1) + t + 1, t)
                if t in (5, LT - 1):
                    first, end = (0, 4) if t == 5 else (4, LT)
                    dve.wait_ge(act_own, TT + 1 + HEADS * LT + 2 * LT + end)
                    rsqrt(end, D, first)
                    for u in range(first, end):
                        v.scalar_tensor_tensor(out=xs[:, u, :], in0=xs[:, u, :], scalar=rs[:, 2, u:u + 1],
                                               in1=fg[:, :], op0=ALU.mult, op1=ALU.mult).then_inc(o_ready, 1)

        @block.tensor
        def _(pe):
            mm = nc.tensor.matmul

            def ready(n, half):
                pe.wait_ge(w_ready[half], n + 2)

            def halves(src, k):
                if src is Y_hi or src is Y_lo:
                    return [src[:, 4 * e:4 * e + 4, k, :] for e in range(2)]
                if src is ctx_hi or src is ctx_lo:
                    return [src[:, k, :]]
                return [src[:, k, e * HALF:(e + 1) * HALF] for e in range(2)]

            def channels(s, n, buf, m, hi, lo, tile_wait=None, dst=None, done=tile_done):
                w = [q[buf][:, :].rearrange("p (k n) -> p k n", k=KT)[:, :, m * P:(m + 1) * P]
                     for q in (whi, wlo)]
                width = NCTX if hi is ctx_hi else HALF
                dst = PD[s] if dst is None else dst
                for k in range(KT):
                    if k % 4 == 0:
                        ready(n, k // 4)
                    if tile_wait is not None:
                        tile_wait(k)
                    for step, (wk, src) in enumerate(((w[0], hi), (w[0], lo), (w[1], hi))):
                        for e, part in enumerate(halves(src, k)):
                            i = mm(dst[:, e * HALF:e * HALF + width], wk[:, k, :], part,
                                   start=(k == 0 and step == 0), stop=(k == KT - 1 and step == 2))
                i.then_inc(done, 1)

            def tokens(s, n, buf, hi, lo, tiles, wait=None):
                w = [q[buf][:, :].rearrange("p (k n) -> p k n", k=KT) for q in (whi, wlo)]
                for e, t in enumerate(tiles):
                    at = slice(t * P, (t + 1) * P)
                    for k in range(KT):
                        if k % 4 == 0:
                            ready(n, k // 4)
                        if wait is not None:
                            wait(k)
                        for step, (src, wk) in enumerate(((hi, w[0]), (hi, w[1]), (lo, w[0]))):
                            i = mm(PD[s][:, e * HALF:e * HALF + CW], src[:, k, at], wk[:, k, :],
                                   start=(k == 0 and step == 0), stop=(k == KT - 1 and step == 2))
                i.then_inc(tile_done, 1)

            pe.wait_ge(consts, 2)
            pe.wait_ge(vec_in, 16 * 9)
            nc.tensor.transpose(PM[:, 0:P], rows1[:, :], ident[:, :])
            nc.tensor.transpose(PM[:, P:P + 16], rows2[:, :], ident[0:16, 0:16]).then_inc(vecT, 1)
            for t in range(TT):
                pe.wait_ge(xn_ready, t + 1)
                if t >= 2:
                    pe.wait_ge(xT_read[t % 2], t // 2)
                for k in range(KT):
                    i = nc.tensor.transpose(PD[t % 2][:, k * P:(k + 1) * P], xtok[:, t, k * P:(k + 1) * P],
                                            ident[:, :])
                i.then_inc(xT_done, 1)
            pe.wait_ge(csil_ready, 1)
            for k in range(KT):
                pe.wait_ge(ada_in[k % 4], k // 4 * 16 + 16)
                for e in range(4):
                    i = mm(PM[0:2, e * HALF:(e + 1) * HALF], csil[:, :, k], ada_raw[k % 4][:, e * HALF:(e + 1) * HALF],
                           start=(k == 0), stop=(k == KT - 1))
                i.then_inc(ada_mm, 1)
            pe.wait_ge(adarow_ready, 1)
            for j in range(2 * KT):
                i = mm(PM[:, 2 * j:2 * j + 2], xtok[0:2, j // KT, (j % KT) * P:(j % KT + 1) * P], ident[0:2, 0:2],
                       start=True, stop=True)
            i.then_inc(adacol_done, 1)

            pe.wait_ge(wg_ready, 1)
            for k in range(KT):
                pe.wait_ge(h_lo, 2 * k + 2)
                for d in range(2):
                    for step, (wk, src, csrc) in enumerate(((wg_hi, R_hi, ctx_hi), (wg_hi, R_lo, ctx_lo),
                                                            (wg_lo, R_hi, ctx_hi))):
                        if d == 0:
                            parts = (src[:, k, 0:HALF], src[:, k, HALF:], csrc[:, k, :])
                        else:
                            parts = (src[:, k, NLAT - 1:HALF - 1:-1], src[:, k, HALF - 1::-1], csrc[:, k, ::-1])
                        for at, part in zip((0, HALF, NLAT), parts):
                            i = mm(PM[0:GM, at:at + (HALF if at < NLAT else NCTX)], wk[:, k, d, :], part,
                                   start=(k == 0 and step == 0 and d == 0),
                                   stop=(k == KT - 1 and step == 2 and d == 1))
            i.then_inc(gates_mm, 1)
            for m in range(2):
                pe.wait_ge(slot_free[m], 1)
                channels(m, N_H, A, m, R_hi, R_lo)
            pe.wait_ge(row_ready, 1)
            for kind, (fwd, bwd) in enumerate(((urow, revr), (brow, mrow))):
                for t in range(TT):
                    for d, rows in ((0, fwd), (1, bwd)):
                        at = 80 * kind + 8 * t + 4 * d
                        mm(PM[:, at:at + 4], rows[0:8, t * P:(t + 1) * P], ident[0:8, 4 * d:4 * d + 4],
                           start=True, stop=True)
            mm(PM[:, 160:320], ones8[:, :], dg8[:, :, :, :].rearrange("p k r j -> p (k r j)"),
               start=True, stop=True).then_inc(gcol_done, 1)

            def head(h, last):
                def free(c):
                    pe.wait_ge(slot_free[c % 2], h * 5 + (c // 2 + 1))

                n = h * 3 + N_H
                free(2)
                channels(0, n, A, 1, ctx_hi, ctx_lo)
                pe.wait_ge(head_cols, h + 1)
                pe.wait_ge(pm_free, h * 2 + 2)
                for d, rows in ((0, nM), (1, nMr)):
                    for e in range(2):
                        at = d * NLAT + e * HALF
                        i = mm(PM[:, at:at + HALF], selm[:, d, :], rows[:, e * HALF:(e + 1) * HALF],
                               start=True, stop=True)
                i.then_inc(nb_done, 1)
                free(3)
                tokens(1, n + 1, B, ctx_hi, ctx_lo, (0, 1))
                for p in range(4):
                    free(4 + p)
                    tokens(p % 2, n + 1, B, R_hi, R_lo, (2 * p, 2 * p + 1))
                pe.wait_ge(qk_ready, h * 2 + 2)
                pe.wait_ge(nm_ready, h * 2 + 2)
                pe.wait_ge(wb_ready, h + 1)
                for t in range(TT):
                    at = t * P if t < CT else NLAT + (t - CT) * P
                    i = nc.tensor.transpose(PM[:, at:at + P], kT[:, t * P:(t + 1) * P], ident[:, :])
                i.then_inc(ktr_done, 1)
                free(8)
                channels(0, n + 2, A, 0, R_hi, R_lo)
                pe.wait_ge(ktok_ready, h * 2 + 1)
                for t in range(LT):
                    i = mm(PM[:, t * L:(t + 1) * L], kT[:, NCTX + t * L:NCTX + (t + 1) * L],
                           qT[:, t * L:(t + 1) * L], start=True, stop=True)
                i.then_inc(s_done, 1)
                free(9)
                channels(1, n + 2, A, 1, R_hi, R_lo)
                pe.wait_ge(ktok_ready, h * 2 + 2)
                pe.wait_ge(kw_ready, h * 2 + 2)
                for s in range(2):
                    pe.wait_ge(slot_free[s], h * 5 + 5)
                for j in range(TT):
                    for d in range(2):
                        if j == TT - 1:
                            continue
                        t = tile_of(d, j)
                        if j >= 1:
                            pe.wait_ge(c_ready, h * 18 + (2 * j + d - 1))
                        mm(PM[:, (2 + d) * HALF:(2 + d) * HALF + DVA - 1], kw[:, d, t, :], vaug[:, t, 0:DVA - 1],
                           start=True, stop=True).then_inc(dc_done, 1)
                    if j < CT:
                        continue
                    if j == CT:
                        pe.wait_ge(sw_ready, h * 2 + 2)
                        pe.wait_ge(qw_ready, h * 2 + 2)
                    for d in range(2):
                        t = tile_of(d, j)
                        lat = (t - CT) * L
                        bank = PM[:, d * HALF:d * HALF + DVA - 1]
                        pe.wait_ge(c_ready, h * 18 + (2 * j + d - 1))
                        if j > CT:
                            pe.wait_ge(h_written, h * 16 + (2 * (j - CT) + d - 1))
                        mm(bank, work[:, d, PAD + lat:PAD + lat + L], vaug[:, t, 0:DVA - 1], start=True, stop=False)
                        mm(bank, WB[:, d, lat:lat + L], Cst[:, d, j % 2, 0:DVA - 1], start=False, stop=True)\
                            .then_inc(num_done, 1)
                if not last:
                    for m in range(2):
                        free(10 + m)
                        channels(m, n + 3, A, m, R_hi, R_lo)
                pe.wait_ge(hn_ready, h + 1)
                for m in range(2):
                    for t in range(LT):
                        at = m * NLAT + t * P
                        i = nc.tensor.transpose(PM[:, at:at + P], Hh[:, t, m * P:(m + 1) * P], ident[:, :])
                i.then_inc(yt_done, 1)

            with pe.Fori(0, HEADS - 1) as h:
                head(h, False)
            head(HEADS - 1, True)

            def free(T):
                pe.wait_ge(slot_free[T % 2], T // 2 + 1)

            pe.wait_ge(pm_free, 2 * HEADS + 2)
            with pe.Fori(0, 2) as i:
                for cc in range(2):
                    for p in range(4):
                        pe.wait_ge(slot_free[p % 2], i * 4 + (T_V // 2 + 2 * cc + p // 2 + 1))
                        tokens(p % 2, i * 2 + (N_V + cc), cc, R_hi, R_lo, (2 * p, 2 * p + 1))
            pe.wait_ge(ada2_used, 4 * KT + 2)
            for q in range(4):
                for k in range(KT):
                    last = mm(PM[:, q * KT + k:q * KT + k + 1], Tacc[:, q, k * P:(k + 1) * P], one1[:, :],
                              start=True, stop=True)
            last.then_inc(T_mm, 1)
            pe.wait_ge(small_in, 32)
            for g in range(4):
                i = nc.tensor.transpose(PM[:, HALF + g * P:HALF + (g + 1) * P], wsp[:, g, :], ident[:, :])
            i.then_inc(wspT_done, 1)

            with pe.Fori(0, 2) as i:
                for hh in range(2):
                    for jj in (2 * hh, 2 * hh + 1):
                        pe.wait_ge(slot_free[jj % 2], i * 2 + (T_U // 2 + jj // 2 + 1))
                        channels(jj % 2, i * 2 + (N_U + hh), hh, jj % 2, R_hi, R_lo)
                    for jj in (2 * hh, 2 * hh + 1):
                        b = jj % 2
                        pe.wait_ge(vn_ready, i * 4 + (jj + 1))
                        pe.wait_ge(wsp_ready, 1)
                        pe.wait_ge(yb_ready, i * 4 + (jj + 1))
                        g = ds(i * 2 + hh, 1)
                        for c8 in range(LT):
                            dst = PM[:, b * NLAT + c8 * P:b * NLAT + (c8 + 1) * P].unsqueeze(1)
                            for step, (src, wk) in enumerate(((vn_hi[b], wsp_hi), (vn_hi[b], wsp_lo),
                                                              (vn_lo[b], wsp_hi))):
                                last = mm(dst, src[:, c8, :], wk[:, g, :], start=(step == 0), stop=(step == 2))
                        last.then_inc(sv_done, 1)

            with pe.Fori(0, 4) as i:
                for m in range(4):
                    pe.wait_ge(slot_free[m % 2], i * 2 + (T_PB // 2 + m // 2 + 1))
                    if m < 2:
                        channels(m, i * 2 + N_PB, A, m, R_hi, R_lo)
                    else:
                        if m == 2:
                            pe.wait_ge(yb_ready, KT + 2)
                        channels(m - 2, i * 2 + (N_PB + 1), B, m - 2, Y_hi, Y_lo)

            def broadcast_gate(which, at):
                for k in range(KT):
                    last = mm(PM[:, at + k * P:at + (k + 1) * P], mod[:, which, k:k + 1].to_broadcast([P, P]),
                              ident[:, :], start=True, stop=True)
                last.then_inc(gB_mm, 1)

            with pe.Fori(0, 4) as i:
                for m in range(2):
                    pe.wait_ge(ga_th, i * 2 + (m + 1))
                    channels(m, i * 2 + N_PA, A, m, R_hi, R_lo, dst=PM[:, m * NLAT:(m + 1) * NLAT], done=ga_done)
                for m in range(2):
                    pe.wait_ge(slot_free[m], i + (T_PA // 2 + 1))
                    channels(m, i * 2 + (N_PA + 1), B, m, Y_hi, Y_lo,
                             (lambda k: pe.wait_ge(ya_ready, k + 1)) if m == 0 else None)

            pe.wait_ge(mod_ready, 1)
            pe.wait_ge(ga_th, KT + 2)
            broadcast_gate(2, 0)
            with pe.Fori(0, 2) as i:
                for cc in range(2):
                    for p in range(4):
                        pe.wait_ge(slot_free[p % 2], i * 4 + (T_O // 2 + 2 * cc + p // 2 + 1))
                        tokens(p % 2, i * 2 + (N_O + cc), cc, R_hi, R_lo, (2 * p, 2 * p + 1),
                               (lambda k: pe.wait_ge(m_ready, k + 1)) if cc + p == 0 else None)
            broadcast_gate(5, 0)
            for t in range(LT):
                pe.wait_ge(xn2_ready, t + 1)
            for k in range(KT):
                free(T_X + k)
                for t in range(LT):
                    last = nc.tensor.transpose(PD[k % 2][:, t * P:(t + 1) * P], xn[:, t, k * P:(k + 1) * P],
                                               ident[:, :])
                last.then_inc(tile_done, 1)

            def down(T, n):
                w = [q[C][:, :].rearrange("p (k n) -> p k n", k=2) for q in (whi, wlo)]
                for t in range(LT):
                    pe.wait_ge(slot_free[t % 2], T[t])
                    at = slice(t * P, (t + 1) * P)
                    for k in range(2):
                        if t == 0:
                            ready(n, k)
                        for step, (src, wk) in enumerate(((f_hi, w[0]), (f_hi, w[1]), (f_lo, w[0]))):
                            for e in range(2):
                                last = mm(PD[t % 2][:, e * HALF:(e + 1) * HALF], src[:, k, at],
                                          wk[:, k, e * HALF:(e + 1) * HALF],
                                          start=(k == 0 and step == 0), stop=(k == 1 and step == 2))
                    last.then_inc(tile_done, 1)

            for m in range(2):
                free(T_F + m)
                channels(m, N_F, A, m, R_hi, R_lo, (lambda k: pe.wait_ge(h2_lo, k + 1)) if m == 0 else None)
            for m in range(2):
                free(T_F + 2 + m)
                channels(m, N_F + 1, B, m, R_hi, R_lo)
            with pe.Fori(0, NFB - 1) as r:
                base = (T_F + 4) // 2 + 1
                n = r * 3 + (N_F + 3)
                for m in range(2):
                    pe.wait_ge(slot_free[m], r * 6 + base)
                    channels(m, n - 1, A, m, R_hi, R_lo)
                pe.wait_ge(f_lo_d, r * 2 + 2)
                down([r * 6 + (base + 1 + t // 2) for t in range(LT)], n)
                for m in range(2):
                    pe.wait_ge(slot_free[m], r * 6 + (base + 5))
                    channels(m, n + 1, B, m, R_hi, R_lo)
            pe.wait_ge(f_lo_d, 2 * NFB)
            T_end = T_F + 4 + FT * (NFB - 1)
            down([(T_end + t) // 2 + 1 for t in range(LT)], N_F + 3 * NFB - 1)


_NAMES = ['x', 'c', 'ctx', 'c_ctx', 'w_ada', 'b_ada', 'norm1_g', 'norm2_g', 'w_in', 'conv_w', 'conv_b', 'gate_b',
          'head_g', 'vnorm_g', 'w_spatial', 'b_spatial', 'w_pa', 'w_pb', 'w_out', 'w_ff1', 'w_ff3', 'w_ff2',
          'final_g']


def kernel(**inputs):
    import concourse.bacc as bacc
    import numpy as np
    from concourse.bass_utils import run_bass_kernel_spmd

    nc = bacc.Bacc("TRN2", target_bir_lowering=False, num_devices=1)
    arrays, aps = {}, []
    for name in _NAMES:
        a = np.ascontiguousarray(inputs[name])
        arrays[f"in_{name}"] = a
        aps.append(nc.dram_tensor(f"in_{name}", a.shape, mybir.dt.from_np(a.dtype), kind="ExternalInput").ap())
    out = nc.dram_tensor("out_x", (1, NLAT, D), F32, kind="ExternalOutput").ap()
    build(nc, *aps, out)
    r = run_bass_kernel_spmd(nc, [arrays], core_ids=[0])
    return r.results[0]["out_x"]
```

```python
from contextlib import ExitStack

import concourse.bass as bass
from concourse import mybir

F32 = mybir.dt.float32
F32R = mybir.dt.float32r
I32 = mybir.dt.int32
ALU = mybir.AluOpType
ACT = mybir.ActivationFunctionType
AX = mybir.AxisListType.X
ds = bass.ds

P = 128
D = 1024
KT = D // P
NLAT, NCTX = 1024, 256
LT, CT = NLAT // P, NCTX // P
TT = LT + CT
HALF = 512
HEADS, DQK, DV = 4, 128, 256
L = 128
DFF = 2816
CW = 256
NFB = DFF // CW
EPS = 1e-6
TAPS = 5
GM = 40
PAD = TAPS // 2
CQ, CK, CV, CO, CG, CU, CVB, CGA, CGB = 0, 512, 1024, 2048, 3072, 3088, 4112, 5136, 6160
NEG = -1.0e30
DVA = DV + 2
QSCALE = 0.25 * DQK ** -0.5

N_H, N_V, N_U, N_PB, N_PA, N_O, N_F = 0, 12, 16, 20, 28, 36, 40
T_H, T_V, T_U, T_PB, T_PA, T_O, T_X, T_F = 0, 40, 56, 64, 80, 88, 104, 112
HT = 10
FT = 12
A, B, C = 0, 1, 2
LINKS_H, LINKS_U = 73, 4
MAGIC = float(0x5F3759DF)


def tile_of(direction, j):
    if direction == 0:
        return j
    return CT - 1 - j if j < CT else TT + CT - 1 - j


class Chain:

    def __init__(self, eng, semaphore):
        self.eng, self.sem, self.base, self.i, self.per, self.n = eng, semaphore, 0, 0, 0, 0

    def link(self, instruction):
        self.n += 1
        instruction.then_inc(self.sem, 1)
        self.eng.wait_ge(self.sem, self.i * self.per + (self.base + self.n))

    def enter(self, i, per):
        self.base, self.n, self.i, self.per = self.base + self.n, 0, i, per

    def leave(self, passes):
        assert self.n == self.per, (self.n, self.per)
        self.base, self.n, self.i, self.per = self.base + passes * self.per, 0, 0, 0


def build(nc, x, c, ctx, c_ctx, w_ada, b_ada, norm1_g, norm2_g, w_in, conv_w, conv_b, gate_b, head_g,
          vnorm_g, w_spatial, b_spatial, w_pa, w_pb, w_out, w_ff1, w_ff3, w_ff2, final_g, out):
    def rows_first(w):
        return w.rearrange("o (k p) n -> (o p) k n", p=P)

    x_t, ctx_t, out_t = rows_first(x), rows_first(ctx), rows_first(out)
    ada_v, win_v = rows_first(w_ada), rows_first(w_in)
    pa_v, pb_v, wo_v = rows_first(w_pa), rows_first(w_pb), rows_first(w_out)
    f1_v, f3_v, f2_v = rows_first(w_ff1), rows_first(w_ff3), rows_first(w_ff2)
    ya_dram = nc.dram_tensor("ya_dram", [P, KT, NLAT], F32, kind="Internal").ap()

    es = ExitStack()
    with es:
        def sb(name, shape, dt=F32, stack=es):
            return stack.enter_context(nc.sbuf_tensor(name, shape, dt))

        def sem(name):
            return es.enter_context(nc.semaphore(name))

        ident = sb("ident", [P, P])
        one1 = sb("one1", [P, 1])
        gb8 = sb("gb8", [8, 2])
        gsel = sb("gsel", [P, 16])
        cols = sb("cols", [P, P])
        cols2 = sb("cols2", [P, 16])
        csil = sb("csil", [P, 2, KT])
        mod = sb("mod", [P, 6, KT])
        b1 = sb("b1", [P, 2, 2 * KT])
        a1 = sb("a1", [P, 2, KT])
        a2 = sb("a2", [P, KT])
        note = sb("note", [P, 17])
        rs = sb("rs", [P, 4, 16])
        R_hi = sb("R_hi", [P, KT, NLAT], F32R)
        with ExitStack() as tmp:
            rows1 = sb("rows1", [P, P], stack=tmp)
            rows2 = sb("rows2", [16, P], stack=tmp)
            wg = sb("wg", [P, KT, 16], stack=tmp)
            wgz = sb("wgz", [P, KT, 2, GM], stack=tmp)
        R_lo = sb("R_lo", [P, KT, NLAT], F32R)
        raw = [sb(f"raw{k}", [P, 4 * CW]) for k in range(2)]
        with ExitStack() as tmp:
            ada_raw = [sb(f"ada_raw{k}", [P, 2 * D], stack=tmp) for k in range(4)]
        whi = [sb(f"whi{k}", [P, 8 * CW], F32R) for k in range(2)]
        wlo = [sb(f"wlo{k}", [P, 8 * CW], F32R) for k in range(2)]

        with ExitStack() as sH:
            ctx_hi = sb("ctx_hi", [P, KT, NCTX], F32R, sH)
            ctx_lo = sb("ctx_lo", [P, KT, NCTX], F32R, sH)
            with ExitStack() as s0:
                xtok = sb("xtok", [P, TT, D], stack=s0)
                xnT = sb("xnT", [P, KT, TT * P], stack=s0)
                cth = sb("cth", [P, 2 * KT], stack=s0)
                wg_hi = sb("wg_hi", [P, KT, 2, GM], F32R, s0)
                wg_lo = sb("wg_lo", [P, KT, 2, GM], F32R, s0)
            with ExitStack() as s1:
                mask = sb("mask", [P, 2, L], stack=s1)
                G5 = sb("G5", [P, 5, 8, TT], stack=s1)
                nM = sb("nM", [8, NLAT], stack=s1)
                nMr = sb("nMr", [8, NLAT], stack=s1)
                hc = sb("hc", [P, 5, 2, TT], stack=s1)
                cwh = sb("cwh", [P, 2, 6], stack=s1)
                hgh = sb("hgh", [P, 2], stack=s1)
                selm = sb("selm", [8, 2, P], stack=s1)
                den = sb("den", [P, 2, 4], stack=s1)
                work = sb("work", [P, 2, NLAT + 2 * PAD], stack=s1)
                kcraw = sb("kcraw", [P, NCTX + 2 * PAD], stack=s1)
                qT = sb("qT", [P, NLAT], stack=s1)
                kT = sb("kT", [P, TT * P], stack=s1)
                WB = sb("WB", [P, 2, NLAT], stack=s1)
                ktok = sb("ktok", [P, TT, DQK], stack=s1)
                vaug = sb("vaug", [P, TT, DVA], stack=s1)
                Cst = sb("Cst", [P, 2, 2, DVA], stack=s1)
                junkH = sb("junkH", [P, DV], stack=s1)
                with ExitStack() as s2:
                    frow = sb("frow", [8, TT * P], stack=s2)
                    lrow = sb("lrow", [8, TT * P], stack=s2)
                    urow = sb("urow", [8, TT * P], stack=s2)
                    brow = sb("brow", [8, TT * P], stack=s2)
                    mrow = sb("mrow", [8, TT * P], stack=s2)
                    mpv = sb("mpv", [8, TT + 1], stack=s2)
                    dg8 = sb("dg8", [8, 2, 8, TT], stack=s2)
                    zer = sb("zer", [8, L], stack=s2)
                    ones8 = sb("ones8", [8, P], stack=s2)
                    gstk = kT
                kw = sb("kw", [P, 2, TT, DQK], stack=s1)
                Hh = sb("Hh", [P, LT, DV], stack=s1)
                sgo = sb("sgo", [P, 2, NLAT], stack=s1)
        with ExitStack() as sU:
            with ExitStack() as s3:
                V = sb("V", [P, LT, D], stack=s3)
                ada2 = [sb(f"ada2_{k}", [P, D], stack=s3) for k in range(4)]
                Tacc = sb("Tacc", [P, 4, D], stack=s3)
            with ExitStack() as s4:
                xs = sb("xs", [P, LT, D], stack=s4)
            Y_hi = sb("Y_hi", [P, LT, KT, P], F32R, sU)
            with ExitStack() as s5:
                ya_raw = sb("ya_raw", [P, LT, KT, P], stack=s5)
            Y_lo = sb("Y_lo", [P, LT, KT, P], F32R, sU)
            with ExitStack() as s6:
                vn_hi = [sb(f"vn_hi{k}", [P, LT, P], F32R, s6) for k in range(2)]
                vn_lo = [sb(f"vn_lo{k}", [P, LT, P], F32R, s6) for k in range(2)]
                uT = [sb(f"uT{k}", [P, NLAT], stack=s6) for k in range(2)]
                wsp = sb("wsp", [P, 4, P], stack=s6)
                wsp_hi = sb("wsp_hi", [P, 4, P], F32R, s6)
                wsp_lo = sb("wsp_lo", [P, 4, P], F32R, s6)
                bspB = sb("bspB", [P, 4, P], stack=s6)
            Mb = sb("Mb", [P, KT, NLAT], stack=sU)
            sg = sb("sg", [P, NLAT], stack=sU)
        with ExitStack() as sF:
            sb("xs_place", [P, LT, D], stack=sF)
            g2B = sb("g2B", [P, D], stack=sF)
            junkF = sb("junkF", [P, D], stack=sF)
            fg = sb("fg", [P, D], stack=sF)
            with ExitStack() as s7:
                xn = sb("xn", [P, LT, D], stack=s7)
            wC_hi = sb("wC_hi", [P, 8 * CW], F32R, sF)
            wC_lo = sb("wC_lo", [P, 8 * CW], F32R, sF)
            f_hi = sb("f_hi", [P, 2, NLAT], F32R, sF)
            f_lo = sb("f_lo", [P, 2, NLAT], F32R, sF)
            sa = sb("sa", [P, 2, NLAT], stack=sF)
            hT = [sb(f"hT{k}", [P, NLAT], stack=sF) for k in range(2)]
        whi.append(wC_hi)
        wlo.append(wC_lo)

        PD = [es.enter_context(nc.psum_tensor(f"PD{s}", [P, 2 * HALF], F32)) for s in range(2)]
        PM = es.enter_context(nc.psum_tensor("PM", [P, 4 * HALF], F32))

        consts = sem("consts")
        vec_in = sem("vec_in")
        gate_in = sem("gate_in")
        x_in = [sem(f"x_in{t}") for t in range(TT)]
        ada_in = [sem(f"ada_in{k}") for k in range(4)]
        raw_in = [sem(f"raw_in{k}") for k in range(2)]
        hi_done = sem("hi_done")
        w_ready = [sem(f"w_ready{k}") for k in range(2)]
        tile_done = sem("tile_done")
        slot_free = [sem(f"slot_free{s}") for s in range(2)]
        dve_own = sem("dve_own")
        act_own = sem("act_own")
        pool_own = sem("pool_own")
        vecT = sem("vecT")
        cols_ready = sem("cols_ready")
        cth_ready = sem("cth_ready")
        csil_ready = sem("csil_ready")
        mod1_ready = sem("mod1_ready")
        xn_ready = sem("xn_ready")
        xT_done = sem("xT_done")
        xT_read = [sem(f"xT_read{s}") for s in range(2)]
        ada_mm = sem("ada_mm")
        adarow_ready = sem("adarow_ready")
        adacol_done = sem("adacol_done")
        h_ready = sem("h_ready")
        h_act = sem("h_act")
        h_hi = sem("h_hi")
        h_lo = sem("h_lo")
        wgz_ready = sem("wgz_ready")
        wg_hi_done = sem("wg_hi_done")
        f_copied = sem("f_copied")
        wg_ready = sem("wg_ready")
        gates_mm = sem("gates_mm")
        sig_arg = sem("sig_arg")
        sig_ln = sem("sig_ln")
        stk_zero = sem("stk_zero")
        row_ready = sem("row_ready")
        gcol_done = sem("gcol_done")
        exp_arg = sem("exp_arg")
        g5_ready = sem("g5_ready")
        head_cols = sem("head_cols")
        conv_done = sem("conv_done")
        th_done = sem("th_done")
        qk_ready = sem("qk_ready")
        nb_done = sem("nb_done")
        nm_ready = sem("nm_ready")
        wb_ready = sem("wb_ready")
        d_ready = sem("d_ready")
        ktr_done = sem("ktr_done")
        ktok_ready = sem("ktok_ready")
        s_done = sem("s_done")
        sw_ready = sem("sw_ready")
        kw_ready = sem("kw_ready")
        qw_ready = sem("qw_ready")
        dc_done = sem("dc_done")
        c_ready = sem("c_ready")
        num_done = sem("num_done")
        h_written = sem("h_written")
        hn_ready = sem("hn_ready")
        yt_done = sem("yt_done")
        sgo_ready = sem("sgo_ready")
        pm_free = sem("pm_free")
        spill = sem("spill")
        small_in = sem("small_in")
        wspT_done = sem("wspT_done")
        wsp_hi_d = sem("wsp_hi_d")
        wsp_ready = sem("wsp_ready")
        ada2_in = [sem(f"ada2_in{k}") for k in range(4)]
        ada2_used = sem("ada2_used")
        T_mm = sem("T_mm")
        mod_ready = sem("mod_ready")
        v_scaled = sem("v_scaled")
        vn_hi_d = sem("vn_hi_d")
        vn_ready = sem("vn_ready")
        sv_done = sem("sv_done")
        y_f32 = sem("y_f32")
        y_hi_d = sem("y_hi_d")
        yb_ready = sem("yb_ready")
        ya_in = [sem(f"ya_in{k}") for k in range(KT)]
        ya_hi_d = sem("ya_hi_d")
        ya_ready = sem("ya_ready")
        ga_done = sem("ga_done")
        ga_th = sem("ga_th")
        ga_used = sem("ga_used")
        m_hi_d = sem("m_hi_d")
        m_ready = sem("m_ready")
        x2_in = sem("x2_in")
        gB_mm = sem("gB_mm")
        xn2_ready = sem("xn2_ready")
        xn2_act = sem("xn2_act")
        h2_hi = sem("h2_hi")
        h2_lo = sem("h2_lo")
        f_hi_d = sem("f_hi_d")
        f_lo_d = sem("f_lo_d")
        fg_in = sem("fg_in")
        g2_ready = sem("g2_ready")
        rs_ready = sem("rs_ready")
        w2_scaled = sem("w2_scaled")
        x_scaled = sem("x_scaled")
        o_pool = sem("o_pool")
        o_ready = sem("o_ready")
        out_done = sem("out_done")

        block = es.enter_context(nc.Block())

        @block.sync
        def _(sp):
            def load_vectors():
                for at, v in ((0, c), (8, c_ctx.rearrange("(o n) -> o n", o=1)), (16, norm1_g), (24, norm2_g)):
                    sp.dma_start(rows1[at:at + KT, :], v.rearrange("o (k p) -> (o k) p", p=P)).then_inc(vec_in, 16)
                sp.dma_start(rows1[32:80, :], b_ada.rearrange("o (k p) -> (o k) p", p=P)).then_inc(vec_in, 16)
                sp.dma_start(rows1[80:88, :], conv_b.rearrange("o (k p) -> (o k) p", p=P)).then_inc(vec_in, 16)
                sp.dma_start(rows1[88:128, :], conv_w.rearrange("o m (k p) -> (o m k) p", p=P)).then_inc(vec_in, 16)
                sp.dma_start(rows2[0:8, :], head_g.rearrange("o h (k p) -> (o h k) p", p=P)).then_inc(vec_in, 16)
                sp.dma_start(rows2[8:16, :], vnorm_g.rearrange("o (k p) -> (o k) p", p=P)).then_inc(vec_in, 16)

            for t in range(TT):
                src = ctx_t[:, t, :] if t < CT else x_t[:, t - CT, :]
                sp.dma_start(xtok[:, t, :], src).then_inc(x_in[t], 16)
                if t == 3:
                    load_vectors()
            for k in range(KT):
                if k >= 4:
                    sp.wait_ge(ada_mm, k - 3)
                sp.dma_start(ada_raw[k % 4][:, :], ada_v[:, k, 0:2 * D]).then_inc(ada_in[k % 4], 16)

            def load(n, *sources):
                for half in range(2):
                    for view, col, width in sources:
                        sp.lower_ap_dma(view[:, 4 * half:4 * half + 4, ds(col, width)])
                    sp.wait_ge(w_ready[half], n + 1)
                    at = 0
                    for view, col, width in sources:
                        dst = raw[half][:, :].rearrange("p (k n) -> p k n", k=4)[:, :, at:at + width]
                        sp.dma_start(dst, view[:, 4 * half:4 * half + 4, ds(col, width)])\
                            .then_inc(raw_in[half], 16)
                        at += width

            def load_rows(n, block_no):
                for half in range(2):
                    sp.lower_ap_dma(f2_v[:, ds(block_no * 2 + half, 1), :])
                    sp.wait_ge(w_ready[half], n + 1)
                    dst = raw[half][:, :].rearrange("p (o n) -> p o n", o=1)
                    sp.dma_start(dst, f2_v[:, ds(block_no * 2 + half, 1), :]).then_inc(raw_in[half], 16)

            def load_qk(h):
                load(h * 3, (win_v, h * DQK + CQ, DQK), (win_v, h * DQK + CK, DQK))

            def load_v(h):
                load(h * 3 + 1, (win_v, h * DV + CV, CW))

            def load_o(h):
                load(h * 3 + 2, (win_v, h * DV + CO, CW))

            def spill_ya(h):
                sp.lower_ap_dma(ya_dram[:, ds(h * 2, 2), :])
                sp.wait_ge(pm_free, h * 2 + 4)
                sp.dma_start(ya_dram[:, ds(h * 2, 2), :], sgo[:, :, :]).then_inc(spill, 16)

            load_qk(0)
            load_v(0)
            with sp.Fori(0, HEADS - 1) as h:
                load_o(h)
                load_qk(h + 1)
                load_v(h + 1)
                spill_ya(h)
            load_o(HEADS - 1)
            load(N_V, (win_v, CVB, DQK), (win_v, CVB + DQK, DQK))
            load(N_V + 1, (win_v, CVB + CW, CW))
            spill_ya(HEADS - 1)
            with sp.Fori(2, 4) as i:
                load(i + N_V, (win_v, i * CW + CVB, CW))
            with sp.Fori(0, 4) as i:
                load(i + N_U, (win_v, i * CW + CU, CW))
            with sp.Fori(0, 4) as i:
                load(i * 2 + N_PB, (win_v, i * CW + CGB, CW))
                load(i * 2 + (N_PB + 1), (pb_v, i * CW, CW))
            with sp.Fori(0, 4) as i:
                load(i * 2 + N_PA, (win_v, i * CW + CGA, CW))
                load(i * 2 + (N_PA + 1), (pa_v, i * CW, CW))
            with sp.Fori(0, 4) as i:
                load(i + N_O, (wo_v, i * CW, CW))
            load(N_F, (f1_v, 0, CW))
            load(N_F + 1, (f3_v, 0, CW))
            load(N_F + 2, (f1_v, CW, CW))
            with sp.Fori(0, NFB - 2) as r:
                load_rows(r * 3 + (N_F + 3), r)
                load(r * 3 + (N_F + 4), (f3_v, r * CW + CW, CW))
                load(r * 3 + (N_F + 5), (f1_v, r * CW + 2 * CW, CW))
            last = NFB - 2
            load_rows(N_F + 3 + 3 * last, last)
            load(N_F + 4 + 3 * last, (f3_v, (last + 1) * CW, CW))
            load_rows(N_F + 5 + 3 * last, last + 1)
            for t in range(LT):
                if t < 4:
                    sp.wait_ge(o_pool, t + 1)
                else:
                    sp.wait_ge(o_ready, t - 3)
                sp.dma_start(out_t[:, t, :], xs[:, t, :]).then_inc(out_done, 16)
            sp.wait_ge(out_done, 16 * LT)

        @block.gpsimd
        def _(pool):
            own = Chain(pool, pool_own)
            own.link(nc.gpsimd.memset(ident[:, :], 0.0))
            nc.gpsimd.affine_select(out=ident[:, :], in_=ident[:, :], compare_op=ALU.not_equal, fill=1.0,
                                    base=0, pattern=[[-1, P]], channel_multiplier=1).then_inc(consts, 1)
            pool.dma_start(wg[:, :, :], win_v[:, :, CG:CG + 16]).then_inc(gate_in, 16)
            for d in range(2):
                for kind in range(2):
                    at = 8 * d + 4 * kind
                    pool.dma_start(gb8[4 * d:4 * d + 4, kind:kind + 1],
                                  gate_b[:, at:at + 4].rearrange("o (h e) -> (o h) e", e=1)).then_inc(gate_in, 16)
            nc.gpsimd.memset(one1[:, :], 1.0).then_inc(consts, 1)
            nc.gpsimd.memset(wgz[:, :, :, :], 0.0).then_inc(consts, 1)
            credits = 0
            for s, count in ((w_ready[0], 1), (w_ready[1], 1), (spill, 1), (ada2_used, 4),
                             (sv_done, 2), (yb_ready, 2), (ga_th, 2), (ga_used, 1),
                             (slot_free[0], 1), (slot_free[1], 1)):
                for _ in range(count):
                    nc.gpsimd.memset(note[:, credits:credits + 1], 0.0).then_inc(s, 1)
                    credits += 1
            pool.wait_ge(h_lo, 2 * KT)
            pool.wait_ge(gates_mm, 1)
            nc.gpsimd.memset(gstk[:, :], 0.0).then_inc(stk_zero, 1)
            nc.gpsimd.memset(zer[:, :], 0.0).then_inc(consts, 1)
            nc.gpsimd.memset(ones8[:, :], 1.0).then_inc(consts, 1)
            nc.gpsimd.memset(mpv[:, :], 0.0).then_inc(consts, 1)
            own.link(nc.gpsimd.memset(mask[:, :, :], 0.0))
            for d, sign in ((0, 1), (1, -1)):
                nc.gpsimd.affine_select(out=mask[:, d, :], in_=mask[:, d, :], compare_op=ALU.is_ge, fill=NEG,
                                        base=0, pattern=[[sign, L]], channel_multiplier=-sign)\
                    .then_inc(consts, 1)
            for pad in (slice(0, PAD), slice(PAD + NLAT, 2 * PAD + NLAT)):
                nc.gpsimd.memset(work[:, :, pad], 0.0).then_inc(consts, 1)
            for pad in (slice(0, PAD), slice(PAD + NCTX, 2 * PAD + NCTX)):
                nc.gpsimd.memset(kcraw[:, pad], 0.0).then_inc(consts, 1)
            nc.gpsimd.memset(vaug[:, :, DV:DVA], 1.0).then_inc(consts, 1)
            with pool.Fori(0, HEADS) as h:
                pool.wait_ge(wb_ready, h + 1)
                pool.wait_ge(qk_ready, h * 2 + 2)
                for d in range(2):
                    nc.gpsimd.tensor_tensor(WB[:, d, :], WB[:, d, :], qT[:, :], ALU.mult)\
                        .then_inc(qw_ready, 1)
                pool.wait_ge(ktok_ready, h * 2 + 2)
                for d in range(2):
                    nc.gpsimd.tensor_tensor(kw[:, d, :, :], ktok[:, :, :],
                                            hc[:, 1, d, :].unsqueeze(2).to_broadcast([P, TT, DQK]),
                                            ALU.mult).then_inc(kw_ready, 1)
            pool.wait_ge(spill, 16 * HEADS + 1)
            pool.dma_start(wsp[:, :, :], w_spatial.rearrange("o g t s -> (o t) g s")).then_inc(small_in, 16)
            pool.dma_start(bspB[:, :, :].rearrange("p g t -> p (g t)"),
                           b_spatial.rearrange("o g t -> o (g t)").to_broadcast([P, 4 * P]))\
                .then_inc(small_in, 16)
            with pool.Fori(0, 4) as i:
                for k in range(KT):
                    pool.wait_ge(ada2_used, i * KT + (k + 1))
                    pool.dma_start(ada2[k % 4][:, :], ada_v[:, k, ds(i * D + 2 * D, D)])\
                        .then_inc(ada2_in[k % 4], 16)
            pool.wait_ge(tile_done, T_PA)
            for k in range(KT):
                pool.dma_start(ya_raw[:, :, k, :], ya_dram[:, k, :].rearrange("p (c t) -> p c t", t=P))\
                    .then_inc(ya_in[k], 16)
            pool.wait_ge(tile_done, T_O)
            for t in range(LT):
                pool.dma_start(xs[:, t, :], x_t[:, t, :]).then_inc(x2_in, 16)
            pool.dma_start(fg[:, :], final_g.rearrange("(o n) -> o n", o=1).to_broadcast([P, D]))\
                .then_inc(fg_in, 16)
            pool.wait_ge(g2_ready, 1)

            def scale_w2(n):
                for half in range(2):
                    pool.wait_ge(raw_in[half], n * 16 + 96)
                    nc.gpsimd.tensor_tensor(raw[half][:, :], raw[half][:, :], g2B[:, :], ALU.mult)\
                        .then_inc(w2_scaled, 1)

            with pool.Fori(0, NFB - 1) as r:
                scale_w2(r * 3 + (N_F + 3))
            scale_w2(N_F + 3 * NFB - 1)
            pool.wait_ge(fg_in, 16)
            for t in range(4):
                pool.wait_ge(x_scaled, t + 1)
                nc.gpsimd.tensor_tensor(xs[:, t, :], xs[:, t, :], fg[:, :], ALU.mult).then_inc(o_pool, 1)

        @block.scalar
        def _(act):
            own = Chain(act, act_own)
            def split_hi(raw_at, buf, free=None, scaled=None):
                if free is not None:
                    act.wait_ge(tile_done, free)
                for half in range(2):
                    if scaled is None:
                        act.wait_ge(raw_in[half], raw_at)
                    else:
                        act.wait_ge(w2_scaled, scaled + half)
                    nc.scalar.activation(whi[buf][:, half * 4 * CW:(half + 1) * 4 * CW], raw[half][:, :],
                                         ACT.Copy).then_inc(hi_done, 1)

            def split_next(n, buf, free, scaled=None):
                split_hi(n * 16 + 96, buf, free, scaled)

            for t in range(TT):
                if t == 7:
                    act.wait_ge(cols_ready, 1)
                    nc.scalar.activation(cth[:, :], cols[:, 0:2 * KT], ACT.Tanh, scale=0.5).then_inc(cth_ready, 1)
                act.wait_ge(x_in[t], 16)
                own.link(nc.scalar.activation(xnT[:, 0, 0:D], xtok[:, t, :], ACT.Square,
                                              accum_out=rs[:, 0, t:t + 1]))
            for t in range(TT):
                act.wait_ge(xT_done, t + 1)
                nc.scalar.activation(xnT[:, :, t * P:(t + 1) * P],
                                     PD[t % 2][:, :].rearrange("p (k t) -> p k t", k=KT), ACT.Copy)\
                    .then_inc(xT_read[t % 2], 1)
            act.wait_ge(wgz_ready, 4)
            nc.scalar.activation(wg_hi[:, :, :, :], wgz[:, :, :, :], ACT.Copy).then_inc(wg_hi_done, 1)
            act.wait_ge(mod1_ready, 1)
            act.wait_ge(xT_read[1], TT // 2)
            act.wait_ge(xT_read[0], TT // 2)
            h32 = xtok[:, :, :].rearrange("p t n -> p (t n)")
            for k in range(KT):
                for s, dst, src in ((0, R_hi, xnT[:, k, NCTX:]), (1, ctx_hi, xnT[:, k, 0:NCTX])):
                    if s == 1 or k % 2 == 1:
                        at = k * TT * P + (0 if s == 0 else NLAT)
                        nc.scalar.activation(h32[:, at:at + (NLAT if s == 0 else NCTX)], src, ACT.Identity,
                                             scale=a1[:, s, k:k + 1], bias=b1[:, s, k:k + 1]).then_inc(h_act, 1)
                    nc.scalar.activation(dst[:, k, :], src, ACT.Identity, scale=a1[:, s, k:k + 1],
                                         bias=b1[:, s, k:k + 1]).then_inc(h_hi, 1)
            act.wait_ge(ada_mm, KT)
            split_hi(32, A)
            split_hi(48, B)
            act.wait_ge(gates_mm, 1)
            for (at, width), src in (((0, NCTX), PM[32:GM, NLAT:NLAT + NCTX]), ((NCTX, NLAT), PM[32:GM, 0:NLAT])):
                nc.scalar.activation(frow[:, at:at + width], src, ACT.Copy).then_inc(f_copied, 1)
            act.wait_ge(sig_arg, 1)
            own.link(nc.scalar.activation(lrow[:, :], lrow[:, :], ACT.Exp, scale=-1.0))
            nc.scalar.activation(lrow[:, :], lrow[:, :], ACT.Ln, bias=1.0).then_inc(sig_ln, 1)
            act.wait_ge(exp_arg, 1)
            nc.scalar.activation(G5[:, 1, :, :], G5[:, 1, :, :], ACT.Exp).then_inc(g5_ready, 1)
            nc.scalar.activation(G5[:, 2, :, :], G5[:, 2, :, :], ACT.Exp, scale=-1.0).then_inc(g5_ready, 1)
            nc.scalar.activation(G5[:, 4, :, :], G5[:, 4, :, :], ACT.Exp).then_inc(g5_ready, 1)
            act.wait_ge(consts, 13)

            with act.Fori(0, HEADS) as h:
                T = h * HT + T_H
                act.wait_ge(tile_done, T + 1)
                nc.scalar.activation(work[:, 0, PAD:PAD + NLAT], PD[0][:, :], ACT.Copy).then_inc(slot_free[0], 1)
                act.wait_ge(tile_done, T + 2)
                nc.scalar.activation(work[:, 1, PAD:PAD + NLAT], PD[1][:, :], ACT.Copy).then_inc(slot_free[1], 1)
                act.wait_ge(tile_done, T + 3)
                nc.scalar.activation(kcraw[:, PAD:PAD + NCTX], PD[0][:, 0:NCTX], ACT.Copy)\
                    .then_inc(slot_free[0], 1)
                act.wait_ge(conv_done, h * 3 + 1)
                nc.scalar.activation(WB[:, 0, :], qT[:, :], ACT.Tanh, scale=0.5).then_inc(th_done, 1)

                def v_out(n):
                    s = (3 + n) % 2
                    act.wait_ge(tile_done, T + (4 + n))
                    nc.scalar.activation(vaug[:, 2 * n:2 * n + 2, 0:DV],
                                         PD[s][:, :].rearrange("p (t n) -> p t n", t=2)[:, :, 0:DV],
                                         ACT.Copy).then_inc(slot_free[s], 1)

                act.wait_ge(conv_done, h * 3 + 2)
                nc.scalar.activation(WB[:, 1, :], kT[:, NCTX:], ACT.Tanh, scale=0.5).then_inc(th_done, 1)
                v_out(0)
                act.wait_ge(conv_done, h * 3 + 3)
                nc.scalar.activation(junkH[:, :], kT[:, 0:NCTX], ACT.Tanh, scale=0.5).then_inc(th_done, 1)
                split_hi(h * 64 + 64, A, T + 3)
                v_out(1)
                act.wait_ge(nb_done, h + 1)
                act.wait_ge(qk_ready, h * 2 + 2)
                for d in range(2):
                    act.wait_ge(nm_ready, h * 2 + (d + 1))
                    for t in range(LT):
                        at = d * NLAT + t * L
                        i = nc.scalar.activation(WB[:, d, t * L:(t + 1) * L], PM[:, at:at + L], ACT.Exp,
                                                 bias=hc[:, 3, d, CT + t:CT + t + 1])
                i.then_inc(wb_ready, 1)
                for n in range(2, 5):
                    v_out(n)
                act.wait_ge(nm_ready, h * 2 + 2)
                for d in range(2):
                    for t in range(LT):
                        at = PAD + t * L
                        i = nc.scalar.activation(work[:, d, at:at + L], work[:, d, at:at + L], ACT.Exp,
                                                 bias=hc[:, 0, d, CT + t:CT + t + 1])
                i.then_inc(d_ready, 1)
                for m in range(2):
                    act.wait_ge(spill, h * 16 + 1)
                    act.wait_ge(tile_done, T + (9 + m))
                    nc.scalar.activation(sgo[:, m, :], PD[m][:, :], ACT.Tanh, scale=0.5).then_inc(slot_free[m], 1)
                    act.wait_ge(slot_free[m], h * 5 + 6)
                    nc.scalar.activation(sgo[:, m, :], sgo[:, m, :], ACT.Identity, scale=hgh[:, m:m + 1],
                                         bias=hgh[:, m:m + 1]).then_inc(sgo_ready, 1)
                split_hi(h * 64 + 96, A)
                split_hi(h * 64 + 112, B)
                own.enter(h, LT)
                for n, t in enumerate((4, 3, 5, 2, 6, 1, 7, 0)):
                    act.wait_ge(h_written, h * 16 + (10 + n // 2 * 2))
                    own.link(nc.scalar.activation(junkH[:, :], Hh[:, t, :], ACT.Square,
                                                  accum_out=rs[:, 0, t:t + 1]))
                own.leave(HEADS)

            act.wait_ge(pm_free, 10)
            with act.Fori(0, 2) as i:
                for cc in range(2):
                    for p in range(4):
                        act.wait_ge(tile_done, i * 8 + (T_V + 4 * cc + p + 1))
                        nc.scalar.activation(V[:, 2 * p:2 * p + 2, ds(i * (2 * CW) + cc * CW, CW)],
                                             PD[p % 2][:, :].rearrange("p (t n) -> p t n", t=2)[:, :, 0:CW],
                                             ACT.Gelu_apprx_tanh).then_inc(slot_free[p % 2], 1)
                    split_next(i * 2 + (N_V + 2 + cc), cc, i * 8 + (T_V + 4 * cc + 4))
            for s in range(2):
                act.wait_ge(slot_free[s], T_U // 2 + 1)
            for t in range(LT):
                own.link(nc.scalar.activation(uT[0][:, :], V[:, t, :], ACT.Square, accum_out=rs[:, 0, t:t + 1]))
            act.wait_ge(wspT_done, 1)
            nc.scalar.activation(wsp_hi[:, :, :], PM[:, HALF:2 * HALF].rearrange("p (g t) -> p g t", g=4),
                                 ACT.Copy).then_inc(wsp_hi_d, 1)

            act.wait_ge(v_scaled, LT)
            with act.Fori(0, 2) as i:
                for hh in range(2):
                    for jj in (2 * hh, 2 * hh + 1):
                        b = jj % 2
                        act.wait_ge(sv_done, i * 4 + (jj + 1))
                        nc.scalar.activation(vn_hi[b][:, :, :], V[:, :, ds(i * (4 * P) + jj * P, P)], ACT.Copy)\
                            .then_inc(vn_hi_d, 1)
                    for jj in (2 * hh, 2 * hh + 1):
                        b = jj % 2
                        act.wait_ge(yb_ready, i * 4 + (jj + 1))
                        act.wait_ge(tile_done, i * 4 + (T_U + jj + 1))
                        nc.scalar.activation(uT[b][:, :], PD[b][:, :], ACT.Gelu_apprx_tanh)\
                            .then_inc(slot_free[b], 1)
                    for jj in (2 * hh, 2 * hh + 1):
                        b = jj % 2
                        act.wait_ge(y_f32, i * 4 + (jj + 1))
                        nc.scalar.activation(Y_hi[:, :, ds(i * 4 + jj, 1), :],
                                             uT[b][:, :].rearrange("p (c o t) -> p c o t", o=1, t=P), ACT.Copy)\
                            .then_inc(y_hi_d, 1)
                    split_next(i * 2 + (N_U + 2 + hh), hh, i * 4 + (T_U + 2 * hh + 2))

            act.wait_ge(yb_ready, KT + 2)
            act.wait_ge(y_hi_d, KT)
            with act.Fori(0, 4) as i:
                for m in range(2):
                    act.wait_ge(tile_done, i * 4 + (T_PB + m + 1))
                    nc.scalar.activation(Mb[:, ds(i * 2 + m, 1), :],
                                         PD[m][:, :].rearrange("p (o t) -> p o t", o=1), ACT.Tanh, scale=0.5)\
                        .then_inc(slot_free[m], 1)
                split_next(i * 2 + (N_PB + 2), A, i * 4 + (T_PB + 2))
                split_next(i * 2 + (N_PB + 3), B, i * 4 + (T_PB + 4))

            for k in range(KT):
                act.wait_ge(ya_in[k], 16)
                nc.scalar.activation(Y_hi[:, :, k, :], ya_raw[:, :, k, :], ACT.Copy).then_inc(ya_hi_d, 1)

            def m_hi(k):
                act.wait_ge(slot_free[k % 2], (T_PA + k) // 2 + 2)
                nc.scalar.activation(R_hi[:, k, :], Mb[:, k, :], ACT.Copy, scale=0.5).then_inc(m_hi_d, 1)

            def gates_a(i, last):
                for m in range(2):
                    act.wait_ge(ga_done, i * 2 + (m + 1))
                    act.wait_ge(ga_used, i * 2 + (m + 1))
                    nc.scalar.activation(sg[:, :], PM[:, m * NLAT:(m + 1) * NLAT], ACT.Tanh, scale=0.5)\
                        .then_inc(ga_th, 1)
                split_next(i * 2 + (N_PA + 2), A, None)
                if last:
                    for k in range(KT):
                        m_hi(k)
                split_next(i * 2 + (N_PA + 3), B, i * 2 + (T_PA + 2))

            with act.Fori(0, 3) as i:
                gates_a(i, False)
            gates_a(3, True)

            for n in range(3):
                split_next(N_O + 2 + n, n % 2, T_O + 4 * n + 4)
            for t in range(LT):
                T = T_O + 12 + t // 2
                act.wait_ge(slot_free[T % 2], T // 2 + 2)
                own.link(nc.scalar.activation(junkF[:, :], xs[:, t, :], ACT.Square, accum_out=rs[:, 0, t:t + 1]))
            act.wait_ge(rs_ready, 1)
            for t in (4, 5):
                nc.scalar.activation(xn[:, t, :], xs[:, t, :], ACT.Copy, scale=rs[:, 2, t:t + 1])\
                    .then_inc(xn2_act, 1)
            split_next(N_F + 1, B, T_O + 16)
            for k in range(KT):
                if k % 2 == 1:
                    if k >= 2:
                        act.wait_ge(h2_lo, k - 1)
                    act.wait_ge(tile_done, T_X + k + 1)
                    nc.scalar.activation(hT[1][:, :], PD[1][:, :], ACT.Identity, scale=a2[:, k:k + 1],
                                         bias=mod[:, 3, k:k + 1]).then_inc(slot_free[1], 1)
                act.wait_ge(slot_free[k % 2], (T_X + k) // 2 + 2)
                nc.scalar.activation(R_hi[:, k, :], hT[k % 2][:, :], ACT.Copy).then_inc(h2_hi, 1)

            def silu_out(free, m):
                act.wait_ge(tile_done, free)
                nc.scalar.activation(sa[:, m, :], PD[m][:, :], ACT.Silu).then_inc(slot_free[m], 1)

            def f_split(count, m):
                act.wait_ge(slot_free[m], count)
                nc.scalar.activation(f_hi[:, m, :], sa[:, m, :], ACT.Copy).then_inc(f_hi_d, 1)

            silu_out(T_F + 1, 0)
            silu_out(T_F + 2, 1)
            split_next(N_F + 2, A, T_F + 2)
            for m in range(2):
                f_split(T_F // 2 + 3, m)

            def ffn(r, last):
                T = r * FT + (T_F + 4)
                n = r * 3 + (N_F + 3)
                split_next(n, C, T - 2, r * 2 + 1)
                for m in range(2):
                    act.wait_ge(f_lo_d, r * 2 + (m + 1))
                    silu_out(T + (m + 1), m)
                split_next(n + 1, B, T)
                if not last:
                    split_next(n + 2, A, T + 2)
                for m in range(2):
                    f_split(r * 6 + (T_F // 2 + 9), m)

            with act.Fori(0, NFB - 2) as r:
                ffn(r, False)
            ffn(NFB - 2, True)
            split_next(N_F + 3 * NFB - 1, C, T_F + 4 + FT * (NFB - 2) + 10, 2 * NFB - 1)
            for t in range(LT):
                act.wait_ge(slot_free[t % 2], (T_F + 4 + FT * (NFB - 1) + t) // 2 + 2)
                own.link(nc.scalar.activation(junkF[:, :], xs[:, t, :], ACT.Square, accum_out=rs[:, 0, t:t + 1]))
                if t == 4:
                    act.wait_ge(rs_ready, 2)
                    for u in range(4):
                        nc.scalar.activation(xs[:, u, :], xs[:, u, :], ACT.Copy, scale=rs[:, 2, u:u + 1])\
                            .then_inc(x_scaled, 1)
        @block.vector
        def _(dve):
            own = Chain(dve, dve_own)
            v = nc.vector

            def rsqrt(n, count, first=0):
                s, a, y, t = (rs[:, k, first:n] for k in range(4))
                own.link(v.tensor_scalar(a, s, 1.0 / count, EPS, ALU.mult, ALU.add))
                own.link(v.tensor_scalar(t.bitcast(I32), a.bitcast(I32), 1, None, ALU.logical_shift_right))
                own.link(v.tensor_scalar(y.bitcast(I32), t.bitcast(I32), -1.0, MAGIC, ALU.mult, ALU.add))
                for _ in range(3):
                    own.link(v.tensor_tensor(t, y, y, ALU.mult))
                    own.link(v.scalar_tensor_tensor(out=t, in0=t, scalar=-0.5, in1=a, op0=ALU.mult, op1=ALU.mult))
                    own.link(v.scalar_tensor_tensor(out=y, in0=t, scalar=1.5, in1=y, op0=ALU.add, op1=ALU.mult))

            def split_lo(n, buf, halves=(0, 1)):
                for half in halves:
                    at = slice(half * 4 * CW, (half + 1) * 4 * CW)
                    dve.wait_ge(hi_done, n * 2 + (half + 1))
                    v.tensor_tensor(wlo[buf][:, at], raw[half][:, :], whi[buf][:, at].bitcast(F32),
                                    ALU.subtract).then_inc(w_ready[half], 1)

            for first, end in ((0, 4), (4, 7), (7, TT)):
                dve.wait_ge(act_own, end)
                rsqrt(end, D, first)
                for t in range(first, end):
                    v.tensor_scalar(xtok[:, t, :], xtok[:, t, :], rs[:, 2, t:t + 1], None, ALU.mult)\
                        .then_inc(xn_ready, 1)
                if first == 0:
                    dve.wait_ge(vecT, 1)
                    own.link(v.tensor_copy(cols2[:, :], PM[:, P:P + 16]))
                    v.tensor_copy(cols[:, :], PM[:, 0:P]).then_inc(cols_ready, 1)
                    dve.wait_ge(cth_ready, 1)
                    dve.wait_ge(cols_ready, 1)
                    flat = csil[:, :, :].rearrange("p s k -> p (s k)")
                    own.link(v.scalar_tensor_tensor(out=flat, in0=cth[:, :], scalar=1.0, in1=cols[:, 0:2 * KT],
                                                    op0=ALU.add, op1=ALU.mult))
                    v.tensor_scalar(flat, flat, 0.5, None, ALU.mult).then_inc(csil_ready, 1)
            dve.wait_ge(gate_in, 16 * 5)
            dve.wait_ge(consts, 3)
            for kind in range(2):
                for d in range(2):
                    at = 32 * kind + 4 * d
                    i = v.tensor_copy(wgz[:, :, d, at:at + 4], wg[:, :, 8 * d + 4 * kind:8 * d + 4 * kind + 4])
                    i.then_inc(wgz_ready, 1)
            dve.wait_ge(wg_hi_done, 1)
            v.tensor_tensor(wg_lo[:, :, :, :], wgz[:, :, :, :], wg_hi[:, :, :, :].bitcast(F32), ALU.subtract)\
                .then_inc(wg_ready, 1)
            dve.wait_ge(ada_mm, KT)
            v.tensor_copy(xtok[0:2, 0:2, :].rearrange("p a b -> p (a b)"), PM[0:2, :]).then_inc(adarow_ready, 1)
            dve.wait_ge(adacol_done, 1)
            own.link(v.tensor_tensor(b1[:, :, :], PM[:, 0:4 * KT].rearrange("p (j s) -> p s j", s=2),
                                     cols[:, 32:48].unsqueeze(1).to_broadcast([P, 2, 2 * KT]), ALU.add))
            for s in range(2):
                i = v.scalar_tensor_tensor(out=a1[:, s, :], in0=b1[:, s, KT:2 * KT], scalar=1.0,
                                           in1=cols[:, 16:24], op0=ALU.add, op1=ALU.mult)
                if s == 0:
                    own.link(i)
            i.then_inc(mod1_ready, 1)
            dve.wait_ge(mod1_ready, 1)
            dve.wait_ge(xT_read[0], TT // 2)
            dve.wait_ge(xT_read[1], TT // 2)
            h32 = xtok[:, :, :].rearrange("p t n -> p (t n)")

            def h_float(k, s):
                at = k * TT * P + (0 if s == 0 else NLAT)
                dst = h32[:, at:at + (NLAT if s == 0 else NCTX)]
                if s == 0 and k % 2 == 0:
                    v.tensor_scalar(dst, xnT[:, k, NCTX:], a1[:, 0, k:k + 1], b1[:, 0, k:k + 1],
                                    ALU.mult, ALU.add).then_inc(h_ready, 1)
                return dst

            for k in range(KT):
                latent = h_float(k, 0)
                for s, hi, lo, h in ((0, R_hi, R_lo, latent), (1, ctx_hi, ctx_lo, h_float(k, 1))):
                    if s == 0 and k % 2 == 0:
                        dve.wait_ge(h_ready, k // 2 + 1)
                    else:
                        dve.wait_ge(h_act, k + (k + 1) // 2 + s)
                    dve.wait_ge(h_hi, 2 * k + s + 1)
                    v.tensor_tensor(lo[:, k, :], h, hi[:, k, :].bitcast(F32), ALU.subtract).then_inc(h_lo, 1)
            split_lo(N_H, A)
            split_lo(N_H + 1, B)

            dve.wait_ge(gates_mm, 1)
            own.link(v.tensor_scalar(urow[:, 0:NCTX], PM[0:8, NLAT:NLAT + NCTX], gb8[:, 0:1], None, ALU.add))
            own.link(v.tensor_scalar(urow[:, NCTX:], PM[0:8, 0:NLAT], gb8[:, 0:1], None, ALU.add))
            dve.wait_ge(f_copied, 2)
            own.link(v.tensor_scalar(frow[:, :], frow[:, :], gb8[:, 1:2], None, ALU.add))
            v.scalar_tensor_tensor(out=lrow[:, :], in0=frow[:, :], scalar=-1.0, in1=frow[:, :],
                                   op0=ALU.mult, op1=ALU.max).then_inc(sig_arg, 1)
            dve.wait_ge(sig_ln, 1)
            own.link(v.scalar_tensor_tensor(out=frow[:, :], in0=frow[:, :], scalar=0.0, in1=lrow[:, :],
                                            op0=ALU.min, op1=ALU.subtract))
            dve.wait_ge(consts, 6)
            for j in range(TT):
                at = slice(j * L, (j + 1) * L)
                i = v.tensor_tensor_scan(brow[:, at], frow[:, at], zer[:, :], 0.0, ALU.add, ALU.add)
            own.link(i)
            own.link(v.tensor_tensor(urow[:, :], urow[:, :], brow[:, :], ALU.subtract))
            for j in range(TT):
                at = slice(j * L, (j + 1) * L)
                own.link(v.tensor_tensor_scan(mrow[:, at], urow[:, at], urow[:, at], mpv[:, j:j + 1],
                                              ALU.max, ALU.max))
                end = slice((j + 1) * L - 1, (j + 1) * L)
                own.link(v.tensor_tensor(mpv[:, j + 1:j + 2], brow[:, end], mrow[:, end], ALU.add))
            for k, vals in ((0, mrow[:, L - 1::L]), (1, mpv[:, 0:TT])):
                v.tensor_tensor(dg8[:, k, :, :], ident[0:8, 0:8].unsqueeze(2).to_broadcast([8, 8, TT]),
                                vals.unsqueeze(1).to_broadcast([8, 8, TT]), ALU.mult)
            v.tensor_scalar(nM[:, :], mrow[:, NCTX:], -1.0, None, ALU.mult)
            dve.wait_ge(stk_zero, 1)
            own.link(v.tensor_tensor(gstk[64:72, :], brow[:, :], mrow[:, :], ALU.add))
            own.link(v.tensor_copy(nMr[:, :], nM[:, NLAT - 1::-1]))
            v.tensor_copy(gstk[0:8, :], urow[:, :])
            for at, src in ((32, urow), (96, gstk[64:72, :])):
                v.tensor_copy(gstk[at:at + 8, 0:NCTX], src[:, NCTX - 1::-1])
                v.tensor_copy(gstk[at:at + 8, NCTX:], src[:, TT * P - 1:NCTX - 1:-1])
            for n, at in enumerate((0, 36, 64, 100)):
                i = v.tensor_copy(gsel[:, 4 * n:4 * n + 4], ident[:, at:at + 4])
            i.then_inc(row_ready, 1)
            dve.wait_ge(gcol_done, 1)
            for k, g in ((0, 0), (1, 2)):
                v.tensor_copy(G5[:, g, :, :],
                              PM[:, 0:160].rearrange("p (t r) -> p r t", r=16)[:, 8 * k:8 * k + 8, :])
            for k, g in ((0, 4), (1, 3)):
                on_all = PM[:, 160 + 80 * k:240 + 80 * k].rearrange("p (r j) -> p r j", j=TT)
                v.tensor_copy(G5[:, g, 0:4, :], on_all[:, 0:4, :])
                v.tensor_copy(G5[:, g, 4:8, 0:CT], on_all[:, 4:8, CT - 1::-1])
                i = v.tensor_copy(G5[:, g, 4:8, CT:], on_all[:, 4:8, TT - 1:CT - 1:-1])
                i.then_inc(pm_free, 1)
            dve.wait_ge(pm_free, 2)
            own.link(v.tensor_tensor(G5[:, 1, :, :], G5[:, 0, :, :], G5[:, 4, :, :], ALU.subtract))
            v.tensor_tensor(G5[:, 4, :, :], G5[:, 3, :, :], G5[:, 4, :, :], ALU.subtract).then_inc(exp_arg, 1)
            dve.wait_ge(g5_ready, 3)
            dve.wait_ge(consts, 13)

            with dve.Fori(0, HEADS) as h:
                own.enter(h, LINKS_H)
                v.tensor_copy(hc[:, :, :, :],
                              G5[:, :, :, :].rearrange("p g (d h) t -> p g d (h t)", d=2)[:, :, :, ds(h * TT, TT)])
                taps = cols[:, 80:128].rearrange("p (m t) -> p m t", t=8)
                v.tensor_copy(cwh[:, 0, :].unsqueeze(2), taps[:, :, ds(h, 1)])
                v.tensor_copy(cwh[:, 1, :].unsqueeze(2), taps[:, :, ds(h + HEADS, 1)])
                v.tensor_scalar(hgh[:, :], cols2[:, ds(h * 2, 2)], 0.5, None, ALU.mult)
                for d in range(2):
                    i = v.tensor_copy(selm[:, d, :], ident[0:8, ds(h + HEADS * d, 1)].to_broadcast([8, P]))
                i.then_inc(head_cols, 1)
                dve.wait_ge(head_cols, h + 1)

                def conv(dst, src, which, width):
                    own.link(v.tensor_scalar(dst, src[:, 0:width], cwh[:, which, 1:2], cwh[:, which, 0:1],
                                             ALU.mult, ALU.add))
                    for m in range(1, TAPS):
                        i = v.scalar_tensor_tensor(out=dst, in0=src[:, m:m + width],
                                                   scalar=cwh[:, which, m + 1:m + 2], in1=dst,
                                                   op0=ALU.mult, op1=ALU.add)
                        if m < TAPS - 1:
                            own.link(i)
                    i.then_inc(conv_done, 1)

                dve.wait_ge(slot_free[0], h * 5 + 2)
                conv(qT[:, :], work[:, 0, :], 0, NLAT)
                dve.wait_ge(slot_free[1], h * 5 + 2)
                conv(kT[:, NCTX:], work[:, 1, :], 1, NLAT)
                dve.wait_ge(slot_free[0], h * 5 + 3)
                conv(kT[:, 0:NCTX], kcraw[:, :], 1, NCTX)
                dve.wait_ge(th_done, h * 3 + 1)
                own.link(v.scalar_tensor_tensor(out=qT[:, :], in0=WB[:, 0, :], scalar=1.0, in1=qT[:, :],
                                                op0=ALU.add, op1=ALU.mult))
                v.tensor_scalar(qT[:, :], qT[:, :], QSCALE, None, ALU.mult).then_inc(qk_ready, 1)
                dve.wait_ge(th_done, h * 3 + 3)
                v.scalar_tensor_tensor(out=kT[:, NCTX:], in0=WB[:, 1, :], scalar=1.0, in1=kT[:, NCTX:],
                                       op0=ALU.add, op1=ALU.mult)
                v.scalar_tensor_tensor(out=kT[:, 0:NCTX], in0=junkH[:, :], scalar=1.0, in1=kT[:, 0:NCTX],
                                       op0=ALU.add, op1=ALU.mult).then_inc(qk_ready, 1)
                split_lo(h * 3 + 2, A)
                dve.wait_ge(nb_done, h + 1)
                for d in range(2):
                    v.tensor_tensor(work[:, d, PAD:PAD + NLAT].rearrange("p (c t) -> p c t", t=L),
                                    PM[:, d * NLAT:(d + 1) * NLAT].rearrange("p (c t) -> p c t", t=L),
                                    mask[:, d, :].unsqueeze(1).to_broadcast([P, LT, L]), ALU.add)\
                        .then_inc(nm_ready, 1)
                dve.wait_ge(ktr_done, h + 1)
                v.tensor_copy(ktok[:, 0:CT, :].rearrange("p t d -> p (t d)"), PM[:, 0:NCTX])\
                    .then_inc(ktok_ready, 1)
                v.tensor_copy(ktok[:, CT:, :].rearrange("p t d -> p (t d)"), PM[:, NLAT:2 * NLAT])\
                    .then_inc(ktok_ready, 1)
                dve.wait_ge(s_done, h + 1)
                dve.wait_ge(d_ready, h + 1)
                for d in range(2):
                    v.tensor_tensor(work[:, d, PAD:PAD + NLAT], PM[:, 0:NLAT], work[:, d, PAD:PAD + NLAT],
                                    ALU.mult).then_inc(sw_ready, 1)
                for j in range(TT):
                    for d in range(2):
                        if j == TT - 1:
                            continue
                        bank = PM[:, (2 + d) * HALF:(2 + d) * HALF + DVA - 1]
                        dve.wait_ge(dc_done, h * 18 + (2 * j + d + 1))
                        if j == 0:
                            v.tensor_copy(Cst[:, d, 1, 0:DVA - 1], bank).then_inc(c_ready, 1)
                        else:
                            dve.wait_ge(c_ready, h * 18 + (2 * j + d - 1))
                            t = tile_of(d, j)
                            v.scalar_tensor_tensor(out=Cst[:, d, (j + 1) % 2, 0:DVA - 1],
                                                   in0=Cst[:, d, j % 2, 0:DVA - 1], scalar=hc[:, 4, d, t:t + 1],
                                                   in1=bank, op0=ALU.mult, op1=ALU.add).then_inc(c_ready, 1)
                    if j in (3, 5):
                        split_lo(h * 3 + (N_H + 3), A, (j // 2 - 1,))
                    if j < CT:
                        continue
                    for d in range(2):
                        t = tile_of(d, j)
                        at = d * HALF if j % 2 else 0
                        bank = (PM if j % 2 else PD[d])[:, at:at + DV]
                        bden = (PM if j % 2 else PD[d])[:, at + DV:at + DV + 1]
                        dve.wait_ge(num_done, h * 16 + (2 * (j - CT) + d + 1))
                        own.link(v.tensor_scalar(den[:, d, 0:1], bden, -1.0, hc[:, 2, d, t:t + 1],
                                                 ALU.mult, ALU.max))
                        own.link(v.tensor_tensor(den[:, d, 1:2], bden, den[:, d, 0:1], ALU.max))
                        own.link(v.reciprocal(den[:, d, 2:3], den[:, d, 1:2]))
                        first = (j - CT < LT // 2)
                        if first:
                            v.tensor_scalar(Hh[:, t - CT, :], bank, den[:, d, 2:3], None, ALU.mult)\
                                .then_inc(h_written, 1)
                        else:
                            v.scalar_tensor_tensor(out=Hh[:, t - CT, :], in0=bank, scalar=den[:, d, 2:3],
                                                   in1=Hh[:, t - CT, :], op0=ALU.mult, op1=ALU.add)\
                                .then_inc(h_written, 1)
                dve.wait_ge(act_own, h * LT + (TT + 1 + LT))
                rsqrt(LT, DV)
                for t in range(LT):
                    i = v.tensor_scalar(Hh[:, t, :], Hh[:, t, :], rs[:, 2, t:t + 1], None, ALU.mult)
                i.then_inc(hn_ready, 1)
                split_lo(h * 3 + (N_H + 4), B)
                dve.wait_ge(yt_done, h + 1)
                for m in range(2):
                    dve.wait_ge(sgo_ready, h * 2 + (m + 1))
                    v.tensor_tensor(sgo[:, m, :], PM[:, m * NLAT:(m + 1) * NLAT], sgo[:, m, :], ALU.mult)\
                        .then_inc(pm_free, 1)
                own.leave(HEADS)

            with dve.Fori(0, 2) as i:
                for cc in range(2):
                    q = i * 2 + cc
                    acc = Tacc[:, ds(q, 1), :]
                    for k in range(KT):
                        dve.wait_ge(ada2_in[k % 4], q * 32 + (k // 4 * 16 + 16))
                        src = ada2[k % 4][:, :].unsqueeze(1)
                        if k == 0:
                            v.tensor_scalar(acc, src, csil[:, 0, 0:1], None, ALU.mult).then_inc(ada2_used, 1)
                        else:
                            dve.wait_ge(ada2_used, q * KT + (k + 4))
                            v.scalar_tensor_tensor(out=acc, in0=src, scalar=csil[:, 0, k:k + 1], in1=acc,
                                                   op0=ALU.mult, op1=ALU.add).then_inc(ada2_used, 1)
                    split_lo(i * 2 + (N_V + 2 + cc), cc)
            dve.wait_ge(T_mm, 1)
            v.tensor_tensor(mod[:, 2:6, :].rearrange("p q k -> p (q k)"), PM[:, 0:4 * KT], cols[:, 48:80], ALU.add)\
                .then_inc(mod_ready, 1)
            dve.wait_ge(mod_ready, 1)
            own.link(v.scalar_tensor_tensor(out=a2[:, :], in0=mod[:, 4, :], scalar=1.0, in1=cols[:, 24:32],
                                            op0=ALU.add, op1=ALU.mult))
            dve.wait_ge(act_own, TT + 1 + HEADS * LT + LT)
            rsqrt(LT, D)
            for t in range(LT):
                v.tensor_scalar(V[:, t, :], V[:, t, :], rs[:, 2, t:t + 1], None, ALU.mult).then_inc(v_scaled, 1)
            dve.wait_ge(wsp_hi_d, 1)
            v.tensor_tensor(wsp_lo[:, :, :], PM[:, HALF:2 * HALF].rearrange("p (g t) -> p g t", g=4),
                            wsp_hi[:, :, :].bitcast(F32), ALU.subtract).then_inc(wsp_ready, 1)

            dve.wait_ge(small_in, 32)
            with dve.Fori(0, 2) as i:
                own.enter(i, LINKS_U)
                for hh in range(2):
                    for jj in (2 * hh, 2 * hh + 1):
                        b = jj % 2
                        dve.wait_ge(v_scaled, LT)
                        dve.wait_ge(vn_hi_d, i * 4 + (jj + 1))
                        v.tensor_tensor(vn_lo[b][:, :, :], V[:, :, ds(i * (4 * P) + jj * P, P)],
                                        vn_hi[b][:, :, :].bitcast(F32), ALU.subtract).then_inc(vn_ready, 1)
                    for jj in (2 * hh, 2 * hh + 1):
                        b = jj % 2
                        dve.wait_ge(sv_done, i * 4 + (jj + 3))
                        half = PM[:, b * NLAT:(b + 1) * NLAT]
                        own.link(v.scalar_tensor_tensor(
                            out=half.rearrange("p (c t) -> p c t", t=P), in0=half.rearrange("p (c t) -> p c t", t=P),
                            scalar=cols2[:, ds(i * 4 + (8 + jj), 1)],
                            in1=bspB[:, ds(i * 2 + jj // 2, 1), :].to_broadcast([P, LT, P]),
                            op0=ALU.mult, op1=ALU.add))
                        dve.wait_ge(slot_free[b], i * 2 + (T_U // 2 + 2 + jj // 2))
                        v.tensor_tensor(uT[b][:, :], half, uT[b][:, :], ALU.mult).then_inc(y_f32, 1)
                        dve.wait_ge(y_hi_d, i * 4 + (jj + 1))
                        v.tensor_tensor(Y_lo[:, :, ds(i * 4 + jj, 1), :],
                                        uT[b][:, :].rearrange("p (c o t) -> p c o t", o=1, t=P),
                                        Y_hi[:, :, ds(i * 4 + jj, 1), :].bitcast(F32), ALU.subtract)\
                            .then_inc(yb_ready, 1)
                    split_lo(i * 2 + (N_U + 2 + hh), hh)
                own.leave(2)

            with dve.Fori(0, 4) as i:
                split_lo(i * 2 + (N_PB + 2), A)
                for m in range(2):
                    at = Mb[:, ds(i * 2 + m, 1), :]
                    dve.wait_ge(slot_free[m], i * 2 + (T_PB // 2 + 2))
                    dve.wait_ge(tile_done, i * 4 + (T_PB + m + 3))
                    v.scalar_tensor_tensor(out=at, in0=at, scalar=1.0,
                                           in1=PD[m][:, :].rearrange("p (o t) -> p o t", o=1),
                                           op0=ALU.add, op1=ALU.mult).then_inc(slot_free[m], 1)

                split_lo(i * 2 + (N_PB + 3), B)

            for k in range(KT):
                dve.wait_ge(ya_hi_d, k + 1)
                v.tensor_tensor(Y_lo[:, :, k, :], ya_raw[:, :, k, :], Y_hi[:, :, k, :].bitcast(F32),
                                ALU.subtract).then_inc(ya_ready, 1)

            def m_lo(k):
                dve.wait_ge(m_hi_d, k + 1)
                v.scalar_tensor_tensor(out=R_lo[:, k, :], in0=Mb[:, k, :], scalar=0.5,
                                       in1=R_hi[:, k, :].bitcast(F32), op0=ALU.mult, op1=ALU.subtract)\
                    .then_inc(m_ready, 1)

            def merge_a(i, last):
                for m in range(2):
                    at = Mb[:, ds(i * 2 + m, 1), :]
                    tile = PD[m][:, :]
                    dve.wait_ge(ga_th, i * 2 + (m + 3))
                    dve.wait_ge(tile_done, i * 2 + (T_PA + m + 1))
                    v.scalar_tensor_tensor(out=tile, in0=sg[:, :], scalar=1.0, in1=tile,
                                           op0=ALU.add, op1=ALU.mult).then_inc(ga_used, 1)
                    dve.wait_ge(ga_used, i * 2 + (m + 2))
                    v.tensor_tensor(at, at, tile.unsqueeze(1), ALU.add).then_inc(slot_free[m], 1)
                    if m == 0:
                        split_lo(i * 2 + (N_PA + 2), A)
                        if last:
                            for k in range(KT - 2):
                                m_lo(k)
                if last:
                    for k in range(KT - 2, KT):
                        m_lo(k)
                split_lo(i * 2 + (N_PA + 3), B)

            with dve.Fori(0, 3) as i:
                merge_a(i, False)
            merge_a(3, True)

            dve.wait_ge(gB_mm, 1)
            own.link(v.tensor_copy(sg[:, :], PM[:, 0:D]))
            dve.wait_ge(x2_in, 16 * LT)

            def residual(at, T, p):
                src = PD[p % 2][:, :].rearrange("p (t n) -> p t n", t=2)[:, :, 0:CW]
                dst = xs[:, 2 * p:2 * p + 2, ds(at, CW)]
                dve.wait_ge(tile_done, T + 1)
                own.link(v.tensor_tensor(src, src, sg[:, ds(at, CW)].unsqueeze(1).to_broadcast([P, 2, CW]),
                                         ALU.mult))
                v.tensor_tensor(dst, src, dst, ALU.add).then_inc(slot_free[p % 2], 1)

            def norm2(first, end):
                dve.wait_ge(act_own, TT + 1 + HEADS * LT + LT + end)
                rsqrt(end, D, first)
                if first == 4:
                    v.tensor_copy(note[:, 0:1], rs[:, 2, 4:5]).then_inc(rs_ready, 1)
                    first = 6
                for t in range(first, end):
                    v.tensor_scalar(xn[:, t, :], xs[:, t, :], rs[:, 2, t:t + 1], None, ALU.mult)\
                        .then_inc(xn2_ready, 1)

            for n in range(4):
                for p in range(4):
                    residual(n * CW, T_O + 4 * n + p, p)
                    if n == 3 and p == 2:
                        norm2(0, 4)
                if n < 3:
                    split_lo(N_O + 2 + n, n % 2)
            dve.wait_ge(gB_mm, 2)
            v.tensor_copy(g2B[:, :], PM[:, 0:D]).then_inc(g2_ready, 1)
            norm2(4, LT)
            split_lo(N_F + 1, B)
            for k in range(KT + 1):
                if k < KT and k % 2 == 0:
                    dve.wait_ge(tile_done, T_X + k + 1)
                    if k >= 2:
                        dve.wait_ge(h2_lo, k - 1)
                    v.tensor_scalar(hT[k % 2][:, :], PD[k % 2][:, :], a2[:, k:k + 1], mod[:, 3, k:k + 1],
                                    ALU.mult, ALU.add).then_inc(slot_free[k % 2], 1)
                if k >= 1:
                    dve.wait_ge(h2_hi, k)
                    v.tensor_tensor(R_lo[:, k - 1, :], hT[(k - 1) % 2][:, :], R_hi[:, k - 1, :].bitcast(F32),
                                    ALU.subtract).then_inc(h2_lo, 1)

            def gate_out(tile, free, m):
                dve.wait_ge(slot_free[m], free)
                dve.wait_ge(tile_done, tile)
                v.tensor_tensor(sa[:, m, :], PD[m][:, :], sa[:, m, :], ALU.mult).then_inc(slot_free[m], 1)

            def f_lo_out(count, m):
                dve.wait_ge(f_hi_d, count)
                v.tensor_tensor(f_lo[:, m, :], sa[:, m, :], f_hi[:, m, :].bitcast(F32), ALU.subtract)\
                    .then_inc(f_lo_d, 1)

            split_lo(N_F + 2, A)
            for m in range(2):
                gate_out(T_F + 3 + m, T_F // 2 + 2, m)
            for m in range(2):
                f_lo_out(m + 1, m)

            def accumulate(tile, t):
                dve.wait_ge(tile_done, tile)
                v.tensor_tensor(xs[:, t, :], PD[t % 2][:, :], xs[:, t, :], ALU.add).then_inc(slot_free[t % 2], 1)

            def ffn(r, last):
                T = r * FT + (T_F + 4)
                n = r * 3 + (N_F + 3)
                split_lo(n, C)
                for t in range(LT):
                    accumulate(T + (3 + t), t)
                    if t in (1, 3):
                        split_lo(n + 1, B, (t // 2,))
                if not last:
                    split_lo(n + 2, A)
                for m in range(2):
                    gate_out(T + (11 + m), r * 6 + (T_F // 2 + 4), m)
                for m in range(2):
                    f_lo_out(r * 2 + (m + 3), m)

            with dve.Fori(0, NFB - 2) as r:
                ffn(r, False)
            ffn(NFB - 2, True)
            split_lo(N_F + 3 * NFB - 1, C)
            dve.wait_ge(fg_in, 16)

            def write_out(first, end):
                for u in range(first, end):
                    v.scalar_tensor_tensor(out=xs[:, u, :], in0=xs[:, u, :], scalar=rs[:, 2, u:u + 1],
                                           in1=fg[:, :], op0=ALU.mult, op1=ALU.mult).then_inc(o_ready, 1)

            for t in range(LT):
                accumulate(T_F + 4 + FT * (NFB - 1) + t + 1, t)
                if t in (4, 6, LT - 1):
                    first, end = {4: (0, 4), 6: (4, 6), LT - 1: (6, LT)}[t]
                    if t == LT - 1:
                        write_out(4, 6)
                    dve.wait_ge(act_own, TT + 1 + HEADS * LT + 2 * LT + end)
                    rsqrt(end, D, first)
                    if t == 4:
                        v.tensor_copy(note[:, t:t + 1], rs[:, 2, 0:1]).then_inc(rs_ready, 1)
            write_out(6, LT)

        @block.tensor
        def _(pe):
            mm = nc.tensor.matmul

            def ready(n, half):
                pe.wait_ge(w_ready[half], n + 2)

            def halves(src, k):
                if src is Y_hi or src is Y_lo:
                    return [src[:, 4 * e:4 * e + 4, k, :] for e in range(2)]
                if src is ctx_hi or src is ctx_lo:
                    return [src[:, k, :]]
                return [src[:, k, e * HALF:(e + 1) * HALF] for e in range(2)]

            def channels(s, n, buf, m, hi, lo, tile_wait=None, dst=None, done=tile_done):
                w = [q[buf][:, :].rearrange("p (k n) -> p k n", k=KT)[:, :, m * P:(m + 1) * P]
                     for q in (whi, wlo)]
                width = NCTX if hi is ctx_hi else HALF
                dst = PD[s] if dst is None else dst
                for k in range(KT):
                    if k % 4 == 0:
                        ready(n, k // 4)
                    if tile_wait is not None:
                        tile_wait(k)
                    for step, (wk, src) in enumerate(((w[0], hi), (w[0], lo), (w[1], hi))):
                        for e, part in enumerate(halves(src, k)):
                            i = mm(dst[:, e * HALF:e * HALF + width], wk[:, k, :], part,
                                   start=(k == 0 and step == 0), stop=(k == KT - 1 and step == 2))
                i.then_inc(done, 1)

            def tokens(s, n, buf, hi, lo, tiles, wait=None):
                w = [q[buf][:, :].rearrange("p (k n) -> p k n", k=KT) for q in (whi, wlo)]
                for e, t in enumerate(tiles):
                    at = slice(t * P, (t + 1) * P)
                    for k in range(KT):
                        if k % 4 == 0:
                            ready(n, k // 4)
                        if wait is not None:
                            wait(k)
                        for step, (src, wk) in enumerate(((hi, w[0]), (hi, w[1]), (lo, w[0]))):
                            i = mm(PD[s][:, e * HALF:e * HALF + CW], src[:, k, at], wk[:, k, :],
                                   start=(k == 0 and step == 0), stop=(k == KT - 1 and step == 2))
                i.then_inc(tile_done, 1)

            pe.wait_ge(consts, 2)

            def x_transposed(t):
                pe.wait_ge(xn_ready, t + 1)
                if t >= 2:
                    pe.wait_ge(xT_read[t % 2], t // 2)
                for k in range(KT):
                    i = nc.tensor.transpose(PD[t % 2][:, k * P:(k + 1) * P], xtok[:, t, k * P:(k + 1) * P],
                                            ident[:, :])
                i.then_inc(xT_done, 1)

            def ada_rows(k):
                pe.wait_ge(csil_ready, 1)
                pe.wait_ge(ada_in[k % 4], k // 4 * 16 + 16)
                for e in range(4):
                    i = mm(PM[0:2, e * HALF:(e + 1) * HALF], csil[:, :, k],
                           ada_raw[k % 4][:, e * HALF:(e + 1) * HALF], start=(k == 0), stop=(k == KT - 1))
                i.then_inc(ada_mm, 1)

            for t in range(4):
                x_transposed(t)
                if t == 0:
                    pe.wait_ge(vec_in, 16 * 9)
                    nc.tensor.transpose(PM[:, 0:P], rows1[:, :], ident[:, :])
                    nc.tensor.transpose(PM[:, P:P + 16], rows2[:, :], ident[0:16, 0:16]).then_inc(vecT, 1)
            for k in range(3):
                ada_rows(k)
                x_transposed(4 + 2 * k)
                x_transposed(5 + 2 * k)
            for k in range(3, KT):
                ada_rows(k)
            pe.wait_ge(adarow_ready, 1)
            for j in range(2 * KT):
                i = mm(PM[:, 2 * j:2 * j + 2], xtok[0:2, j // KT, (j % KT) * P:(j % KT + 1) * P], ident[0:2, 0:2],
                       start=True, stop=True)
            i.then_inc(adacol_done, 1)

            pe.wait_ge(wg_ready, 1)
            for k in range(KT):
                pe.wait_ge(h_lo, 2 * k + 2)
                for d in range(2):
                    for step, (wk, src, csrc) in enumerate(((wg_hi, R_hi, ctx_hi), (wg_hi, R_lo, ctx_lo),
                                                            (wg_lo, R_hi, ctx_hi))):
                        if d == 0:
                            parts = (src[:, k, 0:HALF], src[:, k, HALF:], csrc[:, k, :])
                        else:
                            parts = (src[:, k, NLAT - 1:HALF - 1:-1], src[:, k, HALF - 1::-1], csrc[:, k, ::-1])
                        for at, part in zip((0, HALF, NLAT), parts):
                            i = mm(PM[0:GM, at:at + (HALF if at < NLAT else NCTX)], wk[:, k, d, :], part,
                                   start=(k == 0 and step == 0 and d == 0),
                                   stop=(k == KT - 1 and step == 2 and d == 1))
            i.then_inc(gates_mm, 1)
            for m in range(2):
                pe.wait_ge(slot_free[m], 1)
                channels(m, N_H, A, m, R_hi, R_lo)
            pe.wait_ge(row_ready, 1)
            for t in range(TT):
                mm(PM[:, 16 * t:16 * t + 16], gstk[:, t * P:(t + 1) * P], gsel[:, :], start=True, stop=True)
            mm(PM[:, 160:320], ones8[:, :], dg8[:, :, :, :].rearrange("p k r j -> p (k r j)"),
               start=True, stop=True).then_inc(gcol_done, 1)

            def head(h, last):
                def free(c):
                    pe.wait_ge(slot_free[c % 2], h * 5 + (c // 2 + 1))

                n = h * 3 + N_H
                free(2)
                channels(0, n, A, 1, ctx_hi, ctx_lo)
                pe.wait_ge(head_cols, h + 1)
                pe.wait_ge(pm_free, h * 2 + 2)
                for d, rows in ((0, nM), (1, nMr)):
                    for e in range(2):
                        at = d * NLAT + e * HALF
                        i = mm(PM[:, at:at + HALF], selm[:, d, :], rows[:, e * HALF:(e + 1) * HALF],
                               start=True, stop=True)
                i.then_inc(nb_done, 1)
                free(3)
                tokens(1, n + 1, B, ctx_hi, ctx_lo, (0, 1))
                for p in range(4):
                    free(4 + p)
                    tokens(p % 2, n + 1, B, R_hi, R_lo, (2 * p, 2 * p + 1))
                pe.wait_ge(qk_ready, h * 2 + 2)
                pe.wait_ge(nm_ready, h * 2 + 2)
                pe.wait_ge(wb_ready, h + 1)
                for t in range(TT):
                    at = t * P if t < CT else NLAT + (t - CT) * P
                    i = nc.tensor.transpose(PM[:, at:at + P], kT[:, t * P:(t + 1) * P], ident[:, :])
                i.then_inc(ktr_done, 1)
                free(8)
                channels(0, n + 2, A, 0, R_hi, R_lo)
                pe.wait_ge(ktok_ready, h * 2 + 1)
                for t in range(LT):
                    i = mm(PM[:, t * L:(t + 1) * L], kT[:, NCTX + t * L:NCTX + (t + 1) * L],
                           qT[:, t * L:(t + 1) * L], start=True, stop=True)
                i.then_inc(s_done, 1)
                free(9)
                channels(1, n + 2, A, 1, R_hi, R_lo)
                pe.wait_ge(ktok_ready, h * 2 + 2)
                pe.wait_ge(kw_ready, h * 2 + 2)
                for s in range(2):
                    pe.wait_ge(slot_free[s], h * 5 + 5)
                for j in range(TT):
                    for d in range(2):
                        if j == TT - 1:
                            continue
                        t = tile_of(d, j)
                        if j >= 1:
                            pe.wait_ge(c_ready, h * 18 + (2 * j + d - 1))
                        mm(PM[:, (2 + d) * HALF:(2 + d) * HALF + DVA - 1], kw[:, d, t, :], vaug[:, t, 0:DVA - 1],
                           start=True, stop=True).then_inc(dc_done, 1)
                    if j < CT:
                        continue
                    if j == CT:
                        pe.wait_ge(sw_ready, h * 2 + 2)
                        pe.wait_ge(qw_ready, h * 2 + 2)
                    for d in range(2):
                        t = tile_of(d, j)
                        lat = (t - CT) * L
                        at = d * HALF if j % 2 else 0
                        bank = (PM if j % 2 else PD[d])[:, at:at + DVA - 1]
                        pe.wait_ge(c_ready, h * 18 + (2 * j + d - 1))
                        if j == CT:
                            pe.wait_ge(slot_free[d], h * 5 + 6)
                        if j > CT + 1:
                            pe.wait_ge(h_written, h * 16 + (2 * (j - CT) + d - 3))
                        mm(bank, work[:, d, PAD + lat:PAD + lat + L], vaug[:, t, 0:DVA - 1], start=True, stop=False)
                        mm(bank, WB[:, d, lat:lat + L], Cst[:, d, j % 2, 0:DVA - 1], start=False, stop=True)\
                            .then_inc(num_done, 1)
                if not last:
                    pe.wait_ge(h_written, h * 16 + 14)
                    for m in range(2):
                        free(10 + m)
                        channels(m, n + 3, A, m, R_hi, R_lo)
                pe.wait_ge(hn_ready, h + 1)
                for m in range(2):
                    for t in range(LT):
                        at = m * NLAT + t * P
                        i = nc.tensor.transpose(PM[:, at:at + P], Hh[:, t, m * P:(m + 1) * P], ident[:, :])
                i.then_inc(yt_done, 1)

            with pe.Fori(0, HEADS - 1) as h:
                head(h, False)
            head(HEADS - 1, True)

            def free(T):
                pe.wait_ge(slot_free[T % 2], T // 2 + 1)

            with pe.Fori(0, 2) as i:
                for cc in range(2):
                    for p in range(4):
                        pe.wait_ge(slot_free[p % 2], i * 4 + (T_V // 2 + 2 * cc + p // 2 + 1))
                        tokens(p % 2, i * 2 + (N_V + cc), cc, R_hi, R_lo, (2 * p, 2 * p + 1))
            pe.wait_ge(ada2_used, 4 * KT + 4)
            pe.wait_ge(pm_free, 2 * HEADS + 2)
            for q in range(4):
                for k in range(KT):
                    last = mm(PM[:, q * KT + k:q * KT + k + 1], Tacc[:, q, k * P:(k + 1) * P], one1[:, :],
                              start=True, stop=True)
            last.then_inc(T_mm, 1)
            pe.wait_ge(small_in, 32)
            for g in range(4):
                i = nc.tensor.transpose(PM[:, HALF + g * P:HALF + (g + 1) * P], wsp[:, g, :], ident[:, :])
            i.then_inc(wspT_done, 1)

            with pe.Fori(0, 2) as i:
                for hh in range(2):
                    for jj in (2 * hh, 2 * hh + 1):
                        pe.wait_ge(slot_free[jj % 2], i * 2 + (T_U // 2 + jj // 2 + 1))
                        channels(jj % 2, i * 2 + (N_U + hh), hh, jj % 2, R_hi, R_lo)
                    for jj in (2 * hh, 2 * hh + 1):
                        b = jj % 2
                        pe.wait_ge(vn_ready, i * 4 + (jj + 1))
                        pe.wait_ge(wsp_ready, 1)
                        pe.wait_ge(yb_ready, i * 4 + (jj + 1))
                        g = ds(i * 2 + hh, 1)
                        for c8 in range(LT):
                            dst = PM[:, b * NLAT + c8 * P:b * NLAT + (c8 + 1) * P].unsqueeze(1)
                            for step, (src, wk) in enumerate(((vn_hi[b], wsp_hi), (vn_hi[b], wsp_lo),
                                                              (vn_lo[b], wsp_hi))):
                                last = mm(dst, src[:, c8, :], wk[:, g, :], start=(step == 0), stop=(step == 2))
                        last.then_inc(sv_done, 1)

            with pe.Fori(0, 4) as i:
                for m in range(4):
                    pe.wait_ge(slot_free[m % 2], i * 2 + (T_PB // 2 + m // 2 + 1))
                    if m < 2:
                        channels(m, i * 2 + N_PB, A, m, R_hi, R_lo)
                    else:
                        if m == 2:
                            pe.wait_ge(yb_ready, KT + 2)
                        channels(m - 2, i * 2 + (N_PB + 1), B, m - 2, Y_hi, Y_lo)

            def broadcast_gate(which, at):
                for k in range(KT):
                    last = mm(PM[:, at + k * P:at + (k + 1) * P], mod[:, which, k:k + 1].to_broadcast([P, P]),
                              ident[:, :], start=True, stop=True)
                last.then_inc(gB_mm, 1)

            with pe.Fori(0, 4) as i:
                for m in range(2):
                    pe.wait_ge(ga_th, i * 2 + (m + 1))
                    channels(m, i * 2 + N_PA, A, m, R_hi, R_lo, dst=PM[:, m * NLAT:(m + 1) * NLAT], done=ga_done)
                for m in range(2):
                    pe.wait_ge(slot_free[m], i + (T_PA // 2 + 1))
                    channels(m, i * 2 + (N_PA + 1), B, m, Y_hi, Y_lo,
                             (lambda k: pe.wait_ge(ya_ready, k + 1)) if m == 0 else None)

            pe.wait_ge(mod_ready, 1)
            pe.wait_ge(ga_th, KT + 2)
            broadcast_gate(2, 0)
            with pe.Fori(0, 2) as i:
                for cc in range(2):
                    for p in range(4):
                        pe.wait_ge(slot_free[p % 2], i * 4 + (T_O // 2 + 2 * cc + p // 2 + 1))
                        tokens(p % 2, i * 2 + (N_O + cc), cc, R_hi, R_lo, (2 * p, 2 * p + 1),
                               (lambda k: pe.wait_ge(m_ready, k + 1)) if cc + p == 0 else None)
            broadcast_gate(5, 0)
            pe.wait_ge(xn2_ready, LT - 2)
            pe.wait_ge(xn2_act, 2)
            for k in range(KT):
                free(T_X + k)
                for t in range(LT):
                    last = nc.tensor.transpose(PD[k % 2][:, t * P:(t + 1) * P], xn[:, t, k * P:(k + 1) * P],
                                               ident[:, :])
                last.then_inc(tile_done, 1)

            def down(T, n, last_block=False):
                w = [q[C][:, :].rearrange("p (k n) -> p k n", k=2) for q in (whi, wlo)]
                for t in range(LT):
                    pe.wait_ge(slot_free[t % 2], T[t])
                    at = slice(t * P, (t + 1) * P)
                    for k in range(2):
                        if t == 0:
                            ready(n, k)
                            if last_block:
                                pe.wait_ge(f_lo_d, 2 * NFB - 1 + k)
                        for step, (src, wk) in enumerate(((f_hi, w[0]), (f_hi, w[1]), (f_lo, w[0]))):
                            for e in range(2):
                                last = mm(PD[t % 2][:, e * HALF:(e + 1) * HALF], src[:, k, at],
                                          wk[:, k, e * HALF:(e + 1) * HALF],
                                          start=(k == 0 and step == 0), stop=(k == 1 and step == 2))
                    last.then_inc(tile_done, 1)

            for m in range(2):
                free(T_F + m)
                channels(m, N_F, A, m, R_hi, R_lo, (lambda k: pe.wait_ge(h2_lo, k + 1)) if m == 0 else None)
            for m in range(2):
                free(T_F + 2 + m)
                channels(m, N_F + 1, B, m, R_hi, R_lo)
            with pe.Fori(0, NFB - 1) as r:
                base = (T_F + 4) // 2 + 1
                n = r * 3 + (N_F + 3)
                for m in range(2):
                    pe.wait_ge(slot_free[m], r * 6 + base)
                    channels(m, n - 1, A, m, R_hi, R_lo)
                pe.wait_ge(f_lo_d, r * 2 + 2)
                down([r * 6 + (base + 1 + t // 2) for t in range(LT)], n)
                for m in range(2):
                    pe.wait_ge(slot_free[m], r * 6 + (base + 5))
                    channels(m, n + 1, B, m, R_hi, R_lo)
            T_end = T_F + 4 + FT * (NFB - 1)
            down([(T_end + t) // 2 + 1 for t in range(LT)], N_F + 3 * NFB - 1, True)


_NAMES = ['x', 'c', 'ctx', 'c_ctx', 'w_ada', 'b_ada', 'norm1_g', 'norm2_g', 'w_in', 'conv_w', 'conv_b', 'gate_b',
          'head_g', 'vnorm_g', 'w_spatial', 'b_spatial', 'w_pa', 'w_pb', 'w_out', 'w_ff1', 'w_ff3', 'w_ff2',
          'final_g']


def kernel(**inputs):
    import concourse.bacc as bacc
    import numpy as np
    from concourse.bass_utils import run_bass_kernel_spmd

    nc = bacc.Bacc("TRN2", target_bir_lowering=False, num_devices=1)
    arrays, aps = {}, []
    for name in _NAMES:
        a = np.ascontiguousarray(inputs[name])
        arrays[f"in_{name}"] = a
        aps.append(nc.dram_tensor(f"in_{name}", a.shape, mybir.dt.from_np(a.dtype), kind="ExternalInput").ap())
    out = nc.dram_tensor("out_x", (1, NLAT, D), F32, kind="ExternalOutput").ap()
    build(nc, *aps, out)
    r = run_bass_kernel_spmd(nc, [arrays], core_ids=[0])
    return r.results[0]["out_x"]
```
